# Optimizing a Trainium2 kernel written in Bass

```python
import math
import jax
import jax.numpy as jnp
from jax import lax
import numpy as np

D_MODEL = 1024
BATCH = 1
SEQ = 256
DEPTH = 2

N_MIXERS = 4
EPS = 1e-6
F32 = jnp.float32
OUT_SCALE = 0.5
A_HEADS = 4
A_DQK = 128
A_DV = 256
A_CHUNK = 64
A_IN = 2 * A_HEADS * A_DQK + 2 * A_HEADS * A_DV + 2 * A_HEADS
B_HEADS = 8
B_DH = 128
B_BLOCK = 256
B_TOPK = 3
B_QBLOCK = 128
ROPE_THETA = 500000.0
ROPE_DIMS = B_DH // 4
B_IN = 3 * B_HEADS * B_DH
C_HEADS = 4
C_DK = D_MODEL // C_HEADS
C_DV = 2 * C_DK
C_CHUNK = 128
C_ROPE_THETA = 10000.0
C_IN = 2 * C_HEADS * C_DK + 2 * C_HEADS * C_DV
D_RNN = D_MODEL
D_BLOCKS = 4
D_BW = D_RNN // D_BLOCKS
D_CONV = 4
LRU_C = 8.0
D_FF = ((8 * D_MODEL // 3 + 255) // 256) * 256
N_LAYERS_A = len(range(0, DEPTH, N_MIXERS))
N_LAYERS_B = len(range(1, DEPTH, N_MIXERS))
N_LAYERS_C = len(range(2, DEPTH, N_MIXERS))
N_LAYERS_D = len(range(3, DEPTH, N_MIXERS))


def rmsnorm(x, g):
    xf = x.astype(F32)
    y = xf * lax.rsqrt(jnp.mean(xf * xf, axis=-1, keepdims=True) + EPS)
    return (y * g.astype(F32)).astype(x.dtype)

def rotary(x, pos, n_rot, theta):
    half = n_rot // 2
    inv = theta ** (-jnp.arange(half, dtype=F32) * (2.0 / n_rot))
    ang = pos.astype(F32)[:, None, :, None] * inv
    cos, sin = jnp.cos(ang), jnp.sin(ang)
    xf = x.astype(F32)
    x1, x2 = xf[..., :half], xf[..., half:n_rot]
    out = jnp.concatenate([x1 * cos - x2 * sin, x2 * cos + x1 * sin, xf[..., n_rot:]], axis=-1)
    return out.astype(x.dtype)

def split_heads(t, h):
    b, s, _ = t.shape
    return t.reshape(b, s, h, -1).transpose(0, 2, 1, 3)

def merge_heads(t):
    b, h, s, d = t.shape
    return t.transpose(0, 2, 1, 3).reshape(b, s, h * d)

def to_chunks(t, l):
    b, h, s, d = t.shape
    return t.reshape(b, h, s // l, l, d).transpose(2, 0, 1, 3, 4)

def from_chunks(t):
    nc, b, h, l, d = t.shape
    return t.transpose(1, 2, 0, 3, 4).reshape(b, h, nc * l, d)

def mlstm_mixer(u, w_in, b_gates, g_out, w_out):
    b, s, _ = u.shape
    h, l = A_HEADS, A_CHUNK
    nc = s // l
    sq, sv = h * A_DQK, h * A_DV
    q, k, v, o, gl = jnp.split(u @ w_in, [sq, 2 * sq, 2 * sq + sv, 2 * sq + 2 * sv], axis=-1)
    gl = gl.astype(F32) + b_gates.astype(F32)
    log_i = gl[..., :h]
    log_f = jax.nn.log_sigmoid(gl[..., h:])
    qh = split_heads(q, h).astype(F32) * (A_DQK ** -0.5)
    kh = split_heads(k, h).astype(F32)
    vh = split_heads(v, h).astype(F32)

    def gate_chunks(g):
        return g.transpose(0, 2, 1).reshape(b, h, nc, l).transpose(2, 0, 1, 3)

    causal = jnp.tril(jnp.ones((l, l), dtype=bool))

    def step(carry, xs):
        c_st, n_st, m_st = carry
        qc, kc, vc, ic, fc = xs
        bcum = jnp.cumsum(fc, axis=-1)
        btot = bcum[..., -1]
        dmat = jnp.where(causal, bcum[..., :, None] - bcum[..., None, :] + ic[..., None, :], -jnp.inf)
        inter = bcum + m_st[..., None]
        m_t = jnp.maximum(inter, jnp.max(dmat, axis=-1))
        w_intra = jnp.exp(dmat - m_t[..., None])
        w_inter = jnp.exp(inter - m_t)
        qk = jnp.einsum('bhtd,bhsd->bhts', qc, kc) * w_intra
        num = jnp.einsum('bhts,bhsv->bhtv', qk, vc) + w_inter[..., None] * jnp.einsum('bhvd,bhtd->bhtv', c_st, qc)
        den = jnp.sum(qk, axis=-1) + w_inter * jnp.einsum('bhd,bhtd->bht', n_st, qc)
        h_out = num / jnp.maximum(jnp.abs(den), jnp.exp(-m_t))[..., None]
        dec = btot[..., None] - bcum + ic
        m_new = jnp.maximum(btot + m_st, jnp.max(dec, axis=-1))
        ws = jnp.exp(dec - m_new[..., None])
        wc = jnp.exp(btot + m_st - m_new)
        c_new = wc[..., None, None] * c_st + jnp.einsum('bhs,bhsv,bhsd->bhvd', ws, vc, kc)
        n_new = wc[..., None] * n_st + jnp.einsum('bhs,bhsd->bhd', ws, kc)
        return (c_new, n_new, m_new), h_out

    init = (jnp.zeros((b, h, A_DV, A_DQK), F32), jnp.zeros((b, h, A_DQK), F32), jnp.zeros((b, h), F32))
    xs = (to_chunks(qh, l), to_chunks(kh, l), to_chunks(vh, l), gate_chunks(log_i), gate_chunks(log_f))
    _, hc = lax.scan(step, init, xs)
    hs = rmsnorm(from_chunks(hc), g_out[:, None, :])
    y = merge_heads(hs).astype(u.dtype) * jax.nn.sigmoid(o)
    return y @ w_out

def moba_mixer(u, positions, w_in, g_q, g_k, w_out):
    b, s, _ = u.shape
    h, dh = B_HEADS, B_DH
    q, k, v = jnp.split(u @ w_in, 3, axis=-1)
    qh = rotary(rmsnorm(split_heads(q, h), g_q), positions, ROPE_DIMS, ROPE_THETA)
    kh = rotary(rmsnorm(split_heads(k, h), g_k), positions, ROPE_DIMS, ROPE_THETA)
    vh = split_heads(v, h)
    nblk = -(-s // B_BLOCK)
    sp = nblk * B_BLOCK
    pad = ((0, 0), (0, 0), (0, sp - s), (0, 0))
    qh, kh, vh = jnp.pad(qh, pad), jnp.pad(kh, pad), jnp.pad(vh, pad)
    kb = kh.reshape(b, h, nblk, B_BLOCK, dh)
    vb = vh.reshape(b, h, nblk, B_BLOCK, dh)
    kmean = jnp.mean(kb.astype(F32), axis=3)
    nqb = sp // B_QBLOCK
    per_blk = B_BLOCK // B_QBLOCK
    topk = min(B_TOPK, nblk - 1)
    qblocks = qh.reshape(b, h, nqb, B_QBLOCK, dh).transpose(0, 2, 1, 3, 4).reshape(b * nqb, h, B_QBLOCK, dh)
    scale = dh ** -0.5
    qoff = jnp.arange(B_QBLOCK)
    koff = jnp.arange(B_BLOCK)

    def attend(args):
        idx, qc = args
        bi = idx // nqb
        qi = idx % nqb
        j = qi // per_blk
        kb_b, vb_b = kb[bi], vb[bi]
        qf = qc.astype(F32) * scale
        qpos = qi * B_QBLOCK + qoff
        kpos = j * B_BLOCK + koff
        k_own = kb_b[:, j].astype(F32)
        v_own = vb_b[:, j].astype(F32)
        s_own = jnp.einsum('hqd,hnd->hqn', qf, k_own)
        s_own = jnp.where(kpos[None, None, :] <= qpos[None, :, None], s_own, -jnp.inf)
        if topk > 0:
            gate = jnp.einsum('hqd,hnd->hqn', qf, kmean[bi])
            gate = jnp.where(jnp.arange(nblk)[None, None, :] < j, gate, -jnp.inf)
            _, sel = lax.top_k(gate, topk)
            k_sel = jax.vmap(lambda kh_, ih_: kh_[ih_])(kb_b, sel).astype(F32)
            v_sel = jax.vmap(lambda vh_, ih_: vh_[ih_])(vb_b, sel).astype(F32)
            s_sel = jnp.einsum('hqd,hqtnd->hqtn', qf, k_sel)
            valid = jnp.arange(topk) < j
            s_sel = jnp.where(valid[None, None, :, None], s_sel, -jnp.inf)
            logits = jnp.concatenate([s_sel.reshape(h, B_QBLOCK, topk * B_BLOCK), s_own], axis=-1)
            p = jax.nn.softmax(logits, axis=-1)
            p_sel = p[..., :topk * B_BLOCK].reshape(h, B_QBLOCK, topk, B_BLOCK)
            out = jnp.einsum('hqtn,hqtnd->hqd', p_sel, v_sel) + jnp.einsum('hqn,hnd->hqd', p[..., topk * B_BLOCK:], v_own)
        else:
            p = jax.nn.softmax(s_own, axis=-1)
            out = jnp.einsum('hqn,hnd->hqd', p, v_own)
        return out.astype(qc.dtype)

    out = lax.map(attend, (jnp.arange(b * nqb, dtype=jnp.int32), qblocks))
    out = out.reshape(b, nqb, h, B_QBLOCK, dh).transpose(0, 2, 1, 3, 4).reshape(b, h, sp, dh)[:, :, :s]
    return merge_heads(out) @ w_out

def retention_mixer(u, positions, w_in, g_out, w_out):
    b, s, _ = u.shape
    h, l = C_HEADS, C_CHUNK
    sk, sv = h * C_DK, h * C_DV
    q, k, v, g = jnp.split(u @ w_in, [sk, 2 * sk, 2 * sk + sv], axis=-1)
    qh = rotary(split_heads(q, h), positions, C_DK, C_ROPE_THETA).astype(F32)
    kh = rotary(split_heads(k, h), positions, C_DK, C_ROPE_THETA).astype(F32) * (C_DK ** -0.5)
    vh = split_heads(v, h).astype(F32)
    log_g = jnp.log1p(-jnp.exp2(-5.0 - jnp.arange(h, dtype=F32)))
    idx = jnp.arange(l, dtype=F32)
    diff = idx[:, None] - idx[None, :]
    intra = jnp.where(diff >= 0, jnp.exp(jnp.maximum(diff, 0.0)[None] * log_g[:, None, None]), 0.0)
    xi = jnp.exp((idx + 1.0)[None, :] * log_g[:, None])
    zeta = jnp.exp((l - 1.0 - idx)[None, :] * log_g[:, None])
    g_chunk = jnp.exp(l * log_g)

    def step(r_st, xs):
        qc, kc, vc = xs
        inner = jnp.einsum('bhts,bhsv->bhtv', jnp.einsum('bhtd,bhsd->bhts', qc, kc) * intra, vc)
        cross = jnp.einsum('bhtd,bhdv->bhtv', qc, r_st) * xi[None, :, :, None]
        r_new = g_chunk[None, :, None, None] * r_st + jnp.einsum('bhsd,bhsv->bhdv', kc * zeta[None, :, :, None], vc)
        return r_new, inner + cross

    _, yc = lax.scan(step, jnp.zeros((b, h, C_DK, C_DV), F32), (to_chunks(qh, l), to_chunks(kh, l), to_chunks(vh, l)))
    ys = from_chunks(yc)
    mu = jnp.mean(ys, axis=-1, keepdims=True)
    var = jnp.mean(jnp.square(ys - mu), axis=-1, keepdims=True)
    yn = (ys - mu) * lax.rsqrt(var + EPS) * g_out[:, None, :].astype(F32)
    y = merge_heads(yn).astype(u.dtype) * jax.nn.silu(g)
    return y @ w_out

def lru_combine(c1, c2):
    a1, b1 = c1
    a2, b2 = c2
    return a1 * a2, a2 * b1 + b2

def rglru_mixer(u, w_in, conv_w, conv_b, w_gates, b_gates, lru_param, w_out):
    b, s, _ = u.shape
    gate_br, xb = jnp.split(u @ w_in, 2, axis=-1)
    xc = lax.conv_general_dilated(xb, conv_w[:, None, :].astype(xb.dtype), window_strides=(1,),
                                  padding=[(D_CONV - 1, 0)], dimension_numbers=('NWC', 'WIO', 'NWC'),
                                  feature_group_count=D_RNN) + conv_b
    gates = jnp.einsum('bsnc,nce->bsne', xc.reshape(b, s, D_BLOCKS, D_BW), w_gates) + b_gates
    r = jax.nn.sigmoid(gates[..., :D_BW].astype(F32)).reshape(b, s, D_RNN)
    i = jax.nn.sigmoid(gates[..., D_BW:].astype(F32)).reshape(b, s, D_RNN)
    log_a = -LRU_C * r * jax.nn.softplus(-lru_param.astype(F32))
    a = jnp.exp(log_a)
    bterm = jnp.sqrt(-jnp.expm1(2.0 * log_a)) * (i * xc.astype(F32))
    _, hs = lax.associative_scan(lru_combine, (a, bterm), axis=1)
    y = hs.astype(u.dtype) * jax.nn.gelu(gate_br)
    return y @ w_out

def swiglu(u, w_in, w_out):
    gt, up = jnp.split(u @ w_in, 2, axis=-1)
    return (jax.nn.silu(gt) * up) @ w_out

def first_inputs(seed: int = 0) -> dict:
    key = jax.random.key(seed)
    ks = list(jax.random.split(key, 32))

    def rnd(shape, scale):
        return scale * jax.random.normal(ks.pop(), shape, F32)

    def gain(shape):
        return 1.0 + rnd(shape, 0.02)

    x = rnd((BATCH, SEQ, D_MODEL), 1.0)
    offs = jax.random.randint(ks.pop(), (BATCH, 1), 0, 1024, dtype=jnp.int32)
    positions = jnp.arange(SEQ, dtype=jnp.int32)[None, :] + offs
    norm_mix = gain((DEPTH, D_MODEL))
    norm_ffn = gain((DEPTH, D_MODEL))
    ffn_w_in = rnd((DEPTH, D_MODEL, 2 * D_FF), D_MODEL ** -0.5)
    ffn_w_out = rnd((DEPTH, D_FF, D_MODEL), OUT_SCALE * D_FF ** -0.5)
    a_w_in = rnd((N_LAYERS_A, D_MODEL, A_IN), D_MODEL ** -0.5)
    b_i = -1.0 + rnd((N_LAYERS_A, A_HEADS), 0.1)
    b_f = jnp.linspace(3.0, 6.0, A_HEADS, dtype=F32)[None, :] + rnd((N_LAYERS_A, A_HEADS), 0.1)
    a_b_gates = jnp.concatenate([b_i, b_f], axis=-1)
    a_g_out = gain((N_LAYERS_A, A_HEADS, A_DV))
    a_w_out = rnd((N_LAYERS_A, A_HEADS * A_DV, D_MODEL), OUT_SCALE * (A_HEADS * A_DV) ** -0.5)
    b_w_in = rnd((N_LAYERS_B, D_MODEL, B_IN), D_MODEL ** -0.5)
    b_g_q = gain((N_LAYERS_B, B_DH))
    b_g_k = gain((N_LAYERS_B, B_DH))
    b_w_out = rnd((N_LAYERS_B, B_HEADS * B_DH, D_MODEL), OUT_SCALE * (B_HEADS * B_DH) ** -0.5)
    c_w_in = rnd((N_LAYERS_C, D_MODEL, C_IN), D_MODEL ** -0.5)
    c_g_out = gain((N_LAYERS_C, C_HEADS, C_DV))
    c_w_out = rnd((N_LAYERS_C, C_HEADS * C_DV, D_MODEL), OUT_SCALE * (C_HEADS * C_DV) ** -0.5)
    d_w_in = rnd((N_LAYERS_D, D_MODEL, 2 * D_RNN), D_MODEL ** -0.5)
    d_conv_w = rnd((N_LAYERS_D, D_CONV, D_RNN), D_CONV ** -0.5)
    d_conv_b = rnd((N_LAYERS_D, D_RNN), 0.02)
    d_w_gates = rnd((N_LAYERS_D, D_BLOCKS, D_BW, 2 * D_BW), D_BW ** -0.5)
    d_b_gates = rnd((N_LAYERS_D, D_BLOCKS, 2 * D_BW), 0.1)
    a0 = jax.random.uniform(ks.pop(), (N_LAYERS_D, D_RNN), F32, minval=0.9, maxval=0.999)
    d_lru = jnp.log(a0) - jnp.log1p(-a0)
    d_w_out = rnd((N_LAYERS_D, D_RNN, D_MODEL), OUT_SCALE * D_RNN ** -0.5)
    return {'x': x, 'positions': positions, 'norm_mix': norm_mix, 'norm_ffn': norm_ffn,
            'ffn_w_in': ffn_w_in, 'ffn_w_out': ffn_w_out,
            'a_w_in': a_w_in, 'a_b_gates': a_b_gates, 'a_g_out': a_g_out, 'a_w_out': a_w_out,
            'b_w_in': b_w_in, 'b_g_q': b_g_q, 'b_g_k': b_g_k, 'b_w_out': b_w_out,
            'c_w_in': c_w_in, 'c_g_out': c_g_out, 'c_w_out': c_w_out,
            'd_w_in': d_w_in, 'd_conv_w': d_conv_w, 'd_conv_b': d_conv_b, 'd_w_gates': d_w_gates,
            'd_b_gates': d_b_gates, 'd_lru': d_lru, 'd_w_out': d_w_out}

def first_block(x, positions, norm_mix, norm_ffn, ffn_w_in, ffn_w_out,
              a_w_in, a_b_gates, a_g_out, a_w_out,
              b_w_in, b_g_q, b_g_k, b_w_out,
              c_w_in, c_g_out, c_w_out,
              d_w_in, d_conv_w, d_conv_b, d_w_gates, d_b_gates, d_lru, d_w_out):
    h = x
    for layer in range(DEPTH):
        mixer, r = layer % N_MIXERS, layer // N_MIXERS
        u = rmsnorm(h, norm_mix[layer])
        if mixer == 0:
            y = mlstm_mixer(u, a_w_in[r], a_b_gates[r], a_g_out[r], a_w_out[r])
        elif mixer == 1:
            y = moba_mixer(u, positions, b_w_in[r], b_g_q[r], b_g_k[r], b_w_out[r])
        elif mixer == 2:
            y = retention_mixer(u, positions, c_w_in[r], c_g_out[r], c_w_out[r])
        else:
            y = rglru_mixer(u, d_w_in[r], d_conv_w[r], d_conv_b[r], d_w_gates[r], d_b_gates[r], d_lru[r], d_w_out[r])
        h = h + y
        h = h + swiglu(rmsnorm(h, norm_ffn[layer]), ffn_w_in[layer], ffn_w_out[layer])
    return h


DEPTH_2 = 1

HEAD_DIM = 64
ROPE_THETA_2 = 10000.0
RMS_EPS = 1e-6
NEG_INF = -1e30
BLOCK = 128

A_Q_HEADS = 8
A_KV_HEADS = 2
A_GROUP = A_Q_HEADS // A_KV_HEADS
WINDOW = 128
A_Q_WIDTH = A_Q_HEADS * HEAD_DIM
A_KV_WIDTH = A_KV_HEADS * HEAD_DIM

HY_WIDTH = D_MODEL // 2
HY_ORDER = 2
HY_DIRS = 2
HY_SHORT = 3
HY_BANDS = 16
HY_POS_DIM = 1 + 2 * HY_BANDS
HY_FILTER_HIDDEN = 64
HY_DECAY_TARGET = 1e-2
HY_FAST_PCT = 0.3
HY_SLOW_PCT = 1.5

C_WIDTH = C_HEADS * 2 * HEAD_DIM

N_BRANCH = 3
IN_SIZES = (A_Q_WIDTH, A_KV_WIDTH, A_KV_WIDTH, (HY_ORDER + 1) * HY_WIDTH, C_WIDTH, C_WIDTH, C_WIDTH, N_BRANCH * D_MODEL)
IN_COLS = sum(IN_SIZES)
IN_SPLITS = tuple(sum(IN_SIZES[:i + 1]) for i in range(len(IN_SIZES) - 1))

D_FF_2 = -(-8 * D_MODEL // (3 * 256)) * 256


def rms_norm(x, g):
    xf = x.astype(jnp.float32)
    y = xf * lax.rsqrt(jnp.mean(xf * xf, axis=-1, keepdims=True) + RMS_EPS)
    return (y * g.astype(jnp.float32)).astype(x.dtype)

def rope_tables(seq):
    pos = jnp.arange(seq, dtype=jnp.float32)
    inv = ROPE_THETA_2 ** (-jnp.arange(0, HEAD_DIM, 2, dtype=jnp.float32) / HEAD_DIM)
    ang = pos[:, None] * inv[None, :]
    return jnp.cos(ang), jnp.sin(ang)

def apply_rope(x, cos, sin):
    c = cos[None, :, None, :].astype(x.dtype)
    s = sin[None, :, None, :].astype(x.dtype)
    x1, x2 = jnp.split(x, 2, axis=-1)
    return jnp.concatenate([x1 * c - x2 * s, x2 * c + x1 * s], axis=-1)

def window_attention(q, k, v, sink):
    B, S = q.shape[0], q.shape[1]
    nb = S // BLOCK
    span = BLOCK + 2 * WINDOW
    qb = q.reshape(B, nb, BLOCK, A_KV_HEADS, A_GROUP, HEAD_DIM)
    pad = ((0, 0), (WINDOW, WINDOW), (0, 0), (0, 0))
    kp = jnp.pad(k, pad)
    vp = jnp.pad(v, pad)
    idx = jnp.arange(nb)[:, None] * BLOCK + jnp.arange(span)[None, :]
    kb = kp[:, idx]
    vb = vp[:, idx]
    s = jnp.einsum('bnqhgd,bnkhd->bnhgqk', qb, kb).astype(jnp.float32) / math.sqrt(HEAD_DIM)
    q_pos = jnp.arange(nb)[:, None] * BLOCK + jnp.arange(BLOCK)[None, :]
    k_pos = idx - WINDOW
    dist = k_pos[:, None, :] - q_pos[:, :, None]
    valid = (jnp.abs(dist) <= WINDOW) & (k_pos[:, None, :] >= 0) & (k_pos[:, None, :] < S)
    s = jnp.where(valid[None, :, None, None], s, NEG_INF)
    sink_b = jnp.broadcast_to(sink.astype(jnp.float32).reshape(A_KV_HEADS, A_GROUP)[None, None, :, :, None, None], s.shape[:-1] + (1,))
    p = jax.nn.softmax(jnp.concatenate([s, sink_b], axis=-1), axis=-1)[..., :-1]
    o = jnp.einsum('bnhgqk,bnkhd->bnqhgd', p.astype(v.dtype), vb)
    return o.reshape(B, S, A_Q_HEADS * HEAD_DIM)

def diff_attention(q, k, v, lam):
    B, S = q.shape[0], q.shape[1]
    nb = S // BLOCK
    qb = q.reshape(B, nb, BLOCK, C_HEADS, 2, HEAD_DIM).transpose(1, 0, 3, 4, 2, 5)
    kt = k.transpose(0, 2, 3, 1, 4)
    vt = v.transpose(0, 2, 1, 3)

    def one_block(qblk):
        s = jnp.einsum('bhcqd,bhckd->bhcqk', qblk, kt).astype(jnp.float32) / math.sqrt(HEAD_DIM)
        p = jax.nn.softmax(s, axis=-1)
        a = p[:, :, 0] - lam * p[:, :, 1]
        return jnp.einsum('bhqk,bhkd->bhqd', a.astype(v.dtype), vt)

    o = lax.map(one_block, qb)
    return o.transpose(1, 0, 3, 2, 4).reshape(B, S, C_HEADS, 2 * HEAD_DIM)

def short_conv(u, w, b):
    L = u.shape[1]
    up = jnp.pad(u, ((0, 0), (1, 1), (0, 0)))
    return up[:, :L] * w[0] + up[:, 1:L + 1] * w[1] + up[:, 2:] * w[2] + b

def hyena_filters(L, w1, b1, f1, w2, b2, f2, w3):
    f32 = jnp.float32
    pos = jnp.arange(L, dtype=f32)
    t = pos / max(L - 1, 1)
    bands = jnp.arange(1, HY_BANDS + 1, dtype=f32)
    ang = 2.0 * math.pi * pos[:, None] * bands[None, :] / L
    z = jnp.concatenate([t[:, None], jnp.cos(ang), jnp.sin(ang)], axis=-1)
    h = jnp.sin(f1.astype(f32) * (z @ w1.astype(f32) + b1.astype(f32)))
    h = jnp.sin(f2.astype(f32) * (h @ w2.astype(f32) + b2.astype(f32)))
    h = (h @ w3.astype(f32)).reshape(L, HY_ORDER, HY_DIRS, HY_WIDTH)
    min_decay = math.log(HY_DECAY_TARGET) / HY_SLOW_PCT
    max_decay = math.log(HY_DECAY_TARGET) / HY_FAST_PCT
    deltas = jnp.abs(jnp.linspace(min_decay, max_decay, HY_WIDTH, dtype=f32))
    decay = jnp.exp(-t[:, None] * deltas[None, :])
    h = h * decay[:, None, None, :]
    fwd, bwd = h[:, :, 0], h[:, :, 1]
    c = jnp.concatenate([fwd[:1] + bwd[:1], fwd[1:], jnp.zeros_like(fwd[:1]), bwd[1:][::-1]], axis=0)
    return c * lax.rsqrt(jnp.sum(c * c, axis=0, keepdims=True) + RMS_EPS)

def fft_conv(u, cf):
    L = u.shape[1]
    U = jnp.fft.rfft(u.astype(jnp.float32), n=2 * L, axis=1)
    y = jnp.fft.irfft(U * cf[None], n=2 * L, axis=1)[:, :L]
    return y.astype(u.dtype)

def hyena_branch(u, conv_w, conv_b, w1, b1, f1, w2, b2, f2, w3, hy_d):
    L = u.shape[1]
    u = short_conv(u, conv_w, conv_b)
    v, x1, x2 = jnp.split(u, 3, axis=-1)
    cf = jnp.fft.rfft(hyena_filters(L, w1, b1, f1, w2, b2, f2, w3), axis=0)
    z = x1 * (fft_conv(v, cf[:, 0]) + hy_d[0] * v)
    z = x2 * (fft_conv(z, cf[:, 1]) + hy_d[1] * z)
    return z

def second_inputs(seed: int = 0) -> dict:
    key = jax.random.key(seed)
    ks = jax.random.split(key, 40)

    def nrm(i, shape, scale):
        return jax.random.normal(ks[i], shape, dtype=jnp.float32) * scale

    def gain(i, shape):
        return 1.0 + nrm(i, shape, 0.05)

    L = DEPTH_2
    return {
        'x': nrm(0, (BATCH, SEQ, D_MODEL), 1.0),
        'norm1_g': gain(1, (L, D_MODEL)),
        'w_in': nrm(2, (L, D_MODEL, IN_COLS), D_MODEL ** -0.5),
        'sink_a': nrm(3, (L, A_Q_HEADS), 0.5),
        'qn_a': gain(4, (L, HEAD_DIM)),
        'kn_a': gain(5, (L, HEAD_DIM)),
        'conv_w': nrm(6, (L, HY_SHORT, (HY_ORDER + 1) * HY_WIDTH), 0.6),
        'conv_b': nrm(7, (L, (HY_ORDER + 1) * HY_WIDTH), 0.01),
        'filt_w1': nrm(8, (L, HY_POS_DIM, HY_FILTER_HIDDEN), HY_POS_DIM ** -0.5),
        'filt_b1': nrm(9, (L, HY_FILTER_HIDDEN), 0.1),
        'filt_f1': gain(10, (L, HY_FILTER_HIDDEN)),
        'filt_w2': nrm(11, (L, HY_FILTER_HIDDEN, HY_FILTER_HIDDEN), HY_FILTER_HIDDEN ** -0.5),
        'filt_b2': nrm(12, (L, HY_FILTER_HIDDEN), 0.1),
        'filt_f2': gain(13, (L, HY_FILTER_HIDDEN)),
        'filt_w3': nrm(14, (L, HY_FILTER_HIDDEN, HY_ORDER * HY_DIRS * HY_WIDTH), HY_FILTER_HIDDEN ** -0.5),
        'hy_d': nrm(15, (L, HY_ORDER, HY_WIDTH), 0.1),
        'qn_c': gain(16, (L, HEAD_DIM)),
        'kn_c': gain(17, (L, HEAD_DIM)),
        'lam_q1': nrm(18, (L, HEAD_DIM), 0.1),
        'lam_k1': nrm(19, (L, HEAD_DIM), 0.1),
        'lam_q2': nrm(20, (L, HEAD_DIM), 0.1),
        'lam_k2': nrm(21, (L, HEAD_DIM), 0.1),
        'subln_c': gain(22, (L, 2 * HEAD_DIM)),
        'w_oa': nrm(23, (L, A_Q_WIDTH, D_MODEL), A_Q_WIDTH ** -0.5),
        'w_ob': nrm(24, (L, HY_WIDTH, D_MODEL), HY_WIDTH ** -0.5),
        'w_oc': nrm(25, (L, C_WIDTH, D_MODEL), C_WIDTH ** -0.5),
        'w_out': nrm(26, (L, D_MODEL, D_MODEL), D_MODEL ** -0.5),
        'norm2_g': gain(27, (L, D_MODEL)),
        'ffn_w1': nrm(28, (L, D_MODEL, D_FF_2), D_MODEL ** -0.5),
        'ffn_w3': nrm(29, (L, D_MODEL, D_FF_2), D_MODEL ** -0.5),
        'ffn_w2': nrm(30, (L, D_FF_2, D_MODEL), D_FF_2 ** -0.5),
    }

def second_block(x, norm1_g, w_in, sink_a, qn_a, kn_a, conv_w, conv_b, filt_w1, filt_b1, filt_f1, filt_w2, filt_b2, filt_f2, filt_w3, hy_d, qn_c, kn_c, lam_q1, lam_k1, lam_q2, lam_k2, subln_c, w_oa, w_ob, w_oc, w_out, norm2_g, ffn_w1, ffn_w3, ffn_w2):
    B, S = x.shape[0], x.shape[1]
    cos, sin = rope_tables(S)
    for l in range(DEPTH_2):
        h = rms_norm(x, norm1_g[l])
        proj = h @ w_in[l]
        qa, ka, va, hy_in, qc, kc, vc, gate_logits = jnp.split(proj, IN_SPLITS, axis=-1)

        qa = apply_rope(rms_norm(qa.reshape(B, S, A_Q_HEADS, HEAD_DIM), qn_a[l]), cos, sin)
        ka = apply_rope(rms_norm(ka.reshape(B, S, A_KV_HEADS, HEAD_DIM), kn_a[l]), cos, sin)
        va = va.reshape(B, S, A_KV_HEADS, HEAD_DIM)
        out_a = window_attention(qa, ka, va, sink_a[l])

        out_b = hyena_branch(hy_in, conv_w[l], conv_b[l], filt_w1[l], filt_b1[l], filt_f1[l], filt_w2[l], filt_b2[l], filt_f2[l], filt_w3[l], hy_d[l])

        lambda_init = 0.8 - 0.6 * math.exp(-0.3 * l)
        lam = (jnp.exp(jnp.sum(lam_q1[l].astype(jnp.float32) * lam_k1[l].astype(jnp.float32)))
               - jnp.exp(jnp.sum(lam_q2[l].astype(jnp.float32) * lam_k2[l].astype(jnp.float32)))
               + lambda_init)
        qc = apply_rope(rms_norm(qc.reshape(B, S, 2 * C_HEADS, HEAD_DIM), qn_c[l]), cos, sin).reshape(B, S, C_HEADS, 2, HEAD_DIM)
        kc = apply_rope(rms_norm(kc.reshape(B, S, 2 * C_HEADS, HEAD_DIM), kn_c[l]), cos, sin).reshape(B, S, C_HEADS, 2, HEAD_DIM)
        vc = vc.reshape(B, S, C_HEADS, 2 * HEAD_DIM)
        out_c = diff_attention(qc, kc, vc, lam)
        out_c = (rms_norm(out_c, subln_c[l]) * (1.0 - lambda_init)).reshape(B, S, C_WIDTH)

        g = jax.nn.sigmoid(gate_logits.astype(jnp.float32)).reshape(B, S, N_BRANCH, D_MODEL).astype(x.dtype)
        merged = (g[:, :, 0] * (out_a @ w_oa[l])
                  + g[:, :, 1] * (out_b @ w_ob[l])
                  + g[:, :, 2] * (out_c @ w_oc[l]))
        x = x + merged @ w_out[l]

        h2 = rms_norm(x, norm2_g[l])
        x = x + (jax.nn.silu(h2 @ ffn_w1[l]) * (h2 @ ffn_w3[l])) @ ffn_w2[l]
    return x


def setup_inputs(seed=0):
    out = dict(first_inputs(seed))
    for name, value in second_inputs(seed + 1).items():
        if name != "x":
            out[name + "_2"] = value
    return out


def reference(
    x, positions, norm_mix, norm_ffn, ffn_w_in, ffn_w_out, a_w_in, a_b_gates, a_g_out, a_w_out,
    b_w_in, b_g_q, b_g_k, b_w_out, c_w_in, c_g_out, c_w_out, d_w_in, d_conv_w, d_conv_b,
    d_w_gates, d_b_gates, d_lru, d_w_out, norm1_g_2, w_in_2, sink_a_2, qn_a_2, kn_a_2, conv_w_2,
    conv_b_2, filt_w1_2, filt_b1_2, filt_f1_2, filt_w2_2, filt_b2_2, filt_f2_2, filt_w3_2,
    hy_d_2, qn_c_2, kn_c_2, lam_q1_2, lam_k1_2, lam_q2_2, lam_k2_2, subln_c_2, w_oa_2, w_ob_2,
    w_oc_2, w_out_2, norm2_g_2, ffn_w1_2, ffn_w3_2, ffn_w2_2,
):
    x = first_block(
        x, positions, norm_mix, norm_ffn, ffn_w_in, ffn_w_out, a_w_in, a_b_gates, a_g_out,
        a_w_out, b_w_in, b_g_q, b_g_k, b_w_out, c_w_in, c_g_out, c_w_out, d_w_in, d_conv_w,
        d_conv_b, d_w_gates, d_b_gates, d_lru, d_w_out,
    )
    return second_block(
        x, norm1_g_2, w_in_2, sink_a_2, qn_a_2, kn_a_2, conv_w_2, conv_b_2, filt_w1_2,
        filt_b1_2, filt_f1_2, filt_w2_2, filt_b2_2, filt_f2_2, filt_w3_2, hy_d_2, qn_c_2,
        kn_c_2, lam_q1_2, lam_k1_2, lam_q2_2, lam_k2_2, subln_c_2, w_oa_2, w_ob_2, w_oc_2,
        w_out_2, norm2_g_2, ffn_w1_2, ffn_w3_2, ffn_w2_2,
    )


_drawn_inputs = setup_inputs


def setup_inputs(seed=0):
    import zlib

    import numpy as np

    out = dict(_drawn_inputs(seed))
    spreads = {}
    factors = {'norm_mix': 3.448,
     'norm_ffn': 3.502,
     'a_g_out': 7.305,
     'b_g_q': 8.0,
     'b_g_k': 8.0,
     'sink_a_2': 8.0,
     'qn_a_2': 21.551,
     'kn_a_2': 8.0,
     'conv_b_2': 25.464,
     'filt_f1_2': 14.333,
     'qn_c_2': 3.26,
     'kn_c_2': 3.014,
     'lam_q1_2': 22.335,
     'lam_q2_2': 17.674,
     'subln_c_2': 20.346,
     'filt_b2_2': 2.686,
     'filt_f2_2': 8.0,
     'hy_d_2': 4.791,
     'lam_k2_2': 3.092,
     'norm2_g_2': 8.0}
    for name, (base, spread) in spreads.items():
        noise = np.random.default_rng([zlib.crc32(name.encode()), seed]).standard_normal(out[name].shape)
        drawn = base * np.exp(spread * noise) if base else spread * noise
        out[name] = jnp.asarray(drawn.astype(out[name].dtype))
    for name, factor in factors.items():
        out[name] = (out[name] * factor).astype(out[name].dtype)
    return out
```

```python
from contextlib import ExitStack
import math

import numpy as np
import concourse.bass as bass
from concourse import mybir

F32 = mybir.dt.float32
F32R = mybir.dt.float32r
I32 = mybir.dt.int32
ALU = mybir.AluOpType
ACT = mybir.ActivationFunctionType
AXX = mybir.AxisListType.X

P = 128
S = 256
NT = S // P
DM = 1024
KT = DM // P
EPS = 1e-6
UNIT = 1024
RAW, SPL = 6, 3
DFF = 2816
FB = DFF // 256
AH, ADK, ADV = 4, 128, 256
BH, BD, BROT = 8, 128, 32
HW = 512
WQ, CH = 8, 4
HD = 64
LAM0 = 0.8 - 0.6 * math.exp(0.0)
NFT = 5
TWO_PI = 2.0 * math.pi
C1 = 6.28125
C2 = float(np.float32(TWO_PI - C1))
C3 = float(np.float32(TWO_PI - C1 - C2))
MAGIC = 12582912.0
PI_IN = 3.1415925
MASKED = -1e30

N_IN_A, N_IN_B = 6, 6
U_A = 0
U_AO = U_A + 4 * N_IN_A
U_F0 = U_AO + KT
FFN_UNITS = 4 + 6 * (FB - 1) + 2
U_B = U_F0 + FFN_UNITS
U_BO = U_B + 4 * N_IN_B
U_F1 = U_BO + KT
U_C = U_F1 + FFN_UNITS
U_GA = U_C + 4 * 8
U_OA = U_GA + 8
U_GB = U_OA + 4
U_OB = U_GB + 8
U_GC = U_OB + 4
U_OC = U_GC + 8
U_W = U_OC + 4
U_F2 = U_W + KT
U_END = U_F2 + FFN_UNITS

IN_BLOCKS = ([(U_A + 4 * i, 512, 2 * (i % 2)) for i in range(6)]
             + [(U_B + 4 * i, 512, 2 * (i % 2)) for i in range(6)]
             + [(U_C + 4 * i, 512 if i < 7 else 256, 2 * (i % 2)) for i in range(8)]
             + [(U_GA, 512, 0), (U_GA + 4, 512, 0), (U_GB, 512, 0), (U_GB + 4, 512, 0),
                (U_GC, 512, 0), (U_GC + 4, 512, 0)])
TANH_BLOCKS = {4, 5, 20, 21, 22, 23, 24, 25}
ACT_EVACS = [sum(2 if j in TANH_BLOCKS else 1 for j in range(i + 1)) for i in range(len(IN_BLOCKS))]
DVE_EVACS = [sum(0 if j in TANH_BLOCKS else 1 for j in range(i + 1)) for i in range(len(IN_BLOCKS))]

TBANKS = (2, 3, 4, 5)

CONSTS = {}
_at = 0
for _name, _n in (("ident", P), ("ones", P), ("sel", AH * P), ("zT", S), ("nrmw", 4), ("inv", BROT // 2),
                  ("cosC", NT * HD // 2), ("sinC", NT * HD // 2), ("maskB", 384), ("maskW", NT * S),
                  ("fwd", NT * (NFT + 1) * P), ("bwd", 4 * S)):
    CONSTS[_name] = (_at, _n)
    _at += _n
N_CONST = _at
N_FIRST = CONSTS["inv"][0]


def constants():
    c = np.zeros((P, N_CONST), np.float32)

    def put(name, a):
        o, n = CONSTS[name]
        a = np.asarray(a, np.float64)
        c[:a.shape[0], o:o + n] = a.reshape(a.shape[0], n)

    put("ident", np.eye(P))
    put("ones", np.ones((P, P)))
    sel = np.zeros((AH, AH, P))
    for h in range(AH):
        sel[h, h] = 1.0
    put("sel", sel)
    pos = np.arange(S, dtype=np.float32)
    bands = np.arange(1, 17, dtype=np.float32)
    ang = (np.float32(2.0 * math.pi) * pos[:, None] * bands[None, :] / np.float32(S)).astype(np.float32)
    t = (pos / np.float32(S - 1)).astype(np.float32)
    z = np.concatenate([t[:, None], np.cos(ang), np.sin(ang)], axis=-1)
    put("zT", z.T)
    we, wd = np.full((S,), 0.5), np.full((S,), 0.5)
    we[0], wd[0] = 1.0, 0.0
    put("nrmw", np.stack([we[:P], we[P:], wd[:P], wd[P:]], 1))
    half = BROT // 2
    inv = (np.float32(500000.0) ** (-np.arange(half, dtype=np.float32) * np.float32(2.0 / BROT))).astype(np.float32)
    put("inv", np.tile(inv[None], (P, 1)))
    invc = (np.float32(10000.0) ** (-np.arange(0, HD, 2, dtype=np.float32) / np.float32(HD))).astype(np.float32)
    angc = (pos[:, None] * invc[None, :]).astype(np.float32).astype(np.float64)
    put("cosC", np.cos(angc).reshape(NT, P, HD // 2).transpose(1, 0, 2))
    put("sinC", np.sin(angc).reshape(NT, P, HD // 2).transpose(1, 0, 2))
    i = np.arange(P)
    diag = np.where(i[None, :] <= i[:, None], 0.0, MASKED)
    put("maskB", np.concatenate([diag, np.zeros((P, P)), diag], 1))
    key, tok = np.arange(S), np.arange(S)
    mw = np.where(np.abs(key[None, :] - tok[:, None]) <= 128, 0.0, MASKED)
    put("maskW", mw.reshape(NT, P, S).transpose(1, 0, 2))
    w = 2 * math.pi * np.outer(np.arange(S), np.arange(S)) / (2 * S)
    nyq = np.cos(math.pi * np.arange(S))
    cosm, sinm = np.cos(w), -np.sin(w)
    cosn = cosm[:, :P].copy()
    cosn[:, 0] = nyq
    sinn = sinm[:, :P].copy()
    sinn[:, 0] = nyq
    fwd = np.stack([cosm[:, :P], cosm[:, P:], cosn, sinm[:, :P], sinm[:, P:], sinn], 1)
    put("fwd", fwd.reshape(NT, P, NFT + 1, P).transpose(1, 0, 2, 3))
    ic = 2 * np.cos(w) / (2 * S)
    ic[0] = 1.0 / (2 * S)
    isn = -2 * np.sin(w) / (2 * S)
    isn[0] = nyq / (2 * S)
    put("bwd", np.stack([ic[:P], ic[P:], isn[:P], isn[P:]], 1))
    return c


def decay_table():
    pos = np.arange(S, dtype=np.float32)
    t = (pos / np.float32(S - 1)).astype(np.float32)
    lo, hi = math.log(1e-2) / 1.5, math.log(1e-2) / 0.3
    deltas = np.abs(np.linspace(lo, hi, HW, dtype=np.float32))
    d = np.exp((-t[:, None] * deltas[None, :]).astype(np.float32))
    return np.ascontiguousarray(d.reshape(NT, P, HW).transpose(1, 0, 2).astype(np.float32))


GROWS = {"mix": 0, "ffn": 16, "n1": 32, "n2": 40, "ago": 48, "subln": 56, "b1": 57, "f1": 58, "b2": 59, "f2": 60}
PRM = {}
_at = 0
for _name, _n in (("bg", 8), ("gq", BD), ("gk", BD), ("qa", HD), ("ka", HD), ("qc", HD), ("kc", HD),
                  ("sink", WQ), ("lq1", HD), ("lk1", HD), ("lq2", HD), ("lk2", HD)):
    PRM[_name] = (_at, _n)
    _at += _n
N_PRM = _at

N_WORK = 25200
W_H = N_WORK - 2 * NFT * HW


def build(nc, D, out):
    with ExitStack() as ctx:
        def sb(name, shape, dt=F32):
            return ctx.enter_context(nc.sbuf_tensor(name, shape, dt))

        sems = {}

        def sem(name):
            if name not in sems:
                sems[name] = ctx.enter_context(nc.semaphore(name))
            return sems[name]

        raw = sb("raw", [P, RAW, UNIT])
        whi = sb("whi", [P, SPL, UNIT], F32R)
        wlo = sb("wlo", [P, SPL, UNIT], F32R)
        x = sb("x", [P, NT, DM])
        ath = sb("ath", [P, KT, S], F32R)
        atl = sb("atl", [P, KT, S], F32R)
        brh = sb("brh", [P, 4, S], F32R)
        brl = sb("brl", [P, 4, S], F32R)
        hid = sb("hid", [P, NT, 256])
        sil = sb("sil", [P, NT, 256])
        con = sb("con", [P, N_CONST])
        prm = sb("prm", [P, N_PRM])
        grow = sb("grow", [64, P])
        gcol = sb("gcol", [P, 64])
        wg = sb("wg", [P, KT, 8])
        wgh = sb("wgh", [P, KT, 8], F32R)
        wgl = sb("wgl", [P, KT, 8], F32R)
        ssq = sb("ssq", [P, 6, NT])
        rstd = sb("rstd", [P, 6, NT])
        rhalf = sb("rhalf", [P, 6, NT])
        rq_a = sb("rq_a", [P, 64])
        rq_t = sb("rq_t", [P, 64])
        sm = sb("sm", [P, 512])
        work = sb("work", [P, N_WORK])
        ps = [ctx.enter_context(nc.psum_tensor(f"ps{i}", [P, 512], F32)) for i in range(8)]

        def C(name):
            o, n = CONSTS[name]
            return con[:, o:o + n]

        def R(name):
            o, n = PRM[name]
            return prm[:, o:o + n]

        def W(o, n):
            return work[:, o:o + n]

        ident = C("ident")
        maskW = C("maskW").rearrange("p (t s) -> p t s", t=NT)
        fwd = C("fwd").rearrange("p (t i f) -> p t i f", t=NT, i=NFT + 1)
        bwd = C("bwd").rearrange("p (i t) -> p i t", i=4)
        sel = C("sel").rearrange("p (h m) -> p h m", h=AH)
        cosC = C("cosC").rearrange("p (t f) -> p t f", t=NT)
        sinC = C("sinC").rearrange("p (t f) -> p t f", t=NT)

        A_qk = W(0, 2048).rearrange("p (t n) -> p t n", t=NT)
        A_num = W(0, 2056).rearrange("p (t h n) -> p t h n", t=NT, h=AH)
        A_v = W(2056, 2056).rearrange("p (t h n) -> p t h n", t=NT, h=AH)
        A_o = W(4112, 2048).rearrange("p (t n) -> p t n", t=NT)
        A_qT = W(6160, 1024).rearrange("p (h t) -> p h t", h=AH)
        A_kT = W(7184, 1024).rearrange("p (h t) -> p h t", h=AH)
        A_D = W(8208, 768).rearrange("p (b n) -> p b n", b=2)
        A_P = W(8976, 768).rearrange("p (b n) -> p b n", b=2)
        A_dec = W(9744, 1024).rearrange("p (t n) -> p t n", t=NT)
        A_fb = W(10768, 2048).rearrange("p (b d n) -> p b d n", b=2, d=2)
        A_ed = W(12816, 4096).rearrange("p (o t d n) -> p o t d n", o=2, t=NT, d=2)
        A_sq = W(16912, 2048).rearrange("p (t d n) -> p t d n", t=NT, d=2)
        A_w3 = work[0:64, 18960:18960 + 2048]
        A_dg = W(18960, 1024).rearrange("p (c n) -> p c n", c=8)
        A_rn = W(9744, 1024).rearrange("p (o n) -> p o n", o=2)
        H = W(W_H, 2 * NFT * HW).rearrange("p (o i n) -> p o i n", o=2, i=NFT)
        fil = work[0:64, W_H + 1024:W_H + 2048].rearrange("p (i t) -> p i t", i=4)
        fw12 = work[0:64, W_H + 2048:W_H + 2176].rearrange("p (i n) -> p i n", i=2)
        gate = work[0:4, N_WORK - 2048:N_WORK].rearrange("p (i t) -> p i t", i=8)
        am = sm[:, 352:368].rearrange("p (t c) -> p t c", t=NT)
        glog = sm[:, 368:384].rearrange("p (t c) -> p t c", t=NT)

        B_q = W(0, 2048).rearrange("p (t n) -> p t n", t=NT)
        B_k = W(2048, 2048).rearrange("p (t n) -> p t n", t=NT)
        B_v = W(4096, 2048).rearrange("p (t n) -> p t n", t=NT)
        B_qT = W(6144, 2048).rearrange("p (h t) -> p h t", h=BH)
        B_kT = W(8192, 2048).rearrange("p (h t) -> p h t", h=BH)
        B_L = W(10240, 1152).rearrange("p (b n) -> p b n", b=3)
        B_PT = W(11392, 768).rearrange("p (b n) -> p b n", b=2)
        B_sq = W(12160, 1024).rearrange("p (t n) -> p t n", t=NT)
        B_z = W(13184, 256).rearrange("p (t h n) -> p t h n", t=NT, h=4)
        B_T1 = W(13440, 512).rearrange("p (k t n) -> p k t n", k=2, t=NT)
        B_T2 = W(13952, 128).rearrange("p (k t n) -> p k t n", k=2, t=NT)
        B_ang = W(14080, 192).rearrange("p (i t n) -> p i t n", i=6, t=NT)
        posi = sb("posi", [P, NT], I32)
        posf = sb("posf", [P, NT])

        C_p = W(0, 7680).rearrange("p (t n) -> p t n", t=NT)
        C_th = W(7680, 2048).rearrange("p (t n) -> p t n", t=NT)
        C_mg = W(9728, 2048).rearrange("p (t n) -> p t n", t=NT)
        C_sp = W(9728, 1024).rearrange("p (t n) -> p t n", t=NT)
        C_sn = W(10752, 1024).rearrange("p (t n) -> p t n", t=NT)
        C_qT = W(11776, 1024).rearrange("p (h t) -> p h t", h=4)
        C_kT = W(12800, 1024).rearrange("p (h t) -> p h t", h=4)
        C_cw = W(13824, 2048).rearrange("p (j n) -> p j n", j=4)
        C_Y = W(13824, 2048).rearrange("p (i n) -> p i n", i=4)
        C_tm = W(15872, 1024).rearrange("p (i n) -> p i n", i=2)
        C_L = W(13824, 2048).rearrange("p (b n) -> p b n", b=4)
        C_PT = W(15872, 1024).rearrange("p (b n) -> p b n", b=2)
        C_hd = W(16896, 1024).rearrange("p (o n) -> p o n", o=2)
        C_T1 = W(17920, 512).rearrange("p (k t n) -> p k t n", k=4, t=NT)
        C_T2 = W(18432, 512).rearrange("p (k t n) -> p k t n", k=4, t=NT)
        C_z = W(18944, 1024)
        C_kd = W(19456, 512).rearrange("p (t n) -> p t n", t=NT)
        C_oc = W(18944, 1024).rearrange("p (t n) -> p t n", t=NT)
        assert 18944 + 1024 <= W_H

        raw_loaded = [sem(f"raw_loaded{i}") for i in range(RAW)]
        hi_ready, lo_ready, unit_used = sem("hi_ready"), sem("lo_ready"), sem("unit_used")
        turned, turned_hi, turned_lo = sem("turned"), sem("turned_hi"), sem("turned_lo")
        x_ready, ssq_ready, rstd_ready = sem("x_ready"), sem("ssq_ready"), sem("rstd_ready")
        evac_act, evac_dve = sem("evac_act"), sem("evac_dve")
        hid_T, hid_hi, hid_lo = sem("hid_T"), sem("hid_hi"), sem("hid_lo")
        sil_ready, hid_ready = sem("sil_ready"), sem("hid_ready")

        def unit_view(tile, slot, w):
            return tile[:, slot, :].rearrange("p (k n) -> p k n", k=2)[:, :, 0:w]

        def unit_width(u):
            return 256 if U_C + 28 <= u < U_C + 32 else 512

        block = ctx.enter_context(nc.Block())

        @block.sync
        def _(sp):
            nc.sync.dma_start(con[:, 0:P], D["consts"][:, 0:P]).then_inc(sem("ident_loaded"), 16)
            xv = D["x"][0].rearrange("(t p) n -> p t n", p=P)
            for t in range(NT):
                nc.sync.dma_start(x[:, t, :], xv[:, t, :]).then_inc(sem(f"x_loaded{t}"), 16)

            def load(u, halves):
                if u >= RAW:
                    sp.wait_ge(lo_ready, u - RAW + 1)
                for dst, src in halves:
                    nc.sync.dma_start(dst, src).then_inc(raw_loaded[u % RAW], 16)

            def load_in(u0, w, n0, nw=512):
                for i in range(4):
                    v = unit_view(raw, (u0 + i) % RAW, nw)
                    load(u0 + i, [(v[:, kk, :], w[(2 * i + kk) * P:(2 * i + kk + 1) * P, n0:n0 + nw])
                                  for kk in range(2)])

            def load_out(u0, w, n):
                for k in range(n):
                    v = unit_view(raw, (u0 + k) % RAW, 512)
                    load(u0 + k, [(v[:, nb, :], w[k * P:(k + 1) * P, nb * 512:(nb + 1) * 512])
                                  for nb in range(2)])

            def load_ffn(u0, gate_w, gate_n0, up_w, up_n0, down_w):
                gv = gate_w.rearrange("(k p) n -> p k n", p=P)
                uv = up_w.rearrange("(k p) n -> p k n", p=P)
                dv = down_w.rearrange("(k p) n -> p k n", p=P)

                def up(slot, i, n):
                    dst = raw[:, slot, :].rearrange("p (k n) -> p k n", k=2)
                    return [(dst[:, :, 0:256], gv[:, 2 * i:2 * i + 2, bass.ds(n + gate_n0, 256)]),
                            (dst[:, :, 256:512], uv[:, 2 * i:2 * i + 2, bass.ds(n + up_n0, 256)])]

                for i in range(4):
                    load(u0 + i, up((u0 + i) % RAW, i, 0))
                with sp.Fori(1, FB) as j:
                    for c in range(6):
                        slot = (u0 + 4 + c) % RAW
                        sp.wait_ge(lo_ready, 6 * j + (u0 - 2 + c - RAW + 1))
                        if c < 4:
                            pairs = up(slot, c, j * 256)
                        else:
                            v = unit_view(raw, slot, 512)
                            src = dv[:, bass.ds(2 * j + (c - 6), 1), :]
                            pairs = [(v[:, nb:nb + 1, :], src[:, :, nb * 512:(nb + 1) * 512]) for nb in range(2)]
                        for dst, s in pairs:
                            nc.sync.dma_start(dst, s).then_inc(raw_loaded[slot], 16)
                for k in range(2):
                    u = u0 + 4 + 6 * (FB - 1) + k
                    v = unit_view(raw, u % RAW, 512)
                    load(u, [(v[:, nb, :], down_w[(2 * FB - 2 + k) * P:(2 * FB - 1 + k) * P, nb * 512:(nb + 1) * 512])
                             for nb in range(2)])

            for i in range(6):
                load_in(U_A + 4 * i, D["a_w_in"][0], 512 * i)
            load_out(U_AO, D["a_w_out"][0], KT)
            load_ffn(U_F0, D["ffn_w_in"][0], 0, D["ffn_w_in"][0], DFF, D["ffn_w_out"][0])
            for i in range(6):
                load_in(U_B + 4 * i, D["b_w_in"][0], 512 * i)
            load_out(U_BO, D["b_w_out"][0], KT)
            load_ffn(U_F1, D["ffn_w_in"][1], 0, D["ffn_w_in"][1], DFF, D["ffn_w_out"][1])
            w2 = D["w_in_2"][0]
            for i in range(7):
                load_in(U_C + 4 * i, w2, 512 * i)
            load_in(U_C + 28, w2, 3584, 256)
            for ug, uo, g0, wo in ((U_GA, U_OA, 3840, "w_oa_2"), (U_GB, U_OB, 4864, "w_ob_2"),
                                   (U_GC, U_OC, 5888, "w_oc_2")):
                load_in(ug, w2, g0)
                load_in(ug + 4, w2, g0 + 512)
                load_out(uo, D[wo][0], 4)
            load_out(U_W, D["w_out_2"][0], KT)
            load_ffn(U_F2, D["ffn_w1_2"][0], 0, D["ffn_w3_2"][0], 0, D["ffn_w2_2"][0])
            ov = out[0].rearrange("(t p) n -> p t n", p=P)
            for i in range(4):
                nb, t = divmod(i, 2)
                sp.wait_ge(x_ready, 20 + i + 1)
                nc.sync.dma_start(ov[:, t, nb * 512:(nb + 1) * 512], x[:, t, nb * 512:(nb + 1) * 512])\
                    .then_inc(sem(f"stored{i}"), 16)
            for i in range(4):
                sp.wait_ge(sem(f"stored{i}"), 16)

        @block.gpsimd
        def _(pool):
            nc.gpsimd.memset(grow[:, :], 0.0).then_inc(sem("grow_clear"), 1)
            pool.wait_ge(sem("grow_clear"), 1)
            rows = [("mix", D["norm_mix"].rearrange("l (k p) -> (l k) p", p=P), P),
                    ("ffn", D["norm_ffn"].rearrange("l (k p) -> (l k) p", p=P), P),
                    ("n1", D["norm1_g_2"].rearrange("l (k p) -> (l k) p", p=P), P),
                    ("n2", D["norm2_g_2"].rearrange("l (k p) -> (l k) p", p=P), P),
                    ("ago", D["a_g_out"].rearrange("l h (k p) -> (l h k) p", p=P), P),
                    ("subln", D["subln_c_2"], P), ("b1", D["filt_b1_2"], HD), ("f1", D["filt_f1_2"], HD),
                    ("b2", D["filt_b2_2"], HD), ("f2", D["filt_f2_2"], HD)]
            for name, src, w in rows:
                r = GROWS[name]
                nc.gpsimd.dma_start(grow[r:r + src.shape[0], 0:w], src).then_inc(sem("grow_loaded"), 16)
            nc.gpsimd.dma_start(wg[:, :, :], D["a_w_in"][0].rearrange("(k p) n -> p k n", p=P)[:, :, 3072:3080])\
                .then_inc(sem("wg_loaded"), 16)
            for name, src in (("bg", "a_b_gates"), ("gq", "b_g_q"), ("gk", "b_g_k"), ("qa", "qn_a_2"),
                              ("ka", "kn_a_2"), ("qc", "qn_c_2"), ("kc", "kn_c_2"), ("sink", "sink_a_2"),
                              ("lq1", "lam_q1_2"), ("lk1", "lam_k1_2"), ("lq2", "lam_q2_2"), ("lk2", "lam_k2_2")):
                n = PRM[name][1]
                nc.gpsimd.dma_start(R(name), D[src][0:1, :].to_broadcast([P, n])).then_inc(sem("prm_loaded"), 16)
            nc.gpsimd.dma_start(A_dec, D["decay"]).then_inc(sem("decay_loaded"), 16)
            nc.gpsimd.dma_start(A_w3, D["filt_w3_2"][0]).then_inc(sem("filt_loaded"), 16)
            nc.gpsimd.dma_start(fw12[0:33, 0, :], D["filt_w1_2"][0]).then_inc(sem("filt_loaded"), 16)
            nc.gpsimd.dma_start(fw12[:, 1, :], D["filt_w2_2"][0]).then_inc(sem("filt_loaded"), 16)
            nc.gpsimd.dma_start(posi[:, :], D["positions"][0].rearrange("(t p) -> p t", p=P), allow_slow_non_contiguous=True)\
                .then_inc(sem("pos_loaded"), 16)

            def filter_sums(i):
                o, t = divmod(i, 2)
                pool.wait_ge(sem("fb_ready"), 2 * i + 2)
                nc.gpsimd.tensor_tensor(A_ed[:, o, t, 0, :], A_fb[:, i % 2, 0, :], A_fb[:, i % 2, 1, :], ALU.add)\
                    .then_inc(sem("ed_ready"), 1)
                nc.gpsimd.tensor_tensor(A_ed[:, o, t, 1, :], A_fb[:, i % 2, 0, :], A_fb[:, i % 2, 1, :], ALU.subtract)\
                    .then_inc(sem("ed_ready"), 1)

            for i in range(4):
                filter_sums(i)
            for h in range(AH):
                pool.wait_ge(sem("a_p_ready"), h + 1)
                for c in (0, 256):
                    blk = A_P[:, h % 2, c:c + P]
                    nc.gpsimd.affine_select(out=blk, in_=blk, compare_op=ALU.is_ge, fill=0.0, base=0,
                                            pattern=[[1, P]], channel_multiplier=-1).then_inc(sem("a_p_masked"), 1)

            for b in range(4):
                dst, half = (B_q, b) if b < 2 else (B_k, b - 2)
                kind = b // 2
                pool.wait_ge(sem("b_swapped"), 2 * b + 2)
                pool.wait_ge(sem("b_sq"), 2 * b + 2)
                for t in range(NT):
                    y = dst[:, t, half * 512:(half + 1) * 512].rearrange("p (h d) -> p h d", h=4)
                    nc.gpsimd.tensor_tensor(y, y, B_T1[:, kind, t, :].unsqueeze(1).to_broadcast([P, 4, BD]),
                                            ALU.mult).then_inc(sem("b_scaled"), 1)

            def conv_part(c):
                cols = slice(c * HW, (c + 1) * HW)
                if c:
                    pool.wait_ge(sem("conv_done"), 2 * c)
                else:
                    pool.wait_ge(sem("c_tables"), 1)
                for j in range(3):
                    nc.gpsimd.dma_start(C_cw[:, j, :], D["conv_w_2"][0, j:j + 1, cols].to_broadcast([P, HW]))\
                        .then_inc(sem("taps_loaded"), 16)
                nc.gpsimd.dma_start(C_cw[:, 3, :], D["conv_b_2"][0:1, cols].to_broadcast([P, HW]))\
                    .then_inc(sem("taps_loaded"), 16)
                p0 = 768 + c * HW
                part = C_p[:, :, p0:p0 + HW]
                nc.gpsimd.memset(C_sp[0:1, 0, :], 0.0).then_inc(sem("edge_clear"), 1)
                nc.gpsimd.memset(C_sn[96:128, 1, :], 0.0).then_inc(sem("edge_clear"), 1)
                pool.wait_ge(sem("edge_clear"), 2 * c + 2)
                last = 12 + 2 + c
                pool.wait_ge(evac_act, ACT_EVACS[last])
                pool.wait_ge(evac_dve, DVE_EVACS[last])
                nc.gpsimd.dma_start(C_sp[1:P, :, :], part[0:P - 1, :, :]).then_inc(sem("shifted"), 16)
                nc.gpsimd.dma_start(C_sp[0:1, 1, :], part[P - 1:P, 0, :]).then_inc(sem("shifted"), 16)
                nc.gpsimd.dma_start(C_sn[0:P - 1, :, :], part[1:P, :, :]).then_inc(sem("shifted"), 16)
                nc.gpsimd.dma_start(C_sn[P - 1:P, 0, :], part[0:1, 1, :]).then_inc(sem("shifted"), 16)
                pool.wait_ge(sem("taps_loaded"), 64 * (c + 1))
                pool.wait_ge(sem("shifted"), 64 * (c + 1))

                def tap(j):
                    return C_cw[:, j:j + 1, :].to_broadcast([P, NT, HW])

                nc.gpsimd.tensor_tensor(C_sp, C_sp, tap(0), ALU.mult).then_inc(sem("tap0_done"), 1)
                pool.wait_ge(sem("conv_sum"), c + 1)
                nc.gpsimd.tensor_tensor(part, part, tap(3), ALU.add).then_inc(sem("conv_done"), 2)

            nc.gpsimd.dma_start(C_hd[:, 0, :], D["hy_d_2"][0, 0:1, :].to_broadcast([P, HW]))\
                .then_inc(sem("hyd_loaded"), 16)
            nc.gpsimd.dma_start(C_hd[:, 1, :], D["hy_d_2"][0, 1:2, :].to_broadcast([P, HW]))\
                .then_inc(sem("hyd_loaded"), 16)
            for c in range(3):
                conv_part(c)

        @block.scalar
        def _(act):
            a_ = nc.scalar.activation
            steps = [0]

            def link(ins):
                steps[0] += 1
                ins.then_inc(sem("act_step"), 1)
                act.wait_ge(sem("act_step"), steps[0])

            nc.scalar.dma_start(con[:, P:N_FIRST], D["consts"][:, P:N_FIRST]).then_inc(sem("con1_loaded"), 16)
            nc.scalar.dma_start(con[:, N_FIRST:], D["consts"][:, N_FIRST:]).then_inc(sem("con2_loaded"), 16)

            fed = [0]

            def split_hi(u, slot_raw, slot, loaded, used, w=512):
                act.wait_ge(raw_loaded[slot_raw], loaded)
                if used is not None:
                    act.wait_ge(unit_used, used)
                a_(unit_view(whi, slot, w), unit_view(raw, slot_raw, w), ACT.Copy).then_inc(hi_ready, 1)

            def feed(n):
                for u in range(fed[0], n):
                    split_hi(u, u % RAW, u % SPL, 32 * (u // RAW + 1), u - SPL + 1 if u >= SPL else None,
                             unit_width(u))
                fed[0] = max(fed[0], n)

            def turn_hi(use, scale):
                for p in range(4):
                    act.wait_ge(turned, 4 * use + p + 1)
                    for f in range(2):
                        a_(ath[:, 2 * p + f, :], ps[TBANKS[p]][:, f * S:(f + 1) * S], ACT.Copy,
                           scale=scale(2 * p + f)).then_inc(turned_hi, 1)

            def squares(n):
                for t in range(NT):
                    if n == 0:
                        act.wait_ge(sem(f"x_loaded{t}"), 16)
                    else:
                        act.wait_ge(x_ready, 4 * n)
                    a_(W(t * DM, DM), x[:, t, :], ACT.Square, accum_out=ssq[:, n, t:t + 1]).then_inc(ssq_ready, 1)

            def evac(i, dst, func=ACT.Copy, n=0, tiles=(0,), scale=None):
                u0, w, bk = IN_BLOCKS[i]
                act.wait_ge(unit_used, u0 + 4)
                act.wait_ge(rstd_ready, n + 1)
                for t in tiles:
                    a_(dst(t), ps[bk + t][:, 0:w] if scale is None else ps[bk + t][:, 0:w], func,
                       scale=(rstd if scale is None else scale)[:, n, t:t + 1]).then_inc(evac_act, 1)

            def ffn(n, u0, norm):
                def silu(wait_units):
                    act.wait_ge(unit_used, wait_units)
                    for t in range(NT):
                        a_(sil[:, t, :], ps[t][:, 0:256], ACT.Silu, scale=rstd[:, norm, t:t + 1])\
                            .then_inc(sil_ready, 1)

                def turn(count):
                    act.wait_ge(hid_T, count)
                    a_(brh[:, 0:2, :], ps[2][:, :].rearrange("p (f t) -> p f t", f=2), ACT.Copy)\
                        .then_inc(hid_hi, 1)

                feed(u0 + 5)
                act.wait_ge(rstd_ready, norm + 1)
                silu(u0 + 4)
                with act.Fori(1, FB) as j:
                    def split(c):
                        v = u0 + 4 + c
                        split_hi(v, v % RAW, v % SPL, 32 * j + 32 * (v // RAW), 6 * j + (u0 - 2 + c - SPL + 1))
                    for c in range(1, 5):
                        split(c)
                    turn(j + FB * n)
                    for c in range(5, 7):
                        split(c)
                    silu(6 * j + (u0 - 2 + 4))
                last = u0 + 4 + 6 * (FB - 1)
                fed[0] = last + 1
                feed(last + 2)
                turn(FB * (n + 1))
                feed(last + 5 if last + 5 <= U_END else U_END)

            act.wait_ge(sem("cols_turned"), 1)
            a_(gcol[:, :], ps[6][:, 0:64], ACT.Copy).then_inc(sem("gcol_ready"), 1)
            act.wait_ge(sem("gcol_ready"), 1)
            feed(3)
            turn_hi(0, lambda f: gcol[:, GROWS["mix"] + f:GROWS["mix"] + f + 1])
            squares(0)
            feed(7)
            evac(0, lambda t: A_qk[:, t, 0:512])
            act.wait_ge(sem("f_arg"), 1)
            a_(fil[:, 2, :], fil[:, 0, :], ACT.Sin).then_inc(sem("f_hidden"), 1)
            feed(11)
            evac(1, lambda t: A_qk[:, t, 512:1024])

            def copy_qk(dst, n):
                act.wait_ge(sem("a_qk_turned"), n + 1)
                for c in range(2):
                    a_(dst[:, 2 * c:2 * c + 2, :], ps[4 + c][:, :].rearrange("p (h t) -> p h t", h=2), ACT.Copy)\
                        .then_inc(sem("a_qk_copied"), 1)

            copy_qk(A_qT, 0)
            act.wait_ge(sem("g_abs"), 1)
            link(a_(gate[:, 3, :], gate[:, 2, :], ACT.Exp, scale=-1.0))
            a_(gate[:, 2, :], gate[:, 3, :], ACT.Ln, bias=1.0).then_inc(sem("g_ln"), 1)
            act.wait_ge(sem("f_arg"), 2)
            a_(fil[:, 3, :], fil[:, 0, :], ACT.Sin).then_inc(sem("f_hidden"), 1)
            feed(13)
            copy_qk(A_kT, 1)
            act.wait_ge(sem("g_m"), 1)
            a_(gate[:, 7, :], gate[:, 3, :], ACT.Exp, scale=-1.0).then_inc(sem("g_em"), 1)
            feed(15)

            def v_dst(b):
                return lambda t: A_v[:, t, 2 * b:2 * b + 2, 0:ADV]

            def evac_v(i, b):
                u0, w, bk = IN_BLOCKS[i]
                act.wait_ge(unit_used, u0 + 4)
                a_(v_dst(b)(0), ps[bk][:, :].rearrange("p (h n) -> p h n", h=2), ACT.Copy,
                   scale=rstd[:, 0, 0:1]).then_inc(evac_act, 1)

            def filter_squares(i):
                o, t = divmod(i, 2)
                act.wait_ge(sem("ed_ready"), 2 * i + 2)
                if i >= 2:
                    act.wait_ge(sem("f_norm"), 1)
                for d in range(2):
                    a_(A_sq[:, t, d, :], A_ed[:, o, t, d, :], ACT.Square).then_inc(sem("f_sq"), 1)

            evac_v(2, 0)
            feed(17)
            filter_squares(0)
            feed(19)
            evac_v(3, 1)
            filter_squares(1)
            feed(21)
            feed(23)
            evac(4, lambda t: A_o[:, t, 0:512], ACT.Tanh, 0, (0, 1), rhalf)
            filter_squares(2)
            filter_squares(3)
            feed(24)

            def a_weights(h):
                act.wait_ge(sem("a_d_ready"), h + 1)
                a_(A_D[:, h % 2, :], A_D[:, h % 2, :], ACT.Exp, scale=-1.0).then_inc(sem("a_e_ready"), 1)

            a_weights(0)
            a_weights(1)
            evac(5, lambda t: A_o[:, t, 512:1024], ACT.Tanh, 0, (0, 1), rhalf)
            feed(U_AO + 3)
            act.wait_ge(sem("rn_spread"), 1)
            for o in range(2):
                a_(A_rn[:, o, :], ps[o][:, :], ACT.Copy).then_inc(sem("rn_ready"), 1)

            def a_norms(h):
                for t in range(NT):
                    act.wait_ge(sem("a_pv"), 2 * h + t + 1)
                    a_(W(10768 + 256 * (2 * h + t), 256), ps[(6, 4)[t] + h % 2][:, 0:ADV], ACT.Square,
                       accum_out=sm[:, 32 + 4 * t + h:33 + 4 * t + h]).then_inc(sem("a_ssq"), 1)

            a_norms(0)
            a_norms(1)
            a_weights(2)
            a_weights(3)
            a_norms(2)
            a_norms(3)
            turn_hi(1, lambda f: gcol[:, GROWS["ago"] + f:GROWS["ago"] + f + 1])
            feed(U_F0 + 3)
            turn_hi(2, lambda f: gcol[:, GROWS["ffn"] + f:GROWS["ffn"] + f + 1])
            squares(1)
            ffn(0, U_F0, 1)

            turn_hi(3, lambda f: gcol[:, GROWS["mix"] + 8 + f:GROWS["mix"] + 9 + f])
            squares(2)
            act.wait_ge(sem("b_args"), 1)
            a_(B_ang[:, 4, :, :], B_ang[:, 2, :, :], ACT.Sin).then_inc(sem("b_sines"), 1)
            a_(B_ang[:, 5, :, :], B_ang[:, 3, :, :], ACT.Sin).then_inc(sem("b_sines"), 1)

            def b_squares(b):
                dst, half = (B_q, b) if b < 2 else (B_k, b - 2)
                act.wait_ge(evac_dve, DVE_EVACS[6 + b])
                act.wait_ge(evac_act, ACT_EVACS[6 + b])
                if b:
                    act.wait_ge(sem("b_ssq"), 2 * b)
                for t in range(NT):
                    a_(B_sq[:, t, :], dst[:, t, half * 512:(half + 1) * 512], ACT.Square)\
                        .then_inc(sem("b_sq"), 1)

            def b_copy(b):
                dst, half = (B_qT, b) if b < 2 else (B_kT, b - 2)
                act.wait_ge(sem("b_turned"), b + 1)
                a_(dst[:, 4 * half:4 * half + 2, :], ps[4 + 2 * (b % 2)][:, :].rearrange("p (h t) -> p h t", h=2),
                   ACT.Copy).then_inc(sem("b_copied_act"), 1)

            for b in range(4):
                dst, half = (B_q, b) if b < 2 else (B_k, b - 2)
                feed(U_B + 4 * b + 7)
                evac(6 + b, lambda t: dst[:, t, half * 512:(half + 1) * 512], n=2)
                b_squares(b)
                if 1 <= b < 3:
                    b_copy(b - 1)
            feed(U_B + 23)
            evac(10, lambda t: B_v[:, t, 0:512], n=2)
            b_copy(2)
            b_copy(3)
            feed(U_BO + 3)
            evac(11, lambda t: B_v[:, t, 512:1024], n=2)

            def b_exp(h):
                act.wait_ge(sem("b_max"), h + 1)
                c = sm[:, 64 + 8 * (h % 3):]
                for t, (lo, hi) in enumerate(((0, P), (P, 3 * P))):
                    a_(B_L[:, h % 3, lo:hi], B_L[:, h % 3, lo:hi], ACT.Exp, bias=c[:, t:t + 1],
                       accum_out=c[:, 2 + t:3 + t]).then_inc(sem("b_exp"), 1)

            def b_pt(h):
                act.wait_ge(sem("b_p_turned"), h + 1)
                a_(B_PT[:, h % 2, :], ps[6 + h % 2][:, 0:384], ACT.Copy).then_inc(sem("b_pt"), 1)

            def b_out(h):
                act.wait_ge(sem("b_pv"), h + 1)
                a_(ath[:, h, :], ps[h % 2][:, 0:S], ACT.Copy).then_inc(sem("b_out_hi"), 1)

            for i in range(BH + 2):
                if i < BH:
                    b_exp(i)
                if 0 <= i - 1 < BH:
                    b_pt(i - 1)
                if 0 <= i - 2 < BH:
                    b_out(i - 2)
            feed(U_F1 + 3)
            turn_hi(4, lambda f: gcol[:, GROWS["ffn"] + 8 + f:GROWS["ffn"] + 9 + f])
            squares(3)
            ffn(1, U_F1, 3)

            turn_hi(5, lambda f: gcol[:, GROWS["n1"] + f:GROWS["n1"] + f + 1])
            squares(4)

            def c_evac(i):
                evac(12 + i, lambda t: C_p[:, t, 512 * i:512 * i + IN_BLOCKS[12 + i][1]], n=4)

            def c_squares(g, c0, c1):
                for t in range(NT):
                    if t or g:
                        act.wait_ge(sem("c_ssq"), 2 * g + t)
                    a_(C_z[:, 0:c1 - c0], C_p[:, t, c0:c1], ACT.Square)\
                        .then_inc(sem("c_sq"), 1)

            feed(U_C + 7)
            c_evac(0)
            feed(U_C + 11)
            c_evac(1)
            act.wait_ge(evac_dve, DVE_EVACS[13])
            act.wait_ge(evac_act, ACT_EVACS[13])
            c_squares(0, 0, 640)
            feed(U_C + 15)
            c_evac(2)
            feed(U_C + 19)
            c_evac(3)
            act.wait_ge(sem("c_w_turned"), 1)
            for c in range(2):
                a_(C_qT[:, 2 * c:2 * c + 2, :], ps[4 + c][:, :].rearrange("p (h t) -> p h t", h=2), ACT.Copy)\
                    .then_inc(sem("c_w_copied"), 1)
            a_(C_kT[:, 0:2, :], ps[6][:, :].rearrange("p (h t) -> p h t", h=2), ACT.Copy).then_inc(sem("c_w_copied"), 1)
            feed(U_C + 23)
            c_evac(4)
            feed(U_C + 27)
            c_evac(5)
            feed(U_C + 31)
            c_evac(6)
            act.wait_ge(evac_dve, DVE_EVACS[18])
            act.wait_ge(evac_act, ACT_EVACS[18])
            c_squares(1, 2304, 3328)
            feed(U_C + 35)
            c_evac(7)

            def gate_evac(i, half):
                u0, w, bk = IN_BLOCKS[i]
                act.wait_ge(unit_used, u0 + 4)
                for t in range(NT):
                    a_(C_th[:, t, half * 512:(half + 1) * 512], ps[bk + t][:, :], ACT.Tanh,
                       scale=rhalf[:, 4, t:t + 1]).then_inc(evac_act, 1)

            def w_exp(h):
                act.wait_ge(sem("w_max"), h + 1)
                c = sm[:, 128 + 16 * (h % 2):]
                for t in range(NT):
                    a_(C_L[:, h % 2, t * S:(t + 1) * S], C_L[:, h % 2, t * S:(t + 1) * S], ACT.Exp,
                       bias=c[:, 2 + t:3 + t], accum_out=c[:, 4 + t:5 + t]).then_inc(sem("w_exp"), 1)
                a_(c[:, 6:8], c[:, 2:4], ACT.Exp, bias=R("sink")[:, h:h + 1]).then_inc(sem("w_exp"), 1)

            def w_pt(h):
                act.wait_ge(sem("w_p_turned"), h + 1)
                a_(C_PT[:, h % 2, :], ps[6 + h % 2][:, :], ACT.Copy).then_inc(sem("w_pt"), 1)

            def w_out(i):
                act.wait_ge(sem("w_pv"), 2 * i + 2)
                a_(brh[:, i, :], ps[2 + i % 2][:, 0:S], ACT.Copy).then_inc(sem("w_out_hi"), 1)

            for i in range(WQ + 2):
                feed(U_GA + min(i + 3, 11))
                if i < WQ:
                    w_exp(i)
                if 0 <= i - 1 < WQ:
                    w_pt(i - 1)
                if i == 4:
                    gate_evac(20, 0)
                if i == 8:
                    gate_evac(21, 1)
                if i >= 3 and i % 2 == 1:
                    w_out((i - 3) // 2)
            feed(U_OA + 3)

            feed(U_GB + 5)
            feed(U_GB + 7)
            act.wait_ge(sem("merged"), 4)
            gate_evac(22, 0)
            feed(U_GB + 11)
            gate_evac(23, 1)
            for p in range(2):
                act.wait_ge(sem("h_turned"), p + 1)
                a_(brh[:, 2 * p:2 * p + 2, :], ps[6 + p][:, :].rearrange("p (f t) -> p f t", f=2), ACT.Copy)\
                    .then_inc(sem("h_hi"), 1)
            feed(U_GC + 1)

            act.wait_ge(sem("lam_dots"), 2)
            a_(sm[:, 202:204], sm[:, 200:202], ACT.Exp).then_inc(sem("lam_exps"), 1)

            def d_copy():
                for c in range(2):
                    act.wait_ge(sem("d_turned"), c + 1)
                    for hh in range(2):
                        a_((C_qT, C_kT)[c][:, 2 * hh:2 * hh + 2, :],
                           ps[4 + 2 * c + hh][:, :].rearrange("p (h t) -> p h t", h=2), ACT.Copy)\
                            .then_inc(sem("d_copied"), 1)

            d_copy()

            def d_exp(h):
                act.wait_ge(sem("d_max"), h + 1)
                c = sm[:, 208 + 32 * (h % 2):]
                for comp in range(2):
                    for t in range(NT):
                        i = 2 * comp + t
                        a_(C_L[:, 2 * (h % 2) + comp, t * S:(t + 1) * S], ps[4 + comp][:, t * S:(t + 1) * S], ACT.Exp,
                           scale=c[:, 4 + i:5 + i], bias=c[:, 8 + i:9 + i], accum_out=c[:, 12 + i:13 + i])\
                            .then_inc(sem("d_exp"), 1)

            def d_pt(h):
                act.wait_ge(sem("d_p_turned"), h + 1)
                a_(C_PT[:, h % 2, :], ps[6 + h % 2][:, :], ACT.Copy).then_inc(sem("d_pt"), 1)

            def d_out(h):
                act.wait_ge(sem("d_pv"), h + 1)
                for t in range(NT):
                    a_((sil, hid)[h // 2][:, h % 2, t * P:(t + 1) * P], ps[2 + h % 2][:, t * P:(t + 1) * P], ACT.Square,
                       accum_out=sm[:, 272 + 4 * t + h:273 + 4 * t + h]).then_inc(sem("d_ssq"), 1)
                a_(C_oc[:, :, h * P:(h + 1) * P], ps[2 + h % 2][:, 0:S].rearrange("p (t n) -> p t n", t=NT),
                   ACT.Copy).then_inc(sem("d_oc"), 1)

            for i in range(CH + 2):
                feed(U_GC + min(2 * i + 3, 11))
                if i < CH:
                    d_exp(i)
                if i == 2:
                    act.wait_ge(sem("merged"), 8)
                    gate_evac(24, 0)
                if 0 <= i - 1 < CH:
                    d_pt(i - 1)
                if i == 4:
                    gate_evac(25, 1)
                if 0 <= i - 2 < CH:
                    d_out(i - 2)
            act.wait_ge(sem("sub_ready"), 1)
            for p in range(2):
                act.wait_ge(sem("c_turned"), p + 1)
                a_(brh[:, 2 * p:2 * p + 2, :], ps[6 + p][:, :].rearrange("p (f t) -> p f t", f=2), ACT.Copy,
                   scale=sm[:, 280:281]).then_inc(sem("c_hi"), 1)
            feed(U_W + 3)
            turn_hi(6, lambda f: 0.5)
            feed(U_F2 + 3)
            turn_hi(7, lambda f: gcol[:, GROWS["n2"] + f:GROWS["n2"] + f + 1])
            squares(5)
            ffn(2, U_F2, 5)

        @block.vector
        def _(dve):
            v_ = nc.vector
            steps = [0]

            def link(ins):
                steps[0] += 1
                ins.then_inc(sem("dve_step"), 1)
                dve.wait_ge(sem("dve_step"), steps[0])

            fed = [0]

            def split_lo(u, slot_raw, slot, ready, w=512):
                dve.wait_ge(hi_ready, ready)
                v_.tensor_tensor(unit_view(wlo, slot, w), unit_view(raw, slot_raw, w), unit_view(whi, slot, w),
                                 ALU.subtract).then_inc(lo_ready, 1)

            def feed(n):
                for u in range(fed[0], n):
                    split_lo(u, u % RAW, u % SPL, u + 1, unit_width(u))
                fed[0] = max(fed[0], n)

            def turn_lo(use, scale):
                for p in range(4):
                    dve.wait_ge(turned_hi, 8 * use + 2 * p + 2)
                    for f in range(2):
                        v_.scalar_tensor_tensor(atl[:, 2 * p + f, :], ps[TBANKS[p]][:, f * S:(f + 1) * S],
                                                scale(2 * p + f), ath[:, 2 * p + f, :], ALU.mult, ALU.subtract)\
                            .then_inc(turned_lo, 1)

            def rsqrt(dst, n):
                a, t = rq_a[:, 0:n], rq_t[:, 0:n]
                link(v_.tensor_scalar(t.bitcast(I32), a.bitcast(I32), 1, None, ALU.logical_shift_right))
                link(v_.tensor_scalar(dst.bitcast(I32), t.bitcast(I32), -1.0, float(0x5F3759DF), ALU.mult, ALU.add))
                for _ in range(3):
                    link(v_.tensor_tensor(t, dst, dst, ALU.mult))
                    link(v_.scalar_tensor_tensor(t, t, -0.5, a, ALU.mult, ALU.mult))
                    link(v_.scalar_tensor_tensor(dst, t, 1.5, dst, ALU.add, ALU.mult))

            def row_scale(n):
                dve.wait_ge(ssq_ready, 2 * (n + 1))
                link(v_.tensor_scalar(rq_a[:, 0:NT], ssq[:, n, :], 1.0 / DM, EPS, ALU.mult, ALU.add))
                rsqrt(rstd[:, n, :], NT)
                v_.tensor_scalar(rhalf[:, n, :], rstd[:, n, :], 0.5, None, ALU.mult).then_inc(rstd_ready, 1)
                dve.wait_ge(rstd_ready, n + 1)

            def evac(i, dst, n=0):
                u0, w, bk = IN_BLOCKS[i]
                dve.wait_ge(unit_used, u0 + 4)
                src = ps[bk + 1][:, 0:w]
                if len(dst.shape) == 3:
                    src = src.rearrange("p (h n) -> p h n", h=dst.shape[1])
                v_.tensor_scalar(dst, src, rstd[:, n, 1:2], None, ALU.mult).then_inc(evac_dve, 1)

            def residual(r, u_last):
                dve.wait_ge(unit_used, u_last)
                for nb in range(2):
                    for t in range(NT):
                        xs = x[:, t, nb * 512:(nb + 1) * 512]
                        v_.tensor_tensor(xs, xs, ps[4 + 2 * nb + t][:, :], ALU.add).then_inc(x_ready, 1)

            def ffn(n, u0, norm):
                def hidden(count):
                    for t in range(NT):
                        dve.wait_ge(sil_ready, count + t + 1)
                        v_.scalar_tensor_tensor(hid[:, t, :], ps[t][:, 256:512], rstd[:, norm, t:t + 1], sil[:, t, :],
                                                ALU.mult, ALU.mult).then_inc(hid_ready, 1)

                def turn(count):
                    dve.wait_ge(hid_hi, count)
                    v_.tensor_tensor(brl[:, 0:2, :], ps[2][:, :].rearrange("p (f t) -> p f t", f=2), brh[:, 0:2, :],
                                     ALU.subtract).then_inc(hid_lo, 1)

                feed(u0 + 5)
                hidden(2 * FB * n)
                with dve.Fori(1, FB) as j:
                    def split(c):
                        v = u0 + 4 + c
                        split_lo(v, v % RAW, v % SPL, 6 * j + (u0 - 2 + c + 1))
                    for c in range(1, 5):
                        split(c)
                    turn(j + FB * n)
                    for c in range(5, 7):
                        split(c)
                    hidden(2 * j + 2 * FB * n)
                last = u0 + 4 + 6 * (FB - 1)
                fed[0] = last + 1
                feed(last + 2)
                turn(FB * (n + 1))
                feed(last + 5 if last + 5 <= U_END else U_END)

            def turns(arg, k, cos, red):
                link(v_.tensor_scalar(k, arg, 1.0 / TWO_PI, 0.25 if cos else 0.0, ALU.mult, ALU.add))
                link(v_.tensor_scalar(k, k, MAGIC, MAGIC, ALU.add, ALU.subtract))
                link(v_.scalar_tensor_tensor(red, k, -C1, arg, ALU.mult, ALU.add))
                link(v_.scalar_tensor_tensor(red, k, -C2, red, ALU.mult, ALU.add))
                link(v_.scalar_tensor_tensor(red, k, -C3, red, ALU.mult, ALU.add))
                if cos:
                    link(v_.tensor_scalar(red, red, math.pi / 2, None, ALU.add))
                return v_.tensor_scalar(red, red, PI_IN, -PI_IN, ALU.min, ALU.max)

            v_.memset(A_v[:, :, :, ADV:ADV + 1], 1.0).then_inc(sem("a_ones"), 1)
            dve.wait_ge(sem("wg_loaded"), 16)
            v_.tensor_copy(wgh[:, :, :], wg[:, :, :]).then_inc(sem("wg_split"), 1)
            dve.wait_ge(sem("wg_split"), 1)
            v_.tensor_tensor(wgl[:, :, :], wg[:, :, :], wgh[:, :, :], ALU.subtract).then_inc(sem("wg_split"), 1)
            feed(3)
            turn_lo(0, lambda f: gcol[:, GROWS["mix"] + f:GROWS["mix"] + f + 1])
            row_scale(0)
            feed(7)
            evac(0, A_qk[:, 1, 0:512])

            dve.wait_ge(sem("gl_ready"), 1)
            dve.wait_ge(sem("prm_loaded"), 16 * len(PRM))
            for t in range(NT):
                v_.scalar_tensor_tensor(glog[:, t, :], ps[6][:, 8 * t:8 * t + 8], rstd[:, 0, t:t + 1], R("bg"),
                                        ALU.mult, ALU.add).then_inc(sem("glog"), 1)

            def filter_arg(i, bk):
                dve.wait_ge(sem("f_mm"), i + 1)
                b, f = GROWS["b1"] + 2 * i, GROWS["f1"] + 2 * i
                if i:
                    dve.wait_ge(sem("f_hidden"), i)
                link(v_.tensor_scalar(fil[:, 0, :], ps[bk][0:64, 0:S], gcol[0:64, b:b + 1], gcol[0:64, f:f + 1],
                                      ALU.add, ALU.mult))
                turns(fil[:, 0, :], fil[:, 1, :], False, fil[:, 0, :]).then_inc(sem("f_arg"), 1)

            filter_arg(0, 7)
            feed(11)
            evac(1, A_qk[:, 1, 512:1024])
            dve.wait_ge(sem("gl_turned"), 1)
            v_.tensor_copy(gate[:, 0, :], ps[7][0:4, 0:S]).then_inc(sem("g_rows"), 1)
            v_.tensor_copy(gate[:, 1, :], ps[7][0:4, S:2 * S]).then_inc(sem("g_rows"), 1)
            dve.wait_ge(sem("g_rows"), 2)
            v_.scalar_tensor_tensor(gate[:, 2, :], gate[:, 1, :], -1.0, gate[:, 1, :], ALU.mult, ALU.max)\
                .then_inc(sem("g_abs"), 1)
            filter_arg(1, 6)
            dve.wait_ge(sem("g_ln"), 1)
            link(v_.scalar_tensor_tensor(gate[:, 1, :], gate[:, 1, :], 0.0, gate[:, 2, :], ALU.min, ALU.subtract))
            dve.wait_ge(sem("con1_loaded"), 16)
            link(v_.tensor_tensor_scan(gate[:, 4, :], con[0:4, CONSTS["ones"][0]:CONSTS["ones"][0] + 1]
                                       .to_broadcast([4, S]), gate[:, 1, :], 0.0, ALU.mult, ALU.add))
            link(v_.tensor_tensor(gate[:, 5, :], gate[:, 0, :], gate[:, 4, :], ALU.subtract))
            link(v_.tensor_tensor_scan(gate[:, 6, :], gate[:, 5, :], gate[:, 5, :], 0.0, ALU.max, ALU.max))
            v_.tensor_tensor(gate[:, 3, :], gate[:, 4, :], gate[:, 6, :], ALU.add).then_inc(sem("g_m"), 1)
            feed(15)
            evac(2, A_v[:, 1, 0:2, 0:ADV])
            dve.wait_ge(sem("decay_loaded"), 16)

            def filter_decay(i):
                t = i % 2
                dve.wait_ge(sem("f3"), i + 1)
                if i >= 2:
                    dve.wait_ge(sem("ed_ready"), 2 * (i - 1))
                for d in range(2):
                    v_.tensor_tensor(A_fb[:, i % 2, d, :], ps[(4, 6)[i % 2] + d][:, :], A_dec[:, t, :], ALU.mult)\
                        .then_inc(sem("fb_ready"), 1)

            filter_decay(0)
            feed(17)
            filter_decay(1)
            feed(19)
            evac(3, A_v[:, 1, 2:4, 0:ADV])
            filter_decay(2)
            feed(21)
            filter_decay(3)
            dve.wait_ge(sem("am_turned"), 1)
            v_.tensor_copy(am[:, :, :], ps[5][:, 0:16].rearrange("p (t c) -> p t c", t=NT)).then_inc(sem("am_ready"), 1)
            feed(23)
            dve.wait_ge(sem("f_norm"), 2)
            link(v_.tensor_scalar(rq_a[:, 0:8], ps[4][:, 0:8], EPS, None, ALU.add))
            rsqrt(sm[:, 0:8], 8)
            for c in range(8):
                v_.tensor_scalar(A_dg[:, c, :], ident, sm[:, c:c + 1], None, ALU.mult).then_inc(sem("dg_ready"), 1)
            feed(24)

            def a_dist(h):
                dve.wait_ge(sem("a_scores"), h + 1)
                dve.wait_ge(sem("am_ready"), 1)
                if h >= 2:
                    dve.wait_ge(sem("a_p_ready"), h - 1)
                mb = ps[4 + h % 2]
                v_.tensor_scalar(A_D[:, h % 2, 0:S], mb[:, 0:S], am[:, 0, h:h + 1], 0.0, ALU.subtract, ALU.max)\
                    .then_inc(sem("a_d0"), 1)
                v_.tensor_scalar(A_D[:, h % 2, S:384], mb[:, P:S], am[:, 1, h:h + 1], 0.0, ALU.subtract, ALU.max)\
                    .then_inc(sem("a_d_ready"), 1)

            def a_prob(h):
                dve.wait_ge(sem("a_e_ready"), h + 1)
                if h >= 2:
                    dve.wait_ge(sem("a_pv"), 2 * (h - 1))
                v_.scalar_tensor_tensor(A_P[:, h % 2, :], ps[6 + h % 2][:, 0:384], float(ADK) ** -0.5, A_D[:, h % 2, :],
                                        ALU.mult, ALU.mult).then_inc(sem("a_p_ready"), 1)

            def a_num(h):
                for t in range(NT):
                    dve.wait_ge(sem("a_ssq"), 2 * h + t + 1)
                    v_.tensor_copy(A_num[:, t, h, :], ps[(6, 4)[t] + h % 2][:, 0:ADV + 1]).then_inc(sem("a_num"), 1)

            def spectrum(i):
                dve.wait_ge(sem("spec"), i + 1)
                dve.wait_ge(sem("rn_ready"), 2)
                o, f = divmod(i, NFT)
                v_.tensor_tensor(H[:, o, f, :], ps[2 + i % 2][:, :], A_rn[:, o, :], ALU.mult).then_inc(sem("spec_ready"), 1)

            a_dist(0)
            a_dist(1)
            a_prob(0)
            a_prob(1)
            feed(U_AO + 3)
            spectrum(0)
            spectrum(1)
            a_num(0)
            a_num(1)
            spectrum(2)
            a_dist(2)
            a_dist(3)
            a_prob(2)
            a_prob(3)
            for i in range(3, 6):
                spectrum(i)
            a_num(2)
            a_num(3)
            dve.wait_ge(sem("a_num"), 8)
            dve.wait_ge(sem("a_ssq"), 8)
            dve.wait_ge(evac_act, ACT_EVACS[5])
            den = A_num[:, :, :, ADV]
            r8 = sm[:, 8:16].rearrange("p (t h) -> p t h", t=NT)
            link(v_.tensor_copy(r8, den))
            link(v_.scalar_tensor_tensor(r8, r8, -1.0, r8, ALU.mult, ALU.max))
            link(v_.tensor_tensor(r8, r8, am[:, :, 4:8], ALU.max))
            link(v_.reciprocal(sm[:, 16:24], sm[:, 8:16]))
            link(v_.tensor_tensor(sm[:, 24:32], sm[:, 16:24], sm[:, 16:24], ALU.mult))
            link(v_.tensor_tensor(rq_a[:, 0:8], sm[:, 24:32], sm[:, 32:40], ALU.mult))
            link(v_.tensor_scalar(rq_a[:, 0:8], rq_a[:, 0:8], 1.0 / ADV, EPS, ALU.mult, ALU.add))
            rsqrt(sm[:, 40:48], 8)
            link(v_.scalar_tensor_tensor(sm[:, 48:56], sm[:, 40:48], 0.5, sm[:, 16:24], ALU.mult, ALU.mult))
            for h in range(AH):
                for t in range(NT):
                    o = A_o[:, t, h * ADV:(h + 1) * ADV]
                    n = A_num[:, t, h, 0:ADV]
                    link(v_.scalar_tensor_tensor(o, o, 1.0, n, ALU.add, ALU.mult))
                    v_.tensor_scalar(o, o, sm[:, 48 + 4 * t + h:49 + 4 * t + h], None, ALU.mult)\
                        .then_inc(sem("a_y"), 1)
            turn_lo(1, lambda f: gcol[:, GROWS["ago"] + f:GROWS["ago"] + f + 1])
            for i in range(6, 10):
                spectrum(i)
            feed(U_F0 + 3)
            residual(0, U_F0)
            turn_lo(2, lambda f: gcol[:, GROWS["ffn"] + f:GROWS["ffn"] + f + 1])
            row_scale(1)
            ffn(0, U_F0, 1)

            residual(1, U_B)
            turn_lo(3, lambda f: gcol[:, GROWS["mix"] + 8 + f:GROWS["mix"] + 9 + f])
            row_scale(2)
            dve.wait_ge(sem("pos_loaded"), 16)
            dve.wait_ge(sem("con2_loaded"), 16)
            link(v_.tensor_copy(posf[:, :], posi[:, :]))
            for t in range(NT):
                link(v_.tensor_scalar(B_ang[:, 0, t, :], C("inv"), posf[:, t:t + 1], None, ALU.mult))
            link(turns(B_ang[:, 0, :, :], B_ang[:, 1, :, :], False, B_ang[:, 2, :, :]))
            turns(B_ang[:, 0, :, :], B_ang[:, 1, :, :], True, B_ang[:, 3, :, :]).then_inc(sem("b_args"), 1)
            feed(U_B + 7)
            evac(6, B_q[:, 1, 0:512], n=2)
            dve.wait_ge(sem("b_sines"), 2)
            hr = BROT // 2
            for kind, name in enumerate(("gq", "gk")):
                def g(lo, hi):
                    return R(name)[:, lo:hi].unsqueeze(1).to_broadcast([P, NT, hi - lo])
                cs, sn = B_ang[:, 5, :, :], B_ang[:, 4, :, :]
                v_.tensor_tensor(B_T1[:, kind, :, 0:hr], cs, g(0, hr), ALU.mult).then_inc(sem("b_tables"), 1)
                v_.tensor_tensor(B_T1[:, kind, :, hr:BROT], cs, g(hr, BROT), ALU.mult).then_inc(sem("b_tables"), 1)
                v_.tensor_copy(B_T1[:, kind, :, BROT:], g(BROT, BD)).then_inc(sem("b_tables"), 1)
                v_.scalar_tensor_tensor(B_T2[:, kind, :, 0:hr], sn, -1.0, g(hr, BROT), ALU.mult, ALU.mult)\
                    .then_inc(sem("b_tables"), 1)
                v_.tensor_tensor(B_T2[:, kind, :, hr:BROT], sn, g(0, hr), ALU.mult).then_inc(sem("b_tables"), 1)
            dve.wait_ge(sem("b_tables"), 10)

            def b_rotate(b):
                dst, half = (B_q, b) if b < 2 else (B_k, b - 2)
                kind = b // 2
                dve.wait_ge(evac_act, ACT_EVACS[6 + b])
                dve.wait_ge(evac_dve, DVE_EVACS[6 + b])
                for t in range(NT):
                    y = dst[:, t, half * 512:(half + 1) * 512].rearrange("p (h d) -> p h d", h=4)
                    for lo in (0, hr):
                        v_.tensor_tensor(B_z[:, t, :, lo:lo + hr], y[:, :, hr - lo:BROT - lo],
                                         B_T2[:, kind, t, lo:lo + hr].unsqueeze(1).to_broadcast([P, 4, hr]), ALU.mult)\
                            .then_inc(sem("b_swapped") if lo else sem("b_swap0"), 1)
                for t in range(NT):
                    dve.wait_ge(sem("b_sq"), 2 * b + t + 1)
                    o = 384 + 16 * kind + 8 * t + 4 * half
                    v_.tensor_reduce(sm[:, o:o + 4], B_sq[:, t, :].rearrange("p (h d) -> p h d", h=4), AXX, ALU.add)\
                        .then_inc(sem("b_ssq"), 1)
                dve.wait_ge(sem("b_ssq"), 2 * b + 2)
                if half == 1:
                    link(v_.tensor_scalar(rq_a[:, 0:16], sm[:, 384 + 16 * kind:400 + 16 * kind], 1.0 / BD, EPS,
                                          ALU.mult, ALU.add))
                    rsqrt(sm[:, 416 + 16 * kind:432 + 16 * kind], 16)
                for t in range(NT):
                    y = dst[:, t, half * 512:(half + 1) * 512].rearrange("p (h d) -> p h d", h=4)
                    dve.wait_ge(sem("b_scaled"), 2 * b + t + 1)
                    v_.tensor_tensor(y[:, :, 0:BROT], y[:, :, 0:BROT], B_z[:, t, :, :], ALU.add)\
                        .then_inc(sem("b_rotated"), 1)

            def b_knorm(half):
                dve.wait_ge(sem("b_rotated"), 8 if half else 6)
                for t in range(NT):
                    y = B_k[:, t, half * 512:(half + 1) * 512].rearrange("p (h d) -> p h d", h=4)
                    o = 432 + 8 * t + 4 * half
                    v_.tensor_tensor(y, y, sm[:, o:o + 4].unsqueeze(2).to_broadcast([P, 4, BD]), ALU.mult)\
                        .then_inc(sem("b_knormed"), 1)

            def b_copy(b):
                dst, half = (B_qT, b) if b < 2 else (B_kT, b - 2)
                dve.wait_ge(sem("b_turned"), b + 1)
                v_.tensor_copy(dst[:, 4 * half + 2:4 * half + 4, :],
                               ps[5 + 2 * (b % 2)][:, :].rearrange("p (h t) -> p h t", h=2))\
                    .then_inc(sem("b_copied_dve"), 1)

            b_rotate(0)
            for b in range(1, 4):
                dst, half = (B_q, b) if b < 2 else (B_k, b - 2)
                feed(U_B + 4 * b + 7)
                evac(6 + b, dst[:, 1, half * 512:(half + 1) * 512], n=2)
                if b < 3:
                    b_copy(b - 1)
                b_rotate(b)
                if b == 1:
                    link(v_.tensor_scalar(sm[:, 416:432], sm[:, 416:432], float(BD) ** -0.5, None, ALU.mult))
            b_knorm(0)
            b_knorm(1)
            feed(U_B + 23)
            evac(10, B_v[:, 1, 0:512], n=2)
            b_copy(2)
            b_copy(3)
            feed(U_BO + 3)
            evac(11, B_v[:, 1, 512:1024], n=2)
            maskB = C("maskB")

            def b_logits(h):
                dve.wait_ge(sem("b_scores"), h + 1)
                if h >= 3:
                    dve.wait_ge(sem("b_p_turned"), h - 2)
                c = sm[:, 64 + 8 * (h % 3):]
                for t, (lo, hi) in enumerate(((0, P), (P, 3 * P))):
                    q = sm[:, 416 + 8 * t + h:417 + 8 * t + h]
                    v_.scalar_tensor_tensor(B_L[:, h % 3, lo:hi], ps[4 + h % 2][:, lo:hi], q, maskB[:, lo:hi],
                                            ALU.mult, ALU.add).then_inc(sem("b_l"), 1)
                dve.wait_ge(sem("b_l"), 2 * h + 2)
                for t, (lo, hi) in enumerate(((0, P), (P, 3 * P))):
                    ins = v_.tensor_reduce(c[:, 4 + t:5 + t], B_L[:, h % 3, lo:hi], AXX, ALU.max)
                link(ins)
                v_.tensor_scalar(c[:, 0:2], c[:, 4:6], -1.0, None, ALU.mult).then_inc(sem("b_max"), 1)

            def b_prob(h):
                dve.wait_ge(sem("b_exp"), 2 * h + 2)
                c = sm[:, 64 + 8 * (h % 3):]
                link(v_.reciprocal(c[:, 6:8], c[:, 2:4]))
                for t, (lo, hi) in enumerate(((0, P), (P, 3 * P))):
                    v_.tensor_scalar(B_L[:, h % 3, lo:hi], B_L[:, h % 3, lo:hi], c[:, 6 + t:7 + t], None, ALU.mult)\
                        .then_inc(sem("b_p"), 1)

            def b_out(h):
                dve.wait_ge(sem("b_out_hi"), h + 1)
                v_.tensor_tensor(atl[:, h, :], ps[h % 2][:, 0:S], ath[:, h, :], ALU.subtract).then_inc(sem("b_out_lo"), 1)

            for i in range(BH + 2):
                if i < BH:
                    b_logits(i)
                if 0 <= i - 1 < BH:
                    b_prob(i - 1)
                if 0 <= i - 2 < BH:
                    b_out(i - 2)
            feed(U_F1 + 3)
            residual(2, U_F1)
            turn_lo(4, lambda f: gcol[:, GROWS["ffn"] + 8 + f:GROWS["ffn"] + 9 + f])
            row_scale(3)
            ffn(1, U_F1, 3)

            residual(3, U_C)
            turn_lo(5, lambda f: gcol[:, GROWS["n1"] + f:GROWS["n1"] + f + 1])
            row_scale(4)
            hh = HD // 2
            for kind, name in enumerate(("qa", "ka", "qc", "kc")):
                def g(lo, hi):
                    return R(name)[:, lo:hi].unsqueeze(1).to_broadcast([P, NT, hi - lo])
                v_.tensor_tensor(C_T1[:, kind, :, 0:hh], cosC, g(0, hh), ALU.mult)
                v_.tensor_tensor(C_T1[:, kind, :, hh:HD], cosC, g(hh, HD), ALU.mult)
                v_.scalar_tensor_tensor(C_T2[:, kind, :, 0:hh], sinC, -1.0, g(hh, HD), ALU.mult, ALU.mult)
                ins = v_.tensor_tensor(C_T2[:, kind, :, hh:HD], sinC, g(0, hh), ALU.mult)
            ins.then_inc(sem("c_tables"), 1)
            dve.wait_ge(sem("c_tables"), 1)

            def c_evac(i):
                evac(12 + i, C_p[:, 1, 512 * i:512 * i + IN_BLOCKS[12 + i][1]], n=4)

            def c_norms(g, c0, c1, o):
                nh = (c1 - c0) // HD
                for t in range(NT):
                    dve.wait_ge(sem("c_sq"), 2 * g + t + 1)
                    v_.tensor_reduce(sm[:, o + nh * t:o + nh * t + nh],
                                     C_z[:, 0:c1 - c0].rearrange("p (h d) -> p h d", h=nh), AXX, ALU.add)\
                        .then_inc(sem("c_ssq"), 1)
                dve.wait_ge(sem("c_ssq"), 2 * g + 2)
                link(v_.tensor_scalar(rq_a[:, 0:2 * nh], sm[:, o:o + 2 * nh], 1.0 / HD, EPS, ALU.mult, ALU.add))
                rsqrt(sm[:, o:o + 2 * nh], 2 * nh)

            def c_rotate(t, c0, nh, kind, after):
                y = C_p[:, t, c0:c0 + nh * HD].rearrange("p (h d) -> p h d", h=nh)
                z = C_z[:, 0:nh * HD].rearrange("p (h d) -> p h d", h=nh)
                for lo in (0, hh):
                    ins = v_.tensor_tensor(z[:, :, lo:lo + hh], y[:, :, hh - lo:HD - lo],
                                           C_T2[:, kind, t, lo:lo + hh].unsqueeze(1).to_broadcast([P, nh, hh]), ALU.mult)
                link(ins)
                link(v_.tensor_tensor(y, y, C_T1[:, kind, t, :].unsqueeze(1).to_broadcast([P, nh, HD]), ALU.mult))
                return v_.tensor_tensor(y, y, z, ALU.add)

            def c_scale(t, c0, nh, o, dst=None):
                y = C_p[:, t, c0:c0 + nh * HD].rearrange("p (h d) -> p h d", h=nh)
                return v_.tensor_tensor(y if dst is None else dst, y, sm[:, o:o + nh].unsqueeze(2).to_broadcast([P, nh, HD]), ALU.mult)

            feed(U_C + 7)
            c_evac(0)
            feed(U_C + 11)
            c_evac(1)
            dve.wait_ge(evac_act, ACT_EVACS[13])
            dve.wait_ge(evac_dve, DVE_EVACS[13])
            c_norms(0, 0, 640, 300)
            feed(U_C + 13)
            for t in range(NT):
                link(c_rotate(t, 0, 8, 0, None))
                link(c_rotate(t, 512, 2, 1, None))
                for twin in range(2):
                    kd = C_kd[:, t, :].rearrange("p (h w d) -> p h w d", h=2, w=2)[:, :, twin, :]
                    link(c_scale(t, 512, 2, 308 + 10 * t, kd))
            v_.tensor_scalar(sm[:, 300:320], sm[:, 300:320], float(HD) ** -0.5, None, ALU.mult)\
                .then_inc(sem("c_w_ready"), 1)
            dve.wait_ge(sem("c_w_ready"), 1)
            feed(U_C + 15)
            c_evac(2)
            feed(U_C + 19)
            c_evac(3)

            def conv(c):
                part = C_p[:, :, 768 + c * HW:768 + (c + 1) * HW]

                def tap(j):
                    return C_cw[:, j:j + 1, :].to_broadcast([P, NT, HW])

                dve.wait_ge(sem("taps_loaded"), 64 * (c + 1))
                dve.wait_ge(sem("shifted"), 64 * (c + 1))
                link(v_.tensor_tensor(part, part, tap(1), ALU.mult))
                link(v_.tensor_tensor(C_sn, C_sn, tap(2), ALU.mult))
                link(v_.tensor_tensor(part, part, C_sn, ALU.add))
                dve.wait_ge(sem("tap0_done"), c + 1)
                v_.tensor_tensor(part, part, C_sp, ALU.add).then_inc(sem("conv_sum"), 1)

            feed(U_C + 21)
            conv(0)
            feed(U_C + 23)
            c_evac(4)
            feed(U_C + 25)
            conv(1)
            feed(U_C + 27)
            c_evac(5)
            conv(2)
            feed(U_C + 31)
            c_evac(6)
            dve.wait_ge(evac_act, ACT_EVACS[18])
            dve.wait_ge(evac_dve, DVE_EVACS[18])
            c_norms(1, 2304, 3328, 320)
            feed(U_C + 33)
            for t in range(NT):
                link(c_rotate(t, 2304, 8, 2, None))
                if t == 0:
                    feed(U_C + 34)
                link(c_rotate(t, 2816, 8, 3, None))
                link(c_scale(t, 2816, 8, 328 + 16 * t))
            v_.tensor_scalar(sm[:, 320:352], sm[:, 320:352], float(HD) ** -0.5, None, ALU.mult)\
                .then_inc(sem("c_d_ready"), 1)
            dve.wait_ge(sem("c_d_ready"), 1)
            feed(U_C + 35)
            c_evac(7)

            def w_logits(h):
                dve.wait_ge(sem("w_scores"), h + 1)
                if h >= 2:
                    dve.wait_ge(sem("w_p_turned"), h - 1)
                elif h == 0:
                    dve.wait_ge(sem("conv_done"), 6)
                c = sm[:, 128 + 16 * (h % 2):]
                for t in range(NT):
                    v_.scalar_tensor_tensor(C_L[:, h % 2, t * S:(t + 1) * S], ps[4 + h % 2][:, t * S:(t + 1) * S],
                                            sm[:, 300 + 10 * t + h:301 + 10 * t + h], maskW[:, t, :],
                                            ALU.mult, ALU.add).then_inc(sem("w_l"), 1)
                dve.wait_ge(sem("w_l"), 2 * h + 2)
                link(v_.tensor_reduce(c[:, 0:2], C_L[:, h % 2, :].rearrange("p (t s) -> p t s", t=NT), AXX, ALU.max))
                v_.tensor_scalar(c[:, 2:4], c[:, 0:2], R("sink")[:, h:h + 1], -1.0, ALU.max, ALU.mult)\
                    .then_inc(sem("w_max"), 1)

            def w_prob(h):
                dve.wait_ge(sem("w_exp"), 3 * h + 3)
                c = sm[:, 128 + 16 * (h % 2):]
                link(v_.tensor_tensor(c[:, 8:10], c[:, 4:6], c[:, 6:8], ALU.add))
                link(v_.reciprocal(c[:, 10:12], c[:, 8:10]))
                for t in range(NT):
                    v_.tensor_scalar(C_L[:, h % 2, t * S:(t + 1) * S], C_L[:, h % 2, t * S:(t + 1) * S],
                                     c[:, 10 + t:11 + t], None, ALU.mult).then_inc(sem("w_p"), 1)

            def w_out(i):
                dve.wait_ge(sem("w_out_hi"), i + 1)
                v_.tensor_tensor(brl[:, i, :], ps[2 + i % 2][:, 0:S], brh[:, i, :], ALU.subtract)\
                    .then_inc(sem("w_out_lo"), 1)

            for i in range(WQ + 2):
                feed(U_GA + min(i + 3, 11))
                if i < WQ:
                    w_logits(i)
                if 0 <= i - 1 < WQ:
                    w_prob(i - 1)
                if i >= 3 and i % 2 == 1:
                    w_out((i - 3) // 2)
            feed(U_OA + 3)

            def merge(b, bank0, u_last):
                dve.wait_ge(unit_used, u_last)
                dve.wait_ge(evac_act, ACT_EVACS[21 + 2 * b])
                for nb in range(2):
                    for t in range(NT):
                        th = C_th[:, t, nb * 512:(nb + 1) * 512]
                        m = C_mg[:, t, nb * 512:(nb + 1) * 512]
                        bk = ps[bank0 + 2 * nb + t][:, :]
                        if b == 0:
                            v_.scalar_tensor_tensor(m, th, 1.0, bk, ALU.add, ALU.mult).then_inc(sem("merged"), 1)
                        else:
                            link(v_.scalar_tensor_tensor(th, th, 1.0, bk, ALU.add, ALU.mult))
                            v_.tensor_tensor(m, m, th, ALU.add).then_inc(sem("merged"), 1)

            feed(U_GB + 3)
            merge(0, 4, U_GB)
            feed(U_GB + 5)

            def spectral(o):
                dve.wait_ge(sem("h_fwd"), o + 1)
                ur0, ur1, ui0, ui1 = (ps[4 + i][:, :] for i in range(4))
                hc0, hc1, hn0, hs0, hs1 = (H[:, o, i, :] for i in range(NFT))
                for y, a, ha, b, hb, op in ((0, ur0, hc0, ui0, hs0, ALU.subtract), (1, ur1, hc1, ui1, hs1, ALU.subtract),
                                            (2, ur0, hs0, ui0, hn0, ALU.add), (3, ur1, hs1, ui1, hc1, ALU.add)):
                    v_.tensor_tensor(C_tm[:, 0, :], a, ha, ALU.mult)
                    link(v_.tensor_tensor(C_tm[:, 1, :], b, hb, ALU.mult))
                    v_.tensor_tensor(C_Y[:, y, :], C_tm[:, 0, :], C_tm[:, 1, :], op).then_inc(sem("h_y"), 1)
                    dve.wait_ge(sem("h_y"), 4 * o + y + 1)

            def hyena_gate(o):
                dve.wait_ge(sem("hyd_loaded"), 32)
                for t in range(NT):
                    vv = C_p[:, t, 768:768 + HW]
                    xx = C_p[:, t, 768 + (o + 1) * HW:768 + (o + 2) * HW]
                    link(v_.tensor_tensor(vv, vv, C_hd[:, o, :], ALU.mult))
                    if t == 0:
                        dve.wait_ge(sem("h_bwd"), o + 1)
                    link(v_.tensor_tensor(vv, vv, ps[2 + t][:, :], ALU.add))
                    v_.tensor_tensor(vv, vv, xx, ALU.mult).then_inc(sem("h_z"), 1)

            spectral(0)
            feed(U_GB + 7)
            hyena_gate(0)
            spectral(1)
            feed(U_GB + 11)
            hyena_gate(1)
            for p in range(2):
                dve.wait_ge(sem("h_hi"), p + 1)
                v_.tensor_tensor(brl[:, 2 * p:2 * p + 2, :], ps[6 + p][:, :].rearrange("p (f t) -> p f t", f=2),
                                 brh[:, 2 * p:2 * p + 2, :], ALU.subtract).then_inc(sem("h_lo"), 1)
            for i, (a, b) in enumerate((("lq1", "lk1"), ("lq2", "lk2"))):
                link(v_.tensor_tensor(rq_a[:, 0:64], R(a), R(b), ALU.mult))
                v_.tensor_reduce(sm[:, 200 + i:201 + i], rq_a[:, 0:64], AXX, ALU.add).then_inc(sem("lam_dots"), 1)
                dve.wait_ge(sem("lam_dots"), i + 1)
            feed(U_GC + 1)
            merge(1, 4, U_GC)
            dve.wait_ge(sem("lam_exps"), 1)
            link(v_.tensor_tensor(sm[:, 204:205], sm[:, 203:204], sm[:, 202:203], ALU.subtract))
            link(v_.tensor_scalar(sm[:, 205:206], sm[:, 204:205], LAM0, None, ALU.subtract))
            v_.tensor_scalar(sm[:, 280:281], gcol[:, GROWS["subln"]:GROWS["subln"] + 1], 1.0 - LAM0, None, ALU.mult)\
                .then_inc(sem("sub_ready"), 1)
            dve.wait_ge(sem("sub_ready"), 1)

            def d_max(h):
                dve.wait_ge(sem("d_scores"), 2 * h + 2)
                c = sm[:, 208 + 32 * (h % 2):]
                if h >= 2:
                    dve.wait_ge(sem("d_p"), 2 * (h - 1))
                for comp in range(2):
                    link(v_.tensor_reduce(c[:, 2 * comp:2 * comp + 2],
                                          ps[4 + comp][:, :].rearrange("p (t s) -> p t s", t=NT), AXX, ALU.max))
                src = sm[:, 320:352].rearrange("p (t h) -> p h t", t=NT)[:, 2 * h:2 * h + 2, :]
                link(v_.tensor_copy(c[:, 4:8].rearrange("p (h t) -> p h t", h=2), src))
                v_.scalar_tensor_tensor(c[:, 8:12], c[:, 0:4], -1.0, c[:, 4:8], ALU.mult, ALU.mult)\
                    .then_inc(sem("d_max"), 1)

            def d_prob(h):
                dve.wait_ge(sem("d_exp"), 4 * h + 4)
                c = sm[:, 208 + 32 * (h % 2):]
                link(v_.reciprocal(c[:, 16:20], c[:, 12:16]))
                link(v_.tensor_scalar(c[:, 18:20], c[:, 18:20], sm[:, 205:206], None, ALU.mult))
                for t in range(NT):
                    e0 = C_L[:, 2 * (h % 2), t * S:(t + 1) * S]
                    e1 = C_L[:, 2 * (h % 2) + 1, t * S:(t + 1) * S]
                    link(v_.tensor_scalar(e0, e0, c[:, 16 + t:17 + t], None, ALU.mult))
                    v_.scalar_tensor_tensor(e0, e1, c[:, 18 + t:19 + t], e0, ALU.mult, ALU.add).then_inc(sem("d_p"), 1)

            for i in range(CH + 1):
                feed(U_GC + min(2 * i + 3, 11))
                if i < CH:
                    d_max(i)
                if 0 <= i - 1 < CH:
                    d_prob(i - 1)
            dve.wait_ge(sem("d_ssq"), 8)
            dve.wait_ge(sem("d_oc"), 4)
            link(v_.tensor_scalar(rq_a[:, 0:8], sm[:, 272:280], 1.0 / (2 * HD), EPS, ALU.mult, ALU.add))
            rsqrt(sm[:, 284:292], 8)
            for t in range(NT):
                y = C_oc[:, t, :].rearrange("p (h d) -> p h d", h=CH)
                v_.tensor_tensor(y, y, sm[:, 284 + 4 * t:288 + 4 * t].unsqueeze(2).to_broadcast([P, CH, P]), ALU.mult)\
                    .then_inc(sem("d_y"), 1)
            for p in range(2):
                dve.wait_ge(sem("c_hi"), p + 1)
                v_.scalar_tensor_tensor(brl[:, 2 * p:2 * p + 2, :], ps[6 + p][:, :].rearrange("p (f t) -> p f t", f=2),
                                        sm[:, 280:281], brh[:, 2 * p:2 * p + 2, :], ALU.mult, ALU.subtract)\
                    .then_inc(sem("c_lo"), 1)
            feed(U_W + 3)
            merge(2, 0, U_W)
            turn_lo(6, lambda f: 0.5)
            feed(U_F2 + 3)
            residual(4, U_F2)
            turn_lo(7, lambda f: gcol[:, GROWS["n2"] + f:GROWS["n2"] + f + 1])
            row_scale(5)
            ffn(2, U_F2, 5)
            residual(5, U_END)

        @block.tensor
        def _(pe):
            mm = nc.tensor.matmul

            def split_mm(dst, h, lo, rh, rl, start, stop):
                mm(dst, h, rh, start=start, stop=False)
                mm(dst, h, rl, start=False, stop=False)
                return mm(dst, lo, rh, start=False, stop=stop)

            def up_unit(slot, i, bk, w, ready, turned_need=None):
                if turned_need is not None:
                    pe.wait_ge(turned_lo, turned_need)
                pe.wait_ge(lo_ready, ready)
                rh, rl = unit_view(whi, slot, w), unit_view(wlo, slot, w)
                for kk in range(2):
                    k = 2 * i + kk
                    for t in range(NT):
                        ins = split_mm(ps[bk + t][:, 0:w], ath[:, k, t * P:(t + 1) * P], atl[:, k, t * P:(t + 1) * P],
                                       rh[:, kk, :], rl[:, kk, :], k == 0, k == KT - 1)
                ins.then_inc(unit_used, 1)

            def down_unit(slot, k, first, last, ready, act_h, act_l, bk=4):
                pe.wait_ge(lo_ready, ready)
                rh, rl = unit_view(whi, slot, 512), unit_view(wlo, slot, 512)
                for nb in range(2):
                    for t in range(NT):
                        ins = split_mm(ps[bk + 2 * nb + t][:, :], act_h[:, k, t * P:(t + 1) * P],
                                       act_l[:, k, t * P:(t + 1) * P], rh[:, nb, :], rl[:, nb, :], first, last)
                ins.then_inc(unit_used, 1)

            def units(i, lo=0, hi=4, use=None):
                u0, w, bk = IN_BLOCKS[i]
                if lo == 0:
                    back = i - 1 if i >= 20 else i - 2
                    if back >= 0:
                        pe.wait_ge(evac_act, ACT_EVACS[back])
                        pe.wait_ge(evac_dve, DVE_EVACS[back])
                for c in range(lo, hi):
                    up_unit((u0 + c) % SPL, c, bk, w, u0 + c + 1, None if use is None else 8 * use + 2 * (c + 1))

            def down(u0, n, act_h, act_l, bk=4):
                for k in range(n):
                    down_unit((u0 + k) % SPL, k, k == 0, k == n - 1, u0 + k + 1, act_h, act_l, bk)

            def turn(src, ready):
                for p in range(4):
                    ready(p)
                    for f in range(2):
                        for t in range(NT):
                            c = (2 * p + f) * P
                            ins = nc.tensor.transpose(ps[TBANKS[p]][:, f * S + t * P:f * S + (t + 1) * P],
                                                      src(t)[:, c:c + P], ident)
                    ins.then_inc(turned, 1)

            def ffn(n, u0, use):
                def hid_turn(count):
                    pe.wait_ge(hid_ready, count)
                    for f in range(2):
                        for t in range(NT):
                            ins = nc.tensor.transpose(ps[2][:, f * S + t * P:f * S + (t + 1) * P],
                                                      hid[:, t, f * P:(f + 1) * P], ident)
                    ins.then_inc(hid_T, 1)

                def ffn_down(j, k2, wait, slot, ready, first, last):
                    if k2 == 0:
                        pe.wait_ge(hid_lo, wait)
                    down_unit(slot, k2, first, last, ready, brh, brl)

                for c in range(4):
                    up_unit((u0 + c) % SPL, c, 0, 512, u0 + c + 1, 8 * use + 2 * (c + 1))

                def body(j, first):
                    for c in range(6):
                        slot = (u0 + 4 + c) % SPL
                        ready = 6 * j + (u0 - 2 + c + 1)
                        if c == 0:
                            pe.wait_ge(hid_ready, 2 * j + 2 * FB * n)
                        if c == 2:
                            hid_turn(2 * j + 2 * FB * n)
                        if c < 4:
                            up_unit(slot, c, 0, 512, ready)
                        else:
                            ffn_down(j, c - 4, j + FB * n, slot, ready, first and c == 4, False)

                body(1, True)
                with pe.Fori(2, FB) as j:
                    body(j, False)
                last = u0 + 4 + 6 * (FB - 1)
                hid_turn(2 * FB * (n + 1))
                for k2 in range(2):
                    ffn_down(FB, k2, FB * (n + 1), (last + k2) % SPL, last + k2 + 1, False, k2 == 1)

            pe.wait_ge(sem("ident_loaded"), 16)
            pe.wait_ge(sem("grow_loaded"), 16 * len(GROWS))
            nc.tensor.transpose(ps[6][:, 0:64], grow[:, :], con[0:64, 0:64]).then_inc(sem("cols_turned"), 1)

            def x_first(p):
                if p == 0:
                    for t in range(NT):
                        pe.wait_ge(sem(f"x_loaded{t}"), 16)

            turn(lambda t: x[:, t, :], x_first)
            units(0, use=0)
            pe.wait_ge(sem("wg_split"), 2)
            for t in range(NT):
                for k in range(KT):
                    ins = split_mm(ps[6][:, 8 * t:8 * t + 8], ath[:, k, t * P:(t + 1) * P], atl[:, k, t * P:(t + 1) * P],
                                   wgh[:, k, :], wgl[:, k, :], k == 0, k == KT - 1)
            ins.then_inc(sem("gl_ready"), 1)
            pe.wait_ge(sem("con1_loaded"), 16)
            pe.wait_ge(sem("filt_loaded"), 48)
            mm(ps[7][0:64, 0:S], fw12[0:33, 0, :], con[0:33, CONSTS["zT"][0]:CONSTS["zT"][0] + S],
               start=True, stop=True).then_inc(sem("f_mm"), 1)
            units(1)

            def turn_qk(c0, n):
                for h in range(AH):
                    for t in range(NT):
                        ins = nc.tensor.transpose(ps[4 + h // 2][:, (h % 2) * S + t * P:(h % 2) * S + (t + 1) * P],
                                                  A_qk[:, t, c0 + h * ADK:c0 + (h + 1) * ADK], ident)
                ins.then_inc(sem("a_qk_turned"), 1)

            pe.wait_ge(evac_act, ACT_EVACS[0])
            pe.wait_ge(evac_dve, DVE_EVACS[0])
            turn_qk(0, 0)
            pe.wait_ge(sem("glog"), 2)
            pe.wait_ge(sem("f_arg"), 1)
            for g in range(2):
                for t in range(NT):
                    ins = nc.tensor.transpose(ps[7][0:4, g * S + t * P:g * S + (t + 1) * P],
                                              glog[:, t, 4 * g:4 * g + 4], ident)
            ins.then_inc(sem("gl_turned"), 1)
            pe.wait_ge(sem("f_hidden"), 1)
            mm(ps[6][0:64, 0:S], fw12[:, 1, :], fil[:, 2, :], start=True, stop=True).then_inc(sem("f_mm"), 1)
            units(2, 0, 2)
            pe.wait_ge(evac_act, ACT_EVACS[1])
            pe.wait_ge(evac_dve, DVE_EVACS[1])
            pe.wait_ge(sem("a_qk_copied"), 2)
            turn_qk(512, 1)
            units(2, 2, 4)

            def filter3(i):
                o, t = divmod(i, 2)
                pe.wait_ge(sem("f_hidden"), 2)
                if i >= 2:
                    pe.wait_ge(sem("fb_ready"), 2 * (i - 1))
                for d in range(2):
                    ins = mm(ps[(4, 6)[i % 2] + d][:, :], fil[:, 3, t * P:(t + 1) * P],
                             A_w3[:, (2 * o + d) * HW:(2 * o + d + 1) * HW], start=True, stop=True)
                ins.then_inc(sem("f3"), 1)

            def filter_norm(o):
                pe.wait_ge(sem("f_sq"), 4 * o + 4)
                w0 = CONSTS["nrmw"][0]
                for c in range(4):
                    for i in range(4):
                        d, t = divmod(i, 2)
                        ins = mm(ps[4][:, 4 * o + c:4 * o + c + 1], A_sq[:, t, d, c * P:(c + 1) * P],
                                 con[:, w0 + i:w0 + i + 1], start=(i == 0), stop=(i == 3))
                ins.then_inc(sem("f_norm"), 1)

            pe.wait_ge(sem("a_qk_copied"), 4)
            filter3(0)
            units(3, 0, 2)
            pe.wait_ge(sem("g_rows"), 2)
            pe.wait_ge(sem("f_arg"), 2)
            filter3(1)
            units(3, 2, 4)
            filter3(2)
            units(4, 0, 2)
            filter3(3)
            pe.wait_ge(sem("fb_ready"), 6)
            pe.wait_ge(sem("g_em"), 1)
            for t in range(NT):
                for j, row in enumerate((5, 7)):
                    ins = nc.tensor.transpose(ps[5][:, 8 * t + 4 * j:8 * t + 4 * j + 4],
                                              gate[:, row, t * P:(t + 1) * P], con[0:4, 0:4])
            ins.then_inc(sem("am_turned"), 1)
            filter_norm(0)
            units(4, 2, 4)
            units(5, 0, 2)
            filter_norm(1)

            def a_scores(h):
                if h >= 2:
                    pe.wait_ge(sem("a_num"), 2 * (h - 1))
                    pe.wait_ge(sem("a_ssq"), 2 * (h - 1))
                mm(ps[6 + h % 2][:, 0:S], A_kT[:, h, 0:P], A_qT[:, h, :], start=True, stop=True)
                mm(ps[6 + h % 2][:, S:384], A_kT[:, h, P:S], A_qT[:, h, P:S], start=True, stop=True)
                mm(ps[4 + h % 2][:, 0:S], sel[0:4, h, :], gate[:, 6, :], start=True, stop=True)\
                    .then_inc(sem("a_scores"), 1)

            pe.wait_ge(sem("fb_ready"), 8)
            pe.wait_ge(sem("am_ready"), 1)
            pe.wait_ge(sem("dg_ready"), 8)
            a_scores(0)
            a_scores(1)
            units(5, 2, 4)
            for o in range(2):
                for c in range(4):
                    ins = mm(ps[o][:, c * P:(c + 1) * P], C("ones"), A_dg[:, 4 * o + c, :], start=True, stop=True)
            ins.then_inc(sem("rn_spread"), 1)

            def spectrum(i):
                o, f = divmod(i, NFT)
                if i == 0:
                    pe.wait_ge(sem("con2_loaded"), 16)
                    pe.wait_ge(evac_act, ACT_EVACS[5])
                    pe.wait_ge(sem("ed_ready"), 8)
                if i >= 2:
                    pe.wait_ge(sem("spec_ready"), i - 1)
                d = 0 if f < 3 else 1
                for t in range(NT):
                    ins = mm(ps[2 + i % 2][:, :], fwd[:, t, f, :], A_ed[:, o, t, d, :], start=(t == 0), stop=(t == 1))
                ins.then_inc(sem("spec"), 1)

            def a_pv(h):
                pe.wait_ge(sem("a_p_masked"), 2 * h + 2)
                pe.wait_ge(sem("a_d_ready"), h + 1)
                pe.wait_ge(evac_act, ACT_EVACS[3])
                pe.wait_ge(evac_dve, DVE_EVACS[3])
                pe.wait_ge(sem("a_ones"), 1)
                pt = A_P[:, h % 2, :]
                mm(ps[6 + h % 2][:, 0:ADV + 1], pt[:, 0:P], A_v[:, 0, h, :], start=True, stop=True)\
                    .then_inc(sem("a_pv"), 1)
                mm(ps[4 + h % 2][:, 0:ADV + 1], pt[:, P:S], A_v[:, 0, h, :], start=True, stop=False)
                mm(ps[4 + h % 2][:, 0:ADV + 1], pt[:, S:384], A_v[:, 1, h, :], start=False, stop=True)\
                    .then_inc(sem("a_pv"), 1)

            spectrum(0)
            spectrum(1)
            a_pv(0)
            a_pv(1)
            spectrum(2)
            a_scores(2)
            a_scores(3)
            for i in range(3, 6):
                spectrum(i)
            a_pv(2)
            a_pv(3)

            def y_first(p):
                pe.wait_ge(sem("a_y"), 2 * (p + 1))
                if p == 0:
                    pe.wait_ge(sem("spec_ready"), 6)

            turn(lambda t: A_o[:, t, :], y_first)
            pe.wait_ge(turned_lo, 8 + 4)
            for i in range(6, 10):
                spectrum(i)
            pe.wait_ge(turned_lo, 16)
            down(U_AO, KT, ath, atl)

            def x_sum(r):
                def ready(p):
                    pe.wait_ge(x_ready, 4 * r + 2 * (p // 2 + 1))
                return ready

            def x_sum0(p):
                if p == 0:
                    pe.wait_ge(sem("spec_ready"), 10)
                x_sum(0)(p)

            turn(lambda t: x[:, t, :], x_sum0)
            ffn(0, U_F0, 2)

            turn(lambda t: x[:, t, :], x_sum(1))

            def b_turn(b):
                dst, half = (B_q, b) if b < 2 else (B_k, b - 2)
                if b < 2:
                    pe.wait_ge(sem("b_rotated"), 2 * b + 2)
                else:
                    pe.wait_ge(sem("b_knormed"), 2 * (b - 2) + 2)
                if b >= 2:
                    pe.wait_ge(sem("b_copied_act"), b - 1)
                    pe.wait_ge(sem("b_copied_dve"), b - 1)
                for h in range(4):
                    for t in range(NT):
                        ins = nc.tensor.transpose(
                            ps[4 + 2 * (b % 2) + h // 2][:, (h % 2) * S + t * P:(h % 2) * S + (t + 1) * P],
                            dst[:, t, (4 * half + h) * BD:(4 * half + h + 1) * BD], ident)
                ins.then_inc(sem("b_turned"), 1)

            units(6, use=3)
            units(7)
            b_turn(0)
            units(8)
            b_turn(1)
            units(9)
            units(10)
            b_turn(2)
            b_turn(3)
            units(11)

            def b_scores(h):
                if h == 0:
                    pe.wait_ge(sem("b_copied_act"), 4)
                    pe.wait_ge(sem("b_copied_dve"), 4)
                if h >= 2:
                    pe.wait_ge(sem("b_l"), 2 * (h - 1))
                mm(ps[4 + h % 2][:, 0:P], B_qT[:, h, 0:P], B_kT[:, h, 0:P], start=True, stop=True)
                mm(ps[4 + h % 2][:, P:384], B_qT[:, h, P:S], B_kT[:, h, :], start=True, stop=True)\
                    .then_inc(sem("b_scores"), 1)

            def b_p_turn(h):
                pe.wait_ge(sem("b_p"), 2 * h + 2)
                if h >= 2:
                    pe.wait_ge(sem("b_pt"), h - 1)
                for i in range(3):
                    ins = nc.tensor.transpose(ps[6 + h % 2][:, i * P:(i + 1) * P], B_L[:, h % 3, i * P:(i + 1) * P], ident)
                ins.then_inc(sem("b_p_turned"), 1)

            def b_pv(h):
                pe.wait_ge(sem("b_pt"), h + 1)
                pe.wait_ge(evac_act, ACT_EVACS[11])
                pe.wait_ge(evac_dve, DVE_EVACS[11])
                if h >= 2:
                    pe.wait_ge(sem("b_out_lo"), h - 1)
                o = ps[h % 2]
                mm(o[:, 0:S], B_v[:, 0, h * BD:(h + 1) * BD], B_PT[:, h % 2, 0:S], start=True, stop=False)
                mm(o[:, P:S], B_v[:, 1, h * BD:(h + 1) * BD], B_PT[:, h % 2, S:384], start=False, stop=True)\
                    .then_inc(sem("b_pv"), 1)

            b_scores(0)
            b_scores(1)
            for h in range(BH + 1):
                if h < BH:
                    b_p_turn(h)
                if h + 2 < BH:
                    b_scores(h + 2)
                if h >= 1:
                    b_pv(h - 1)
            pe.wait_ge(sem("b_out_lo"), BH)
            down(U_BO, KT, ath, atl)
            turn(lambda t: x[:, t, :], x_sum(2))
            ffn(1, U_F1, 4)

            turn(lambda t: x[:, t, :], x_sum(3))
            units(12, use=5)
            units(13)
            units(14)
            pe.wait_ge(sem("c_w_ready"), 1)
            for pr in range(4):
                for t in range(NT):
                    nc.tensor.transpose(ps[4 + pr // 2][:, (pr % 2) * S + t * P:(pr % 2) * S + (t + 1) * P],
                                        C_p[:, t, pr * P:(pr + 1) * P], ident)
            for g in range(2):
                for t in range(NT):
                    ins = nc.tensor.transpose(ps[6][:, g * S + t * P:g * S + (t + 1) * P],
                                              C_kd[:, t, g * P:(g + 1) * P], ident)
            ins.then_inc(sem("c_w_turned"), 1)
            for i in range(15, 20):
                units(i)

            def w_scores(h):
                if h == 0:
                    pe.wait_ge(sem("c_w_copied"), 3)
                if h >= 2:
                    pe.wait_ge(sem("w_l"), 2 * (h - 1))
                g, pr = h // 4, h // 2
                rows = slice(64 * (h % 2), 64 * (h % 2) + 64)
                for t in range(NT):
                    ins = mm(ps[4 + h % 2][:, t * S:(t + 1) * S], C_qT[rows, pr, t * P:(t + 1) * P], C_kT[rows, g, :],
                             start=True, stop=True)
                ins.then_inc(sem("w_scores"), 1)

            def p_turn(h, p_sem, pt_sem, out_sem, src):
                pe.wait_ge(sem(p_sem), 2 * h + 2)
                if h >= 2:
                    pe.wait_ge(sem(pt_sem), h - 1)
                for s in range(2):
                    for t in range(NT):
                        ins = nc.tensor.transpose(ps[6 + h % 2][:, s * S + t * P:s * S + (t + 1) * P],
                                                  src[:, t * S + s * P:t * S + (s + 1) * P], ident)
                ins.then_inc(sem(out_sem), 1)

            def w_pv(h):
                pe.wait_ge(sem("w_pt"), h + 1)
                i = h // 2
                if h % 2 == 0 and i >= 2:
                    pe.wait_ge(sem("w_out_lo"), i - 1)
                if h == 0:
                    pe.wait_ge(evac_act, ACT_EVACS[19])
                    pe.wait_ge(evac_dve, DVE_EVACS[19])
                rows = slice(64 * (h % 2), 64 * (h % 2) + 64)
                g = h // 4
                for s in range(2):
                    ins = mm(ps[2 + i % 2][rows, 0:S], C_p[:, s, 640 + g * HD:640 + (g + 1) * HD],
                             C_PT[:, h % 2, s * S:(s + 1) * S], start=(s == 0), stop=(s == 1))
                ins.then_inc(sem("w_pv"), 1)

            w_scores(0)
            w_scores(1)
            for h in range(WQ + 1):
                if h < WQ:
                    units(20 + h // 4, h % 4, h % 4 + 1)
                    p_turn(h, "w_p", "w_pt", "w_p_turned", C_L[:, h % 2, :])
                if h + 2 < WQ:
                    w_scores(h + 2)
                if h >= 1:
                    w_pv(h - 1)
            pe.wait_ge(sem("w_out_lo"), 4)
            down(U_OA, 4, brh, brl, 4)

            def forward(o):
                if o == 0:
                    pe.wait_ge(sem("conv_done"), 6)
                    pe.wait_ge(sem("merged"), 4)
                else:
                    pe.wait_ge(sem("h_z"), 2)
                for i in range(4):
                    for t in range(NT):
                        ins = mm(ps[4 + i][:, :], fwd[:, t, (0, 1, 5, 4)[i], :], C_p[:, t, 768:768 + HW],
                                 start=(t == 0), stop=(t == 1))
                ins.then_inc(sem("h_fwd"), 1)

            def backward(o):
                pe.wait_ge(sem("h_y"), 4 * o + 4)
                for t in range(NT):
                    for i in range(4):
                        ins = mm(ps[2 + t][:, :], bwd[:, i, t * P:(t + 1) * P], C_Y[:, i, :], start=(i == 0), stop=(i == 3))
                ins.then_inc(sem("h_bwd"), 1)

            units(22, 0, 2)
            forward(0)
            units(22, 2, 4)
            backward(0)
            units(23, 0, 2)
            forward(1)
            units(23, 2, 4)
            backward(1)
            for p in range(2):
                if p == 0:
                    pe.wait_ge(sem("h_z"), 4)
                for f in range(2):
                    for t in range(NT):
                        c = 768 + (2 * p + f) * P
                        ins = nc.tensor.transpose(ps[6 + p][:, f * S + t * P:f * S + (t + 1) * P], C_p[:, t, c:c + P], ident)
                ins.then_inc(sem("h_turned"), 1)
            pe.wait_ge(sem("h_lo"), 2)
            down(U_OB, 4, brh, brl, 4)

            pe.wait_ge(sem("c_d_ready"), 1)
            pe.wait_ge(sem("merged"), 8)
            for c in range(2):
                for h in range(CH):
                    for t in range(NT):
                        c0 = (2304, 2816)[c] + h * P
                        ins = nc.tensor.transpose(
                            ps[4 + 2 * c + h // 2][:, (h % 2) * S + t * P:(h % 2) * S + (t + 1) * P],
                            C_p[:, t, c0:c0 + P], ident)
                ins.then_inc(sem("d_turned"), 1)

            def d_scores(h):
                if h == 0:
                    pe.wait_ge(sem("d_copied"), 4)
                for comp in range(2):
                    if h:
                        pe.wait_ge(sem("d_exp"), 4 * (h - 1) + 2 * comp + 2)
                    rows = slice(64 * comp, 64 * comp + 64)
                    for t in range(NT):
                        ins = mm(ps[4 + comp][:, t * S:(t + 1) * S], C_qT[rows, h, t * P:(t + 1) * P], C_kT[rows, h, :],
                                 start=True, stop=True)
                    ins.then_inc(sem("d_scores"), 1)

            def d_pv(h):
                pe.wait_ge(sem("d_pt"), h + 1)
                if h == 0:
                    pe.wait_ge(sem("h_z"), 4)
                if h >= 2:
                    pe.wait_ge(sem("d_oc"), h - 1)
                for t in range(NT):
                    for s in range(2):
                        ins = mm(ps[2 + h % 2][:, t * P:(t + 1) * P], C_PT[:, h % 2, s * S + t * P:s * S + (t + 1) * P],
                                 C_p[:, s, 3328 + h * P:3328 + (h + 1) * P], start=(s == 0), stop=(s == 1))
                ins.then_inc(sem("d_pv"), 1)

            d_scores(0)
            for h in range(CH + 1):
                if h < CH:
                    units(24 + h // 2, 2 * (h % 2), 2 * (h % 2) + 2)
                    if h + 1 < CH:
                        d_scores(h + 1)
                    p_turn(h, "d_p", "d_pt", "d_p_turned", C_L[:, 2 * (h % 2), :])
                if h >= 1:
                    d_pv(h - 1)
            for p in range(2):
                if p == 0:
                    pe.wait_ge(sem("d_y"), 2)
                for f in range(2):
                    for t in range(NT):
                        c = (2 * p + f) * P
                        ins = nc.tensor.transpose(ps[6 + p][:, f * S + t * P:f * S + (t + 1) * P], C_oc[:, t, c:c + P], ident)
                ins.then_inc(sem("c_turned"), 1)
            pe.wait_ge(sem("c_lo"), 2)
            pe.wait_ge(evac_act, ACT_EVACS[25])
            down(U_OC, 4, brh, brl, 0)

            def merged_ready(p):
                pe.wait_ge(sem("merged"), 8 + 2 * (p // 2 + 1))
                if p == 0:
                    pe.wait_ge(sem("merged"), 12)

            turn(lambda t: C_mg[:, t, :], merged_ready)
            pe.wait_ge(turned_lo, 8 * 7)
            down(U_W, KT, ath, atl)
            turn(lambda t: x[:, t, :], x_sum(4))
            ffn(2, U_F2, 7)


_INS = ["x", "positions", "norm_mix", "norm_ffn", "ffn_w_in", "ffn_w_out", "a_w_in", "a_b_gates", "a_g_out",
        "a_w_out", "b_w_in", "b_g_q", "b_g_k", "b_w_out", "norm1_g_2", "w_in_2", "sink_a_2", "qn_a_2", "kn_a_2",
        "conv_w_2", "conv_b_2", "filt_w1_2", "filt_b1_2", "filt_f1_2", "filt_w2_2", "filt_b2_2", "filt_f2_2",
        "filt_w3_2", "hy_d_2", "qn_c_2", "kn_c_2", "lam_q1_2", "lam_k1_2", "lam_q2_2", "lam_k2_2", "subln_c_2",
        "w_oa_2", "w_ob_2", "w_oc_2", "w_out_2", "norm2_g_2", "ffn_w1_2", "ffn_w3_2", "ffn_w2_2"]


def kernel(**inputs):
    import concourse.bacc as _bacc
    from concourse.bass_utils import run_bass_kernel_spmd as _run

    nc = _bacc.Bacc("TRN2", target_bir_lowering=False, num_devices=1)
    arrays, D = {}, {}
    for name in _INS:
        arrays[f"in_{name}"] = np.ascontiguousarray(inputs[name])
    arrays["in_consts"] = constants()
    arrays["in_decay"] = decay_table()
    for key, a in arrays.items():
        D[key[3:]] = nc.dram_tensor(key, a.shape, mybir.dt.from_np(a.dtype), kind="ExternalInput").ap()
    out = nc.dram_tensor("out", (1, S, DM), F32, kind="ExternalOutput").ap()
    build(nc, D, out)
    r = _run(nc, [arrays], core_ids=[0])
    return r.results[0]["out"]
```

```python
from contextlib import ExitStack
import math

import numpy as np
import concourse.bass as bass
from concourse import mybir

F32 = mybir.dt.float32
F32R = mybir.dt.float32r
I32 = mybir.dt.int32
ALU = mybir.AluOpType
ACT = mybir.ActivationFunctionType
AXX = mybir.AxisListType.X

P = 128
S = 256
NT = S // P
DM = 1024
KT = DM // P
EPS = 1e-6
UNIT = 1024
RING = 6
AHEAD = 1
DFF = 2816
FB = DFF // 256
AH, ADK, ADV = 4, 128, 256
BH, BD, BROT = 8, 128, 32
HW = 512
WQ, CH = 8, 4
HD = 64
LAM0 = 0.8 - 0.6 * math.exp(0.0)
NFT = 5
TWO_PI = 2.0 * math.pi
C1 = 6.28125
C2 = float(np.float32(TWO_PI - C1))
C3 = float(np.float32(TWO_PI - C1 - C2))
MAGIC = 12582912.0
PI_IN = 3.1415925
MASKED = -1e30

N_IN_A, N_IN_B = 6, 6
U_A = 0
U_AO = U_A + 4 * N_IN_A
U_F0 = U_AO + KT
FFN_UNITS = 4 + 6 * (FB - 1) + 2
U_B = U_F0 + FFN_UNITS
U_BO = U_B + 4 * N_IN_B
U_F1 = U_BO + KT
U_C = U_F1 + FFN_UNITS
U_GA = U_C + 4 * 8
U_OA = U_GA + 8
U_GB = U_OA + 4
U_OB = U_GB + 8
U_GC = U_OB + 4
U_OC = U_GC + 8
U_W = U_OC + 4
U_F2 = U_W + KT
U_END = U_F2 + FFN_UNITS

IN_BLOCKS = ([(U_A + 4 * i, 512, 2 * (i % 2)) for i in range(6)]
             + [(U_B + 4 * i, 512, 2 * (i % 2)) for i in range(6)]
             + [(U_C + 4 * i, 512 if i < 7 else 256, 2 * (i % 2) if i < 5 else 0) for i in range(8)]
             + [(U_GA, 512, 0), (U_GA + 4, 512, 0), (U_GB, 512, 0), (U_GB + 4, 512, 0),
                (U_GC, 512, 0), (U_GC + 4, 512, 0)])
ACT_BLOCKS = {4, 5} | set(range(12, 26))
ACT_EVACS = [sum(2 if j in ACT_BLOCKS else 1 for j in range(i + 1)) for i in range(len(IN_BLOCKS))]
DVE_EVACS = [sum(0 if j in ACT_BLOCKS else 1 for j in range(i + 1)) for i in range(len(IN_BLOCKS))]

BR_BANKS = (0, 1, 6, 7)
W_STEPS = [U_C + n for n in (22, 24, 26, 28, 32, 34, 36, 38, 40)]
D_STEPS = [U_GC + n for n in (2, 4, 5, 6, 8)]
B_SCORE = (4, 5, 4, 5, 0, 0, 0, 0)
B_TURN = (6, 7, 6, 7, 2, 2, 2, 2)
B_PV = (1, 1, 1, 1, 3, 3, 3, 3)
B_UNITS = [(U_B + 20 + h, 1) for h in range(4)] + [(U_BO, 2)] + [(U_BO + h - 3, 1) for h in range(5, 9)]
D_SCORE = (2, 4)
DOWN_BANKS = (4, 5, 6, 7)
TBANKS = (2, 3, 4, 5)

CONSTS = {}
_at = 0
for _name, _n in (("ident", P), ("ones", P), ("sel", AH * P), ("zT", S), ("nrmw", 4), ("inv", BROT // 2),
                  ("cosC", NT * HD // 2), ("sinC", NT * HD // 2), ("maskB", 384), ("maskW", NT * S),
                  ("fwd", NT * (NFT + 1) * P), ("bwd", 4 * S)):
    CONSTS[_name] = (_at, _n)
    _at += _n
N_CONST = _at
N_FIRST = CONSTS["inv"][0]


def constants():
    c = np.zeros((P, N_CONST), np.float32)

    def put(name, a):
        o, n = CONSTS[name]
        a = np.asarray(a, np.float64)
        c[:a.shape[0], o:o + n] = a.reshape(a.shape[0], n)

    put("ident", np.eye(P))
    put("ones", np.ones((P, P)))
    sel = np.zeros((AH, AH, P))
    for h in range(AH):
        sel[h, h] = 1.0
    put("sel", sel)
    pos = np.arange(S, dtype=np.float32)
    bands = np.arange(1, 17, dtype=np.float32)
    ang = (np.float32(2.0 * math.pi) * pos[:, None] * bands[None, :] / np.float32(S)).astype(np.float32)
    t = (pos / np.float32(S - 1)).astype(np.float32)
    z = np.concatenate([t[:, None], np.cos(ang), np.sin(ang)], axis=-1)
    put("zT", z.T)
    we, wd = np.full((S,), 0.5), np.full((S,), 0.5)
    we[0], wd[0] = 1.0, 0.0
    put("nrmw", np.sqrt(np.stack([we[:P], we[P:], wd[:P], wd[P:]], 1)))
    half = BROT // 2
    inv = (np.float32(500000.0) ** (-np.arange(half, dtype=np.float32) * np.float32(2.0 / BROT))).astype(np.float32)
    put("inv", np.tile(inv[None], (P, 1)))
    invc = (np.float32(10000.0) ** (-np.arange(0, HD, 2, dtype=np.float32) / np.float32(HD))).astype(np.float32)
    angc = (pos[:, None] * invc[None, :]).astype(np.float32).astype(np.float64)
    put("cosC", np.cos(angc).reshape(NT, P, HD // 2).transpose(1, 0, 2))
    put("sinC", np.sin(angc).reshape(NT, P, HD // 2).transpose(1, 0, 2))
    i = np.arange(P)
    diag = np.where(i[None, :] <= i[:, None], 0.0, MASKED)
    put("maskB", np.concatenate([diag, np.zeros((P, P)), diag], 1))
    key, tok = np.arange(S), np.arange(S)
    mw = np.where(np.abs(key[None, :] - tok[:, None]) <= 128, 0.0, MASKED)
    put("maskW", mw.reshape(NT, P, S).transpose(1, 0, 2))
    w = 2 * math.pi * np.outer(np.arange(S), np.arange(S)) / (2 * S)
    nyq = np.cos(math.pi * np.arange(S))
    cosm, sinm = np.cos(w), -np.sin(w)
    cosn = cosm[:, :P].copy()
    cosn[:, 0] = nyq
    sinn = sinm[:, :P].copy()
    sinn[:, 0] = nyq
    fwd = np.stack([cosm[:, :P], cosm[:, P:], cosn, sinm[:, :P], sinm[:, P:], sinn], 1)
    put("fwd", fwd.reshape(NT, P, NFT + 1, P).transpose(1, 0, 2, 3))
    ic = 2 * np.cos(w) / (2 * S)
    ic[0] = 1.0 / (2 * S)
    isn = -2 * np.sin(w) / (2 * S)
    isn[0] = nyq / (2 * S)
    put("bwd", np.stack([ic[:P], ic[P:], isn[:P], isn[P:]], 1))
    return c


def decay_table():
    pos = np.arange(S, dtype=np.float32)
    t = (pos / np.float32(S - 1)).astype(np.float32)
    lo, hi = math.log(1e-2) / 1.5, math.log(1e-2) / 0.3
    deltas = np.abs(np.linspace(lo, hi, HW, dtype=np.float32))
    d = np.exp((-t[:, None] * deltas[None, :]).astype(np.float32))
    return np.ascontiguousarray(d.reshape(NT, P, HW).transpose(1, 0, 2).astype(np.float32))


GROWS = {"mix": 0, "ffn": 16, "n1": 32, "n2": 40, "ago": 48, "subln": 56, "b1": 57, "f1": 58, "b2": 59, "f2": 60}
PRM = {}
_at = 0
for _name, _n in (("bg", 8), ("gq", BD), ("gk", BD), ("qa", HD), ("ka", HD), ("qc", HD), ("kc", HD),
                  ("sink", WQ), ("lq1", HD), ("lk1", HD), ("lq2", HD), ("lk2", HD)):
    PRM[_name] = (_at, _n)
    _at += _n
N_PRM = _at

N_WORK = 25200
W_H = N_WORK - 2 * NFT * HW


def build(nc, D, out):
    with ExitStack() as ctx:
        def sb(name, shape, dt=F32):
            return ctx.enter_context(nc.sbuf_tensor(name, shape, dt))

        sems = {}

        def sem(name):
            if name not in sems:
                sems[name] = ctx.enter_context(nc.semaphore(name))
            return sems[name]

        ring_at = -(-nc.sbuf_base // 32) * 32
        raw = sb("raw", [P, RING, UNIT])
        wlo = nc.alloc_sbuf_tensor_at("wlo", [P, RING, UNIT], F32R, offset=ring_at)
        whi = sb("whi", [P, RING, UNIT], F32R)
        x = sb("x", [P, NT, DM])
        ath = sb("ath", [P, KT, S], F32R)
        atl = sb("atl", [P, KT, S], F32R)
        brh = sb("brh", [P, 4, S], F32R)
        brl = sb("brl", [P, 4, S], F32R)
        hid = sb("hid", [P, NT, 256])
        sil = sb("sil", [P, NT, 256])
        con = sb("con", [P, N_CONST])
        prm = sb("prm", [P, N_PRM])
        grow = sb("grow", [64, P])
        gcol = sb("gcol", [P, 64])
        wg = sb("wg", [P, KT, 8])
        wgh = sb("wgh", [P, KT, 8], F32R)
        wgl = sb("wgl", [P, KT, 8], F32R)
        ssq = sb("ssq", [P, 6, NT])
        rstd = sb("rstd", [P, 6, NT])
        rhalf = sb("rhalf", [P, 6, NT])
        rq_a = sb("rq_a", [P, 64])
        rq_t = sb("rq_t", [P, 64])
        sm = sb("sm", [P, 512])
        work = sb("work", [P, N_WORK])
        ps = [ctx.enter_context(nc.psum_tensor(f"ps{i}", [P, 512], F32)) for i in range(8)]

        def C(name):
            o, n = CONSTS[name]
            return con[:, o:o + n]

        def R(name):
            o, n = PRM[name]
            return prm[:, o:o + n]

        def W(o, n):
            return work[:, o:o + n]

        ident = C("ident")
        maskW = C("maskW").rearrange("p (t s) -> p t s", t=NT)
        fwd = C("fwd").rearrange("p (t i f) -> p t i f", t=NT, i=NFT + 1)
        bwd = C("bwd").rearrange("p (i t) -> p i t", i=4)
        sel = C("sel").rearrange("p (h m) -> p h m", h=AH)
        cosC = C("cosC").rearrange("p (t f) -> p t f", t=NT)
        sinC = C("sinC").rearrange("p (t f) -> p t f", t=NT)

        A_qk = W(0, 2048).rearrange("p (t n) -> p t n", t=NT)
        A_num = W(0, 2056).rearrange("p (t h n) -> p t h n", t=NT, h=AH)
        A_v = W(2056, 2056).rearrange("p (t h n) -> p t h n", t=NT, h=AH)
        A_o = W(4112, 2048).rearrange("p (t n) -> p t n", t=NT)
        A_qT = W(6160, 1024).rearrange("p (h t) -> p h t", h=AH)
        A_kT = W(7184, 1024).rearrange("p (h t) -> p h t", h=AH)
        A_D = W(8208, 768).rearrange("p (b n) -> p b n", b=2)
        A_P = W(8976, 768).rearrange("p (b n) -> p b n", b=2)
        A_dec = W(9744, 1024).rearrange("p (t n) -> p t n", t=NT)
        A_fb = W(10768, 2048).rearrange("p (b d n) -> p b d n", b=2, d=2)
        A_ed = W(12816, 4096).rearrange("p (o t d n) -> p o t d n", o=2, t=NT, d=2)
        A_sq = W(16912, 2048).rearrange("p (t d n) -> p t d n", t=NT, d=2)
        A_w3 = work[0:64, 18960:18960 + 2048]
        A_dg = W(18960, 1024).rearrange("p (c n) -> p c n", c=8)
        A_rn = W(9744, 1024).rearrange("p (o n) -> p o n", o=2)
        H = W(W_H, 2 * NFT * HW).rearrange("p (o i n) -> p o i n", o=2, i=NFT)
        fil = work[0:64, W_H + 1024:W_H + 2048].rearrange("p (i t) -> p i t", i=4)
        fw12 = work[0:64, W_H + 2048:W_H + 2176].rearrange("p (i n) -> p i n", i=2)
        gate = work[0:4, N_WORK - 2048:N_WORK].rearrange("p (i t) -> p i t", i=8)
        am = sm[:, 352:368].rearrange("p (t c) -> p t c", t=NT)
        glog = sm[:, 368:384].rearrange("p (t c) -> p t c", t=NT)

        B_q = W(0, 2048).rearrange("p (t n) -> p t n", t=NT)
        B_k = W(2048, 2048).rearrange("p (t n) -> p t n", t=NT)
        B_v = W(4096, 2048).rearrange("p (t n) -> p t n", t=NT)
        B_qT = W(6144, 2048).rearrange("p (h t) -> p h t", h=BH)
        B_kT = W(8192, 2048).rearrange("p (h t) -> p h t", h=BH)
        B_L = W(10240, 1152).rearrange("p (b n) -> p b n", b=3)
        B_PT = W(11392, 768).rearrange("p (b n) -> p b n", b=2)
        B_sq = W(12160, 1024).rearrange("p (t n) -> p t n", t=NT)
        B_z = W(13184, 256).rearrange("p (t h n) -> p t h n", t=NT, h=4)
        B_T1 = W(13440, 512).rearrange("p (k t n) -> p k t n", k=2, t=NT)
        B_T2 = W(13952, 128).rearrange("p (k t n) -> p k t n", k=2, t=NT)
        B_ang = W(14080, 192).rearrange("p (i t n) -> p i t n", i=6, t=NT)
        posi = sb("posi", [P, NT], I32)
        posf = sb("posf", [P, NT])

        C_p = W(0, 7680).rearrange("p (t n) -> p t n", t=NT)
        C_th = W(7680, 2048).rearrange("p (t n) -> p t n", t=NT)
        C_mg = W(9728, 2048).rearrange("p (t n) -> p t n", t=NT)
        C_sp = W(9728, 1024).rearrange("p (t n) -> p t n", t=NT)
        C_sn = W(10752, 1024).rearrange("p (t n) -> p t n", t=NT)
        C_qT = W(11776, 1024).rearrange("p (h t) -> p h t", h=4)
        C_kT = W(12800, 1024).rearrange("p (h t) -> p h t", h=4)
        C_cw = W(14848, 1024).rearrange("p (j n) -> p j n", j=2)
        C_cx = W(16896, 1024).rearrange("p (j n) -> p j n", j=2)
        C_Y = W(13824, 2048).rearrange("p (i n) -> p i n", i=4)
        C_tm = W(15872, 1024).rearrange("p (i n) -> p i n", i=2)
        C_L = W(13824, 2048).rearrange("p (b n) -> p b n", b=4)
        C_PT = W(15872, 1024).rearrange("p (b n) -> p b n", b=2)
        C_hd = W(16896, 1024).rearrange("p (o n) -> p o n", o=2)
        C_T1 = W(17920, 512).rearrange("p (k t n) -> p k t n", k=4, t=NT)
        C_T2 = W(18432, 512).rearrange("p (k t n) -> p k t n", k=4, t=NT)
        C_z = W(18944, 1024)
        C_z1 = W(13824, 1024)
        hid_flat = hid[:, :, :].rearrange("p t n -> p (t n)")
        sil_flat = sil[:, :, :].rearrange("p t n -> p (t n)")
        H_prod = [C_tm[:, 0, :], C_tm[:, 1, :], hid_flat, sil_flat]
        C_kd = W(19456, 512).rearrange("p (t n) -> p t n", t=NT)
        C_oc = W(18944, 1024).rearrange("p (t n) -> p t n", t=NT)
        assert 18944 + 1024 <= W_H

        raw_loaded = [sem(f"raw_loaded{i}") for i in range(RING)]
        hi_ready, lo_ready, unit_used = sem("hi_ready"), sem("lo_ready"), sem("unit_used")
        turned, turned_hi, turned_lo = sem("turned"), sem("turned_hi"), sem("turned_lo")
        x_ready, ssq_ready, rstd_ready = sem("x_ready"), sem("ssq_ready"), sem("rstd_ready")
        evac_act, evac_dve = sem("evac_act"), sem("evac_dve")
        hid_T, hid_hi, hid_lo = sem("hid_T"), sem("hid_hi"), sem("hid_lo")
        sil_ready, hid_ready = sem("sil_ready"), sem("hid_ready")

        def unit_view(tile, slot, w):
            return tile[:, slot, :].rearrange("p (k n) -> p k n", k=2)[:, :, 0:w]

        def unit_width(u):
            return 256 if U_C + 28 <= u < U_C + 32 else 512

        block = ctx.enter_context(nc.Block())

        @block.sync
        def _(sp):
            nc.sync.dma_start(con[:, 0:P], D["consts"][:, 0:P]).then_inc(sem("ident_loaded"), 16)
            xv = D["x"][0].rearrange("(t p) n -> p t n", p=P)
            sp.wait_ge(sem("cleared"), 1)
            mix = D["norm_mix"].rearrange("l (k p) -> (l k) p", p=P)
            nc.sync.dma_start(grow[0:mix.shape[0], :], mix).then_inc(sem("mix_loaded"), 16)
            for t in range(NT):
                nc.sync.dma_start(x[:, t, :], xv[:, t, :]).then_inc(sem(f"x_loaded{t}"), 16)
            rows = [("ffn", D["norm_ffn"].rearrange("l (k p) -> (l k) p", p=P), P),
                    ("n1", D["norm1_g_2"].rearrange("l (k p) -> (l k) p", p=P), P),
                    ("n2", D["norm2_g_2"].rearrange("l (k p) -> (l k) p", p=P), P),
                    ("ago", D["a_g_out"].rearrange("l h (k p) -> (l h k) p", p=P), P),
                    ("subln", D["subln_c_2"], P), ("b1", D["filt_b1_2"], HD), ("f1", D["filt_f1_2"], HD),
                    ("b2", D["filt_b2_2"], HD), ("f2", D["filt_f2_2"], HD)]
            for name, src, w in rows:
                r = GROWS[name]
                nc.sync.dma_start(grow[r:r + src.shape[0], 0:w], src).then_inc(sem("grow_loaded"), 16)

            def load(u, halves):
                if u >= RING:
                    sp.wait_ge(unit_used, u - RING + 1)
                for dst, src in halves:
                    nc.sync.dma_start(dst, src).then_inc(raw_loaded[u % RING], 16)

            def load_in(u0, w, n0, nw=512):
                for i in range(4):
                    v = unit_view(raw, (u0 + i) % RING, nw)
                    load(u0 + i, [(v[:, kk, :], w[(2 * i + kk) * P:(2 * i + kk + 1) * P, n0:n0 + nw])
                                  for kk in range(2)])

            def load_out(u0, w, n):
                for k in range(n):
                    v = unit_view(raw, (u0 + k) % RING, 512)
                    load(u0 + k, [(v[:, nb, :], w[k * P:(k + 1) * P, nb * 512:(nb + 1) * 512])
                                  for nb in range(2)])

            def load_ffn(u0, gate_w, gate_n0, up_w, up_n0, down_w):
                gv = gate_w.rearrange("(k p) n -> p k n", p=P)
                uv = up_w.rearrange("(k p) n -> p k n", p=P)
                dv = down_w.rearrange("(k p) n -> p k n", p=P)

                def up(slot, i, n):
                    dst = raw[:, slot, :].rearrange("p (k n) -> p k n", k=2)
                    return [(dst[:, :, 0:256], gv[:, 2 * i:2 * i + 2, bass.ds(n + gate_n0, 256)]),
                            (dst[:, :, 256:512], uv[:, 2 * i:2 * i + 2, bass.ds(n + up_n0, 256)])]

                for i in range(4):
                    load(u0 + i, up((u0 + i) % RING, i, 0))
                with sp.Fori(1, FB) as j:
                    for c in range(6):
                        slot = (u0 + 4 + c) % RING
                        sp.wait_ge(unit_used, 6 * j + (u0 - 2 + c - RING + 1))
                        if c < 4:
                            pairs = up(slot, c, j * 256)
                        else:
                            v = unit_view(raw, slot, 512)
                            src = dv[:, bass.ds(2 * j + (c - 6), 1), :]
                            pairs = [(v[:, nb:nb + 1, :], src[:, :, nb * 512:(nb + 1) * 512]) for nb in range(2)]
                        for dst, s in pairs:
                            nc.sync.dma_start(dst, s).then_inc(raw_loaded[slot], 16)
                for k in range(2):
                    u = u0 + 4 + 6 * (FB - 1) + k
                    v = unit_view(raw, u % RING, 512)
                    load(u, [(v[:, nb, :], down_w[(2 * FB - 2 + k) * P:(2 * FB - 1 + k) * P, nb * 512:(nb + 1) * 512])
                             for nb in range(2)])

            for i in range(6):
                load_in(U_A + 4 * i, D["a_w_in"][0], 512 * i)
            load_out(U_AO, D["a_w_out"][0], KT)
            load_ffn(U_F0, D["ffn_w_in"][0], 0, D["ffn_w_in"][0], DFF, D["ffn_w_out"][0])
            for i in range(6):
                load_in(U_B + 4 * i, D["b_w_in"][0], 512 * i)
            load_out(U_BO, D["b_w_out"][0], KT)
            load_ffn(U_F1, D["ffn_w_in"][1], 0, D["ffn_w_in"][1], DFF, D["ffn_w_out"][1])
            w2 = D["w_in_2"][0]
            for i in range(7):
                load_in(U_C + 4 * i, w2, 512 * i)
            load_in(U_C + 28, w2, 3584, 256)
            for ug, uo, g0, wo in ((U_GA, U_OA, 3840, "w_oa_2"), (U_GB, U_OB, 4864, "w_ob_2"),
                                   (U_GC, U_OC, 5888, "w_oc_2")):
                load_in(ug, w2, g0)
                load_in(ug + 4, w2, g0 + 512)
                load_out(uo, D[wo][0], 4)
            load_out(U_W, D["w_out_2"][0], KT)
            load_ffn(U_F2, D["ffn_w1_2"][0], 0, D["ffn_w3_2"][0], 0, D["ffn_w2_2"][0])
            ov = out[0].rearrange("(t p) n -> p t n", p=P)
            for i in range(4):
                nb, t = divmod(i, 2)
                sp.wait_ge(x_ready, 20 + i + 1)
                nc.sync.dma_start(ov[:, t, nb * 512:(nb + 1) * 512], x[:, t, nb * 512:(nb + 1) * 512])\
                    .then_inc(sem(f"stored{i}"), 16)
            for i in range(4):
                sp.wait_ge(sem(f"stored{i}"), 16)

        @block.gpsimd
        def _(pool):
            nc.gpsimd.dma_start(wg[:, :, :], D["a_w_in"][0].rearrange("(k p) n -> p k n", p=P)[:, :, 3072:3080])\
                .then_inc(sem("wg_loaded"), 16)
            for name, src in (("bg", "a_b_gates"), ("gq", "b_g_q"), ("gk", "b_g_k"), ("qa", "qn_a_2"),
                              ("ka", "kn_a_2"), ("qc", "qn_c_2"), ("kc", "kn_c_2"), ("sink", "sink_a_2"),
                              ("lq1", "lam_q1_2"), ("lk1", "lam_k1_2"), ("lq2", "lam_q2_2"), ("lk2", "lam_k2_2")):
                n = PRM[name][1]
                nc.gpsimd.dma_start(R(name), D[src][0:1, :].to_broadcast([P, n])).then_inc(sem("prm_loaded"), 16)
            nc.gpsimd.dma_start(A_dec, D["decay"]).then_inc(sem("decay_loaded"), 16)
            nc.gpsimd.dma_start(A_w3, D["filt_w3_2"][0]).then_inc(sem("filt_loaded"), 16)
            nc.gpsimd.dma_start(fw12[0:33, 0, :], D["filt_w1_2"][0]).then_inc(sem("filt_loaded"), 16)
            nc.gpsimd.dma_start(fw12[:, 1, :], D["filt_w2_2"][0]).then_inc(sem("filt_loaded"), 16)
            nc.gpsimd.dma_start(posi[:, :], D["positions"][0].rearrange("(t p) -> p t", p=P), allow_slow_non_contiguous=True)\
                .then_inc(sem("pos_loaded"), 16)

            def filter_sums(i):
                o, t = divmod(i, 2)
                pool.wait_ge(sem("fb_ready"), 2 * i + 2)
                nc.gpsimd.tensor_tensor(A_ed[:, o, t, 0, :], A_fb[:, i % 2, 0, :], A_fb[:, i % 2, 1, :], ALU.add)\
                    .then_inc(sem("ed_ready"), 1)
                nc.gpsimd.tensor_tensor(A_ed[:, o, t, 1, :], A_fb[:, i % 2, 0, :], A_fb[:, i % 2, 1, :], ALU.subtract)\
                    .then_inc(sem("ed_ready"), 1)

            def filter_fold(o):
                pool.wait_ge(sem("f_sq"), 4 * o + 4)
                nc.gpsimd.tensor_tensor(A_sq[:, :, 0, :], A_sq[:, :, 0, :], A_sq[:, :, 1, :], ALU.add)\
                    .then_inc(sem("f_sum"), 1)
                pool.wait_ge(sem("f_sum"), 2 * o + 1)
                nc.gpsimd.tensor_tensor(A_sq[:, 0, 0, :], A_sq[:, 0, 0, :], A_sq[:, 1, 0, :], ALU.add)\
                    .then_inc(sem("f_sum"), 1)

            for i in range(4):
                filter_sums(i)
                cut = [N_FIRST + (N_CONST - N_FIRST) * j // 4 for j in (i, i + 1)]
                nc.gpsimd.dma_start(con[:, cut[0]:cut[1]], D["consts"][:, cut[0]:cut[1]]).then_inc(sem("con2_loaded"), 16)
                if i >= 2:
                    filter_fold(i - 2)
            for h in range(AH):
                pool.wait_ge(sem("a_p_ready"), h + 1)
                for c in (0, 256):
                    blk = A_P[:, h % 2, c:c + P]
                    nc.gpsimd.affine_select(out=blk, in_=blk, compare_op=ALU.is_ge, fill=0.0, base=0,
                                            pattern=[[1, P]], channel_multiplier=-1).then_inc(sem("a_p_masked"), 1)

            for b in range(4):
                dst, half = (B_q, b) if b < 2 else (B_k, b - 2)
                kind = b // 2
                pool.wait_ge(sem("b_swapped"), 2 * b + 2)
                pool.wait_ge(sem("b_sq"), 2 * b + 2)
                for t in range(NT):
                    y = dst[:, t, half * 512:(half + 1) * 512].rearrange("p (h d) -> p h d", h=4)
                    nc.gpsimd.tensor_tensor(y, y, B_T1[:, kind, t, :].unsqueeze(1).to_broadcast([P, 4, BD]),
                                            ALU.mult).then_inc(sem("b_scaled"), 1)

            pool.wait_ge(sem("c_tables"), 1)
            nc.gpsimd.memset(C_sp[0:1, 0, :], 0.0).then_inc(sem("edge_clear"), 1)
            nc.gpsimd.memset(C_sn[96:128, 1, :], 0.0).then_inc(sem("edge_clear"), 1)
            pool.wait_ge(sem("edge_clear"), 2)

            def conv_load(c):
                cols = slice(c * HW, (c + 1) * HW)
                if c:
                    pool.wait_ge(sem("conv_done"), c)
                for dst, src in ((C_cw[:, 0:2, :], D["conv_w_2"][0, 0:2, cols].unsqueeze(0).to_broadcast([P, 2, HW])),
                                 (C_cx[:, 0, :], D["conv_w_2"][0, 2:3, cols].to_broadcast([P, HW])),
                                 (C_cx[:, 1, :], D["conv_b_2"][0:1, cols].to_broadcast([P, HW]))):
                    nc.gpsimd.dma_start(dst, src).then_inc(sem("taps_loaded"), 16)

            def conv_part(c):
                p0 = 768 + c * HW
                part = C_p[:, :, p0:p0 + HW]
                last = 12 + 2 + c
                pool.wait_ge(evac_act, ACT_EVACS[last])
                pool.wait_ge(evac_dve, DVE_EVACS[last])
                nc.gpsimd.dma_start(C_sp[1:P, :, :], part[0:P - 1, :, :]).then_inc(sem("shifted"), 16)
                nc.gpsimd.dma_start(C_sp[0:1, 1, :], part[P - 1:P, 0, :]).then_inc(sem("shifted"), 16)
                nc.gpsimd.dma_start(C_sn[0:P - 1, :, :], part[1:P, :, :]).then_inc(sem("shifted"), 16)
                nc.gpsimd.dma_start(C_sn[P - 1:P, 0, :], part[0:1, 1, :]).then_inc(sem("shifted"), 16)
                pool.wait_ge(sem("taps_loaded"), 48 * (c + 1))
                pool.wait_ge(sem("shifted"), 64 * (c + 1))

                def tap(a):
                    return a.to_broadcast([P, NT, HW])

                def step(dst, a, b, op):
                    nc.gpsimd.tensor_tensor(dst, a, b, op).then_inc(sem("conv_step"), 1)

                step(C_sp, C_sp, tap(C_cw[:, 0:1, :]), ALU.mult)
                step(part, part, tap(C_cw[:, 1:2, :]), ALU.mult)
                step(C_sn, C_sn, tap(C_cx[:, 0:1, :]), ALU.mult)
                pool.wait_ge(sem("conv_step"), 6 * c + 2)
                step(part, part, C_sp, ALU.add)
                pool.wait_ge(sem("conv_step"), 6 * c + 4)
                step(part, part, C_sn, ALU.add)
                pool.wait_ge(sem("conv_step"), 6 * c + 5)
                step(part, part, tap(C_cx[:, 1:2, :]), ALU.add)
                pool.wait_ge(sem("conv_step"), 6 * c + 6)
                pool.nop().then_inc(sem("conv_done"), 1)

            for c in range(3):
                conv_load(c)
                conv_part(c)
            for o in range(2):
                nc.gpsimd.dma_start(C_hd[:, o, :], D["hy_d_2"][0, o:o + 1, :].to_broadcast([P, HW]))\
                    .then_inc(sem("hyd_loaded"), 16)

            def hyena_products():
                for o in range(2):
                    for y in range(4):
                        pool.wait_ge(sem("h_prod"), 8 * o + 2 * y + 2)
                        nc.gpsimd.tensor_tensor(C_Y[:, y, :], C_Y[:, y, :], H_prod[y],
                                                ALU.subtract if y < 2 else ALU.add).then_inc(sem("h_y"), 1)

            pool.wait_ge(evac_act, ACT_EVACS[18])
            pool.wait_ge(sem("c_ssq"), 5)
            z = C_z.rearrange("p (h d) -> p h d", h=16)
            d_steps = 0
            for t in range(NT):
                y = C_p[:, t, 2304:3328].rearrange("p (h d) -> p h d", h=16)
                for kind in range(2):
                    hs = slice(8 * kind, 8 * kind + 8)
                    for lo in (0, HD // 2):
                        hi = lo + HD // 2
                        nc.gpsimd.tensor_tensor(
                            z[:, hs, lo:hi], y[:, hs, HD // 2 - lo:HD - lo],
                            C_T2[:, 2 + kind, t, lo:hi].unsqueeze(1).to_broadcast([P, 8, HD // 2]), ALU.mult)\
                            .then_inc(sem("d_rot"), 1)
                d_steps += 4
                pool.wait_ge(sem("d_rot"), d_steps)
                for kind in range(2):
                    hs = slice(8 * kind, 8 * kind + 8)
                    nc.gpsimd.tensor_tensor(y[:, hs, :], y[:, hs, :],
                                            C_T1[:, 2 + kind, t, :].unsqueeze(1).to_broadcast([P, 8, HD]), ALU.mult)\
                        .then_inc(sem("d_rot"), 1)
                d_steps += 2
                pool.wait_ge(sem("d_rot"), d_steps)
                nc.gpsimd.tensor_tensor(y, y, z, ALU.add).then_inc(sem("d_rot"), 1)
                d_steps += 1
                pool.wait_ge(sem("d_rot"), d_steps)
                pool.wait_ge(sem("c_d_norms"), 1)
                o = 328 + 16 * t
                nc.gpsimd.tensor_tensor(y[:, 8:16, :], y[:, 8:16, :],
                                        sm[:, o:o + 8].unsqueeze(2).to_broadcast([P, 8, HD]), ALU.mult)\
                    .then_inc(sem("c_d_ready"), 1)
            hyena_products()

        @block.scalar
        def _(act):
            a_ = nc.scalar.activation
            steps = [0]

            def link(ins):
                steps[0] += 1
                ins.then_inc(sem("act_step"), 1)
                act.wait_ge(sem("act_step"), steps[0])

            nc.scalar.dma_start(con[:, P:N_FIRST], D["consts"][:, P:N_FIRST]).then_inc(sem("con1_loaded"), 16)

            fed = [0]

            def split_hi(slot, loaded, w=512):
                act.wait_ge(raw_loaded[slot], loaded)
                a_(unit_view(whi, slot, w), unit_view(raw, slot, w), ACT.Copy).then_inc(hi_ready, 1)

            def feed(n):
                for u in range(fed[0], n):
                    split_hi(u % RING, 32 * (u // RING + 1), unit_width(u))
                fed[0] = max(fed[0], n)

            def turn_hi(use, scale):
                for p in range(4):
                    act.wait_ge(turned, 4 * use + p + 1)
                    for f in range(2):
                        a_(ath[:, 2 * p + f, :], ps[TBANKS[p]][:, f * S:(f + 1) * S], ACT.Copy,
                           scale=scale(2 * p + f)).then_inc(turned_hi, 1)

            def squares(n):
                for t in range(NT):
                    if n == 0:
                        act.wait_ge(sem(f"x_loaded{t}"), 16)
                    else:
                        act.wait_ge(x_ready, 4 * n)
                    a_(W(t * DM, DM), x[:, t, :], ACT.Square, accum_out=ssq[:, n, t:t + 1]).then_inc(ssq_ready, 1)

            def evac(i, dst, func=ACT.Copy, n=0, tiles=(0,), scale=None):
                u0, w, bk = IN_BLOCKS[i]
                act.wait_ge(unit_used, u0 + 4)
                act.wait_ge(rstd_ready, n + 1)
                for t in tiles:
                    a_(dst(t), ps[bk + t][:, 0:w] if scale is None else ps[bk + t][:, 0:w], func,
                       scale=(rstd if scale is None else scale)[:, n, t:t + 1]).then_inc(evac_act, 1)

            def ffn(n, u0, norm):
                def silu(wait_units):
                    act.wait_ge(unit_used, wait_units)
                    for t in range(NT):
                        a_(sil[:, t, :], ps[t][:, 0:256], ACT.Silu, scale=rstd[:, norm, t:t + 1])\
                            .then_inc(sil_ready, 1)

                def turn(count):
                    act.wait_ge(hid_T, count)
                    a_(brh[:, 0:2, :], ps[2][:, :].rearrange("p (f t) -> p f t", f=2), ACT.Copy)\
                        .then_inc(hid_hi, 1)

                feed(u0 + 5)
                act.wait_ge(rstd_ready, norm + 1)
                act.wait_ge(sem("first_tile"), n + 1)
                a_(sil[:, 0, :], ps[0][:, 0:256], ACT.Silu, scale=rstd[:, norm, 0:1]).then_inc(sil_ready, 1)
                act.wait_ge(unit_used, u0 + 4)
                a_(sil[:, 1, :], ps[1][:, 0:256], ACT.Silu, scale=rstd[:, norm, 1:2]).then_inc(sil_ready, 1)
                with act.Fori(1, FB) as j:
                    def split(c):
                        v = u0 + 4 + c
                        split_hi(v % RING, 32 * j + 32 * (v // RING))
                    for c in range(1, 5):
                        split(c)
                    turn(j + FB * n)
                    for c in range(5, 7):
                        split(c)
                    silu(6 * j + (u0 - 2 + 4))
                last = u0 + 4 + 6 * (FB - 1)
                fed[0] = last + 1
                feed(last + 2)
                turn(FB * (n + 1))
                feed(min(last + 5 + AHEAD, U_END))

            act.wait_ge(sem("cols_turned"), 1)
            a_(gcol[:, 0:16], ps[6][:, 0:16], ACT.Copy).then_inc(sem("gcol_ready"), 1)
            act.wait_ge(sem("gcol_ready"), 1)
            feed(1)
            turn_hi(0, lambda f: gcol[:, GROWS["mix"] + f:GROWS["mix"] + f + 1])
            act.wait_ge(sem("cols_turned"), 2)
            a_(gcol[:, 16:64], ps[7][:, 272:320], ACT.Copy).then_inc(sem("gcol_ready"), 1)
            feed(3 + AHEAD)
            squares(0)
            feed(7 + AHEAD)
            evac(0, lambda t: A_qk[:, t, 0:512])
            act.wait_ge(sem("f_arg"), 1)
            a_(fil[:, 2, :], fil[:, 0, :], ACT.Sin).then_inc(sem("f_hidden"), 1)
            feed(11 + AHEAD)
            evac(1, lambda t: A_qk[:, t, 512:1024])

            def copy_qk(dst, n):
                act.wait_ge(sem("a_qk_turned"), n + 1)
                for c in range(2):
                    a_(dst[:, 2 * c:2 * c + 2, :], ps[4 + c][:, :].rearrange("p (h t) -> p h t", h=2), ACT.Copy)\
                        .then_inc(sem("a_qk_copied"), 1)

            copy_qk(A_qT, 0)
            act.wait_ge(sem("g_abs"), 1)
            link(a_(gate[:, 3, :], gate[:, 2, :], ACT.Exp, scale=-1.0))
            a_(gate[:, 2, :], gate[:, 3, :], ACT.Ln, bias=1.0).then_inc(sem("g_ln"), 1)
            act.wait_ge(sem("f_arg"), 2)
            a_(fil[:, 3, :], fil[:, 0, :], ACT.Sin).then_inc(sem("f_hidden"), 1)
            feed(13 + AHEAD)
            copy_qk(A_kT, 1)
            act.wait_ge(sem("g_m"), 1)
            a_(gate[:, 7, :], gate[:, 3, :], ACT.Exp, scale=-1.0).then_inc(sem("g_em"), 1)
            feed(15 + AHEAD)

            def v_dst(b):
                return lambda t: A_v[:, t, 2 * b:2 * b + 2, 0:ADV]

            def evac_v(i, b):
                u0, w, bk = IN_BLOCKS[i]
                act.wait_ge(unit_used, u0 + 4)
                a_(v_dst(b)(0), ps[bk][:, :].rearrange("p (h n) -> p h n", h=2), ACT.Copy,
                   scale=rstd[:, 0, 0:1]).then_inc(evac_act, 1)

            def filter_squares(i):
                o, t = divmod(i, 2)
                act.wait_ge(sem("ed_ready"), 2 * i + 2)
                if i >= 2:
                    act.wait_ge(sem("f_norm"), 1)
                for d in range(2):
                    w = CONSTS["nrmw"][0] + 2 * d + t
                    a_(A_sq[:, t, d, :], A_ed[:, o, t, d, :], ACT.Square, scale=con[:, w:w + 1])\
                        .then_inc(sem("f_sq"), 1)

            evac_v(2, 0)
            feed(17 + AHEAD)
            filter_squares(0)
            feed(19 + AHEAD)
            evac_v(3, 1)
            filter_squares(1)
            feed(21 + AHEAD)
            feed(23 + AHEAD)
            evac(4, lambda t: A_o[:, t, 0:512], ACT.Tanh, 0, (0, 1), rhalf)
            filter_squares(2)
            filter_squares(3)
            feed(24 + AHEAD)

            def a_weights(h):
                act.wait_ge(sem("a_d_ready"), h + 1)
                a_(A_D[:, h % 2, :], A_D[:, h % 2, :], ACT.Exp, scale=-1.0).then_inc(sem("a_e_ready"), 1)

            a_weights(0)
            a_weights(1)
            evac(5, lambda t: A_o[:, t, 512:1024], ACT.Tanh, 0, (0, 1), rhalf)
            feed(U_AO + 3 + AHEAD)
            act.wait_ge(sem("rn_spread"), 1)
            for o in range(2):
                a_(A_rn[:, o, :], ps[o][:, :], ACT.Copy).then_inc(sem("rn_ready"), 1)

            def a_norms(h):
                for t in range(NT):
                    act.wait_ge(sem("a_pv"), 2 * h + t + 1)
                    a_(W(10768 + 256 * (2 * h + t), 256), ps[(6, 4)[t] + h % 2][:, 0:ADV], ACT.Square,
                       accum_out=sm[:, 32 + 4 * t + h:33 + 4 * t + h]).then_inc(sem("a_ssq"), 1)

            a_norms(0)
            a_norms(1)
            a_weights(2)
            a_weights(3)
            a_norms(2)
            a_norms(3)
            turn_hi(1, lambda f: gcol[:, GROWS["ago"] + f:GROWS["ago"] + f + 1])
            feed(U_F0 + 3 + AHEAD)
            turn_hi(2, lambda f: gcol[:, GROWS["ffn"] + f:GROWS["ffn"] + f + 1])
            squares(1)
            ffn(0, U_F0, 1)

            turn_hi(3, lambda f: gcol[:, GROWS["mix"] + 8 + f:GROWS["mix"] + 9 + f])
            squares(2)
            act.wait_ge(sem("b_args"), 1)
            a_(B_ang[:, 4, :, :], B_ang[:, 2, :, :], ACT.Sin).then_inc(sem("b_sines"), 1)
            a_(B_ang[:, 5, :, :], B_ang[:, 3, :, :], ACT.Sin).then_inc(sem("b_sines"), 1)

            def b_squares(b):
                dst, half = (B_q, b) if b < 2 else (B_k, b - 2)
                act.wait_ge(evac_dve, DVE_EVACS[6 + b])
                act.wait_ge(evac_act, ACT_EVACS[6 + b])
                if b:
                    act.wait_ge(sem("b_ssq"), 2 * b)
                for t in range(NT):
                    a_(B_sq[:, t, :], dst[:, t, half * 512:(half + 1) * 512], ACT.Square)\
                        .then_inc(sem("b_sq"), 1)

            def b_copy(b):
                dst, half = (B_qT, b) if b < 2 else (B_kT, b - 2)
                act.wait_ge(sem("b_turned"), b + 1)
                a_(dst[:, 4 * half:4 * half + 2, :], ps[4 + 2 * (b % 2)][:, :].rearrange("p (h t) -> p h t", h=2),
                   ACT.Copy).then_inc(sem("b_copied_act"), 1)

            for b in range(4):
                dst, half = (B_q, b) if b < 2 else (B_k, b - 2)
                feed(U_B + 4 * b + 7 + AHEAD)
                evac(6 + b, lambda t: dst[:, t, half * 512:(half + 1) * 512], n=2)
                b_squares(b)
                if 1 <= b < 3:
                    b_copy(b - 1)
            feed(U_B + 21)
            b_copy(2)
            b_copy(3)
            evac(10, lambda t: B_v[:, t, 0:512], n=2)

            def b_feed(i):
                u, n = B_UNITS[i] if i <= BH else (U_BO, KT)
                feed(u + n)

            def b_exp(h):
                act.wait_ge(sem("b_max"), h + 1)
                c = sm[:, 64 + 8 * (h % 3):]
                for t, (lo, hi) in enumerate(((0, P), (P, 3 * P))):
                    a_(B_L[:, h % 3, lo:hi], B_L[:, h % 3, lo:hi], ACT.Exp, bias=c[:, t:t + 1],
                       accum_out=c[:, 2 + t:3 + t]).then_inc(sem("b_exp"), 1)

            def b_pt(h):
                act.wait_ge(sem("b_p_turned"), h + 1)
                a_(B_PT[:, h % 2, :], ps[B_TURN[h]][:, 0:384], ACT.Copy).then_inc(sem("b_pt"), 1)

            def b_out(h):
                act.wait_ge(sem("b_pv"), h + 1)
                dst = brh if h < 4 else ath
                a_(dst[:, h, :], ps[B_PV[h]][:, 0:S], ACT.Copy).then_inc(sem("b_out_hi"), 1)

            for i in range(BH + 2):
                b_feed(i)
                if i < BH:
                    b_exp(i)
                if 0 <= i - 1 < BH:
                    b_pt(i - 1)
                if i == 4:
                    evac(11, lambda t: B_v[:, t, 512:1024], n=2)
                if 0 <= i - 2 < BH:
                    b_out(i - 2)
            feed(U_F1 + 3 + AHEAD)
            turn_hi(4, lambda f: gcol[:, GROWS["ffn"] + 8 + f:GROWS["ffn"] + 9 + f])
            squares(3)
            ffn(1, U_F1, 3)

            turn_hi(5, lambda f: gcol[:, GROWS["n1"] + f:GROWS["n1"] + f + 1])
            squares(4)

            def c_evac(i):
                evac(12 + i, lambda t: C_p[:, t, 512 * i:512 * i + IN_BLOCKS[12 + i][1]], n=4, tiles=(0, 1))

            def c_squares(pieces):
                for dst, t, c0, c1 in pieces:
                    a_(dst, C_p[:, t, c0:c1], ACT.Square).then_inc(sem("c_sq"), 1)

            for i in range(4):
                feed(U_C + 4 * i + 7 + AHEAD)
                c_evac(i)
                if i == 1:
                    act.wait_ge(evac_act, ACT_EVACS[13])
                    c_squares([(C_z[:, 0:640], 0, 0, 640), (C_z1[:, 0:640], 1, 0, 640)])
            feed(U_C + 23 + AHEAD)
            c_evac(4)
            act.wait_ge(sem("c_w_turned"), 1)
            for c in range(2):
                a_(C_qT[:, 2 * c:2 * c + 2, :], ps[4 + c][:, :].rearrange("p (h t) -> p h t", h=2), ACT.Copy)\
                    .then_inc(sem("c_w_copied"), 1)
            a_(C_kT[:, 0:2, :], ps[6][:, :].rearrange("p (h t) -> p h t", h=2), ACT.Copy).then_inc(sem("c_w_copied"), 1)

            def gate_evac(i, half):
                u0, w, bk = IN_BLOCKS[i]
                act.wait_ge(unit_used, u0 + 4)
                for t in range(NT):
                    a_(C_th[:, t, half * 512:(half + 1) * 512], ps[bk + t][:, :], ACT.Tanh,
                       scale=rhalf[:, 4, t:t + 1]).then_inc(evac_act, 1)

            def w_exp(h):
                act.wait_ge(sem("w_max"), h + 1)
                c = sm[:, 128 + 16 * (h % 2):]
                for t in range(NT):
                    a_(C_L[:, h % 2, t * S:(t + 1) * S], C_L[:, h % 2, t * S:(t + 1) * S], ACT.Exp,
                       bias=c[:, 2 + t:3 + t], accum_out=c[:, 4 + t:5 + t]).then_inc(sem("w_exp"), 1)
                a_(c[:, 6:8], c[:, 2:4], ACT.Exp, bias=R("sink")[:, h:h + 1]).then_inc(sem("w_exp"), 1)

            def w_pt(h):
                act.wait_ge(sem("w_p_turned"), h + 1)
                a_(C_PT[:, h % 2, :], ps[6 + h % 2][:, :], ACT.Copy).then_inc(sem("w_pt"), 1)

            def w_out(i):
                act.wait_ge(sem("w_pv"), 2 * i + 2)
                a_(brh[:, i, :], ps[2 + i % 2][:, 0:S], ACT.Copy).then_inc(sem("w_out_hi"), 1)

            for i in range(WQ + 2):
                feed(W_STEPS[min(i, WQ)])
                if i == 2:
                    c_evac(5)
                if i == 4:
                    c_evac(6)
                    act.wait_ge(evac_act, ACT_EVACS[18])
                    c_squares([(C_z, 0, 2304, 3328), (hid_flat, 1, 2304, 2816), (sil_flat, 1, 2816, 3328)])
                if i == 5:
                    c_evac(7)
                if i == 7:
                    gate_evac(20, 0)
                if i < WQ:
                    w_exp(i)
                if 0 <= i - 1 < WQ:
                    w_pt(i - 1)
                if i >= 3 and i % 2 == 1:
                    w_out((i - 3) // 2)
            feed(U_OA + 2)
            gate_evac(21, 1)
            feed(U_OA + 3 + AHEAD)

            def d_copy(c):
                act.wait_ge(sem("d_turned"), c + 1)
                for hh in range(2):
                    a_((C_qT, C_kT)[c][:, 2 * hh:2 * hh + 2, :],
                       ps[2 + hh][:, :].rearrange("p (h t) -> p h t", h=2), ACT.Copy).then_inc(sem("d_copied"), 1)

            feed(U_GB + 1 + AHEAD)
            d_copy(0)
            feed(U_GB + 2 + AHEAD)
            d_copy(1)

            feed(U_GB + 5 + AHEAD)
            feed(U_GB + 7 + AHEAD)
            act.wait_ge(sem("merged"), 4)
            gate_evac(22, 0)
            feed(U_GB + 11 + AHEAD)
            gate_evac(23, 1)
            for p in range(2):
                act.wait_ge(sem("h_turned"), p + 1)
                a_(brh[:, 2 * p:2 * p + 2, :], ps[6 + p][:, :].rearrange("p (f t) -> p f t", f=2), ACT.Copy)\
                    .then_inc(sem("h_hi"), 1)
            feed(U_GC + 2)

            act.wait_ge(sem("lam_dots"), 2)
            a_(sm[:, 202:204], sm[:, 200:202], ACT.Exp).then_inc(sem("lam_exps"), 1)

            def d_exp(h):
                act.wait_ge(sem("d_max"), h + 1)
                c = sm[:, 208 + 32 * (h % 2):]
                for comp in range(2):
                    for t in range(NT):
                        i = 2 * comp + t
                        a_(C_L[:, 2 * (h % 2) + comp, t * S:(t + 1) * S],
                           ps[D_SCORE[h % 2] + comp][:, t * S:(t + 1) * S], ACT.Exp,
                           scale=c[:, 4 + i:5 + i], bias=c[:, 8 + i:9 + i], accum_out=c[:, 12 + i:13 + i])\
                            .then_inc(sem("d_exp"), 1)

            def d_pt(h):
                act.wait_ge(sem("d_p_turned"), h + 1)
                a_(C_PT[:, h % 2, :], ps[6][:, :], ACT.Copy).then_inc(sem("d_pt"), 1)

            def d_out(h):
                act.wait_ge(sem("d_pv"), h + 1)
                for t in range(NT):
                    a_((sil, hid)[h // 2][:, h % 2, t * P:(t + 1) * P], ps[7][:, t * P:(t + 1) * P], ACT.Square,
                       accum_out=sm[:, 272 + 4 * t + h:273 + 4 * t + h]).then_inc(sem("d_ssq"), 1)
                a_(C_oc[:, :, h * P:(h + 1) * P], ps[7][:, 0:S].rearrange("p (t n) -> p t n", t=NT),
                   ACT.Copy).then_inc(sem("d_oc"), 1)

            d_exp(0)
            for i in range(CH + 2):
                feed(D_STEPS[min(i, CH)])
                if 0 < i < CH:
                    d_exp(i)
                if i == 2:
                    act.wait_ge(sem("merged"), 8)
                    gate_evac(24, 0)
                if 0 <= i - 1 < CH:
                    d_pt(i - 1)
                if 0 <= i - 2 < CH:
                    d_out(i - 2)
            feed(U_OC + 2)
            gate_evac(25, 1)
            act.wait_ge(sem("sub_ready"), 1)
            for p in range(2):
                act.wait_ge(sem("c_turned"), p + 1)
                a_(brh[:, 2 * p:2 * p + 2, :], ps[4 + p][:, :].rearrange("p (f t) -> p f t", f=2), ACT.Copy,
                   scale=sm[:, 280:281]).then_inc(sem("c_hi"), 1)
            feed(U_W + 3 + AHEAD)
            turn_hi(6, lambda f: 0.5)
            feed(U_F2 + 3 + AHEAD)
            turn_hi(7, lambda f: gcol[:, GROWS["n2"] + f:GROWS["n2"] + f + 1])
            squares(5)
            ffn(2, U_F2, 5)

        @block.vector
        def _(dve):
            v_ = nc.vector
            steps = [0]

            def link(ins):
                steps[0] += 1
                ins.then_inc(sem("dve_step"), 1)
                dve.wait_ge(sem("dve_step"), steps[0])

            fed = [0]

            def split_lo(slot, ready, w=512):
                dve.wait_ge(hi_ready, ready)
                v_.tensor_tensor(unit_view(wlo, slot, w), unit_view(raw, slot, w), unit_view(whi, slot, w),
                                 ALU.subtract).then_inc(lo_ready, 1)

            def feed(n):
                for u in range(fed[0], n):
                    split_lo(u % RING, u + 1, unit_width(u))
                fed[0] = max(fed[0], n)

            def turn_lo(use, scale):
                for p in range(4):
                    dve.wait_ge(turned_hi, 8 * use + 2 * p + 2)
                    for f in range(2):
                        v_.scalar_tensor_tensor(atl[:, 2 * p + f, :], ps[TBANKS[p]][:, f * S:(f + 1) * S],
                                                scale(2 * p + f), ath[:, 2 * p + f, :], ALU.mult, ALU.subtract)\
                            .then_inc(turned_lo, 1)

            def rsqrt(dst, n):
                a, t = rq_a[:, 0:n], rq_t[:, 0:n]
                link(v_.tensor_scalar(t.bitcast(I32), a.bitcast(I32), 1, None, ALU.logical_shift_right))
                link(v_.tensor_scalar(dst.bitcast(I32), t.bitcast(I32), -1.0, float(0x5F3759DF), ALU.mult, ALU.add))
                for _ in range(3):
                    link(v_.tensor_tensor(t, dst, dst, ALU.mult))
                    link(v_.scalar_tensor_tensor(t, t, -0.5, a, ALU.mult, ALU.mult))
                    link(v_.scalar_tensor_tensor(dst, t, 1.5, dst, ALU.add, ALU.mult))

            def row_scale(n):
                dve.wait_ge(ssq_ready, 2 * (n + 1))
                link(v_.tensor_scalar(rq_a[:, 0:NT], ssq[:, n, :], 1.0 / DM, EPS, ALU.mult, ALU.add))
                rsqrt(rstd[:, n, :], NT)
                v_.tensor_scalar(rhalf[:, n, :], rstd[:, n, :], 0.5, None, ALU.mult).then_inc(rstd_ready, 1)
                dve.wait_ge(rstd_ready, n + 1)

            def evac(i, dst, n=0):
                u0, w, bk = IN_BLOCKS[i]
                dve.wait_ge(unit_used, u0 + 4)
                src = ps[bk + 1][:, 0:w]
                if len(dst.shape) == 3:
                    src = src.rearrange("p (h n) -> p h n", h=dst.shape[1])
                v_.tensor_scalar(dst, src, rstd[:, n, 1:2], None, ALU.mult).then_inc(evac_dve, 1)

            def residual(r, u_last):
                dve.wait_ge(unit_used, u_last)
                for nb in range(2):
                    for t in range(NT):
                        xs = x[:, t, nb * 512:(nb + 1) * 512]
                        v_.tensor_tensor(xs, xs, ps[4 + 2 * nb + t][:, :], ALU.add).then_inc(x_ready, 1)

            def ffn(n, u0, norm):
                def hidden(count):
                    for t in range(NT):
                        dve.wait_ge(sil_ready, count + t + 1)
                        v_.scalar_tensor_tensor(hid[:, t, :], ps[t][:, 256:512], rstd[:, norm, t:t + 1], sil[:, t, :],
                                                ALU.mult, ALU.mult).then_inc(hid_ready, 1)

                def turn(count):
                    dve.wait_ge(hid_hi, count)
                    v_.tensor_tensor(brl[:, 0:2, :], ps[2][:, :].rearrange("p (f t) -> p f t", f=2), brh[:, 0:2, :],
                                     ALU.subtract).then_inc(hid_lo, 1)

                feed(u0 + 5)
                hidden(2 * FB * n)
                with dve.Fori(1, FB) as j:
                    def split(c):
                        v = u0 + 4 + c
                        split_lo(v % RING, 6 * j + (u0 - 2 + c + 1))
                    for c in range(1, 5):
                        split(c)
                    turn(j + FB * n)
                    for c in range(5, 7):
                        split(c)
                    hidden(2 * j + 2 * FB * n)
                last = u0 + 4 + 6 * (FB - 1)
                fed[0] = last + 1
                feed(last + 2)
                turn(FB * (n + 1))
                feed(min(last + 5 + AHEAD, U_END))

            def turns(arg, k, cos, red):
                link(v_.tensor_scalar(k, arg, 1.0 / TWO_PI, 0.25 if cos else 0.0, ALU.mult, ALU.add))
                link(v_.tensor_scalar(k, k, MAGIC, MAGIC, ALU.add, ALU.subtract))
                link(v_.scalar_tensor_tensor(red, k, -C1, arg, ALU.mult, ALU.add))
                link(v_.scalar_tensor_tensor(red, k, -C2, red, ALU.mult, ALU.add))
                link(v_.scalar_tensor_tensor(red, k, -C3, red, ALU.mult, ALU.add))
                if cos:
                    link(v_.tensor_scalar(red, red, math.pi / 2, None, ALU.add))
                return v_.tensor_scalar(red, red, PI_IN, -PI_IN, ALU.min, ALU.max)

            v_.memset(grow[:, :], 0.0).then_inc(sem("cleared"), 1)
            v_.memset(A_v[:, :, :, ADV:ADV + 1], 1.0).then_inc(sem("cleared"), 1)
            feed(1)
            turn_lo(0, lambda f: gcol[:, GROWS["mix"] + f:GROWS["mix"] + f + 1])
            feed(3 + AHEAD)
            dve.wait_ge(sem("wg_loaded"), 16)
            v_.tensor_copy(wgh[:, :, :], wg[:, :, :]).then_inc(sem("wg_split"), 1)
            dve.wait_ge(sem("wg_split"), 1)
            v_.tensor_tensor(wgl[:, :, :], wg[:, :, :], wgh[:, :, :], ALU.subtract).then_inc(sem("wg_split"), 1)
            row_scale(0)
            feed(7 + AHEAD)
            evac(0, A_qk[:, 1, 0:512])

            dve.wait_ge(sem("gl_ready"), 1)
            dve.wait_ge(sem("prm_loaded"), 16 * len(PRM))
            for t in range(NT):
                v_.scalar_tensor_tensor(glog[:, t, :], ps[6][:, 8 * t:8 * t + 8], rstd[:, 0, t:t + 1], R("bg"),
                                        ALU.mult, ALU.add).then_inc(sem("glog"), 1)

            def filter_arg(i, bk):
                dve.wait_ge(sem("f_mm"), i + 1)
                b, f = GROWS["b1"] + 2 * i, GROWS["f1"] + 2 * i
                if i:
                    dve.wait_ge(sem("f_hidden"), i)
                link(v_.tensor_scalar(fil[:, 0, :], ps[bk][0:64, 0:S], gcol[0:64, b:b + 1], gcol[0:64, f:f + 1],
                                      ALU.add, ALU.mult))
                turns(fil[:, 0, :], fil[:, 1, :], False, fil[:, 0, :]).then_inc(sem("f_arg"), 1)

            filter_arg(0, 7)
            feed(11 + AHEAD)
            evac(1, A_qk[:, 1, 512:1024])
            dve.wait_ge(sem("gl_turned"), 1)
            v_.tensor_copy(gate[:, 0, :], ps[7][0:4, 0:S]).then_inc(sem("g_rows"), 1)
            v_.tensor_copy(gate[:, 1, :], ps[7][0:4, S:2 * S]).then_inc(sem("g_rows"), 1)
            dve.wait_ge(sem("g_rows"), 2)
            v_.scalar_tensor_tensor(gate[:, 2, :], gate[:, 1, :], -1.0, gate[:, 1, :], ALU.mult, ALU.max)\
                .then_inc(sem("g_abs"), 1)
            filter_arg(1, 6)
            dve.wait_ge(sem("g_ln"), 1)
            link(v_.scalar_tensor_tensor(gate[:, 1, :], gate[:, 1, :], 0.0, gate[:, 2, :], ALU.min, ALU.subtract))
            dve.wait_ge(sem("con1_loaded"), 16)
            link(v_.tensor_tensor_scan(gate[:, 4, :], con[0:4, CONSTS["ones"][0]:CONSTS["ones"][0] + 1]
                                       .to_broadcast([4, S]), gate[:, 1, :], 0.0, ALU.mult, ALU.add))
            link(v_.tensor_tensor(gate[:, 5, :], gate[:, 0, :], gate[:, 4, :], ALU.subtract))
            link(v_.tensor_tensor_scan(gate[:, 6, :], gate[:, 5, :], gate[:, 5, :], 0.0, ALU.max, ALU.max))
            v_.tensor_tensor(gate[:, 3, :], gate[:, 4, :], gate[:, 6, :], ALU.add).then_inc(sem("g_m"), 1)
            feed(15 + AHEAD)
            evac(2, A_v[:, 1, 0:2, 0:ADV])
            dve.wait_ge(sem("decay_loaded"), 16)

            def filter_decay(i):
                t = i % 2
                dve.wait_ge(sem("f3"), i + 1)
                if i >= 2:
                    dve.wait_ge(sem("ed_ready"), 2 * (i - 1))
                for d in range(2):
                    v_.tensor_tensor(A_fb[:, i % 2, d, :], ps[(4, 6)[i % 2] + d][:, :], A_dec[:, t, :], ALU.mult)\
                        .then_inc(sem("fb_ready"), 1)

            filter_decay(0)
            feed(17 + AHEAD)
            filter_decay(1)
            feed(19 + AHEAD)
            evac(3, A_v[:, 1, 2:4, 0:ADV])
            filter_decay(2)
            feed(21 + AHEAD)
            filter_decay(3)
            dve.wait_ge(sem("am_turned"), 1)
            v_.tensor_copy(am[:, :, :], ps[5][:, 0:16].rearrange("p (t c) -> p t c", t=NT)).then_inc(sem("am_ready"), 1)
            feed(23 + AHEAD)
            dve.wait_ge(sem("f_norm"), 2)
            v_.tensor_scalar(rq_a[:, 0:8], ps[4][:, 0:8], EPS, None, ALU.add).then_inc(sem("f_norm_read"), 1)
            dve.wait_ge(sem("f_norm_read"), 1)
            rsqrt(sm[:, 0:8], 8)
            for c in range(8):
                v_.tensor_scalar(A_dg[:, c, :], ident, sm[:, c:c + 1], None, ALU.mult).then_inc(sem("dg_ready"), 1)
            feed(24 + AHEAD)

            def a_dist(h):
                dve.wait_ge(sem("a_scores"), h + 1)
                dve.wait_ge(sem("am_ready"), 1)
                if h >= 2:
                    dve.wait_ge(sem("a_p_ready"), h - 1)
                mb = ps[4 + h % 2]
                v_.tensor_scalar(A_D[:, h % 2, 0:S], mb[:, 0:S], am[:, 0, h:h + 1], 0.0, ALU.subtract, ALU.max)\
                    .then_inc(sem("a_d0"), 1)
                v_.tensor_scalar(A_D[:, h % 2, S:384], mb[:, P:S], am[:, 1, h:h + 1], 0.0, ALU.subtract, ALU.max)\
                    .then_inc(sem("a_d_ready"), 1)

            def a_prob(h):
                dve.wait_ge(sem("a_e_ready"), h + 1)
                if h >= 2:
                    dve.wait_ge(sem("a_pv"), 2 * (h - 1))
                v_.scalar_tensor_tensor(A_P[:, h % 2, :], ps[6 + h % 2][:, 0:384], float(ADK) ** -0.5, A_D[:, h % 2, :],
                                        ALU.mult, ALU.mult).then_inc(sem("a_p_ready"), 1)

            def a_num(h):
                for t in range(NT):
                    dve.wait_ge(sem("a_ssq"), 2 * h + t + 1)
                    v_.tensor_copy(A_num[:, t, h, :], ps[(6, 4)[t] + h % 2][:, 0:ADV + 1]).then_inc(sem("a_num"), 1)

            def spectrum(i):
                dve.wait_ge(sem("spec"), i + 1)
                dve.wait_ge(sem("rn_ready"), 2)
                o, f = divmod(i, NFT)
                v_.tensor_tensor(H[:, o, f, :], ps[2 + i % 2][:, :], A_rn[:, o, :], ALU.mult).then_inc(sem("spec_ready"), 1)

            a_dist(0)
            a_dist(1)
            a_prob(0)
            a_prob(1)
            feed(U_AO + 3 + AHEAD)
            spectrum(0)
            spectrum(1)
            a_num(0)
            a_num(1)
            spectrum(2)
            a_dist(2)
            a_dist(3)
            a_prob(2)
            a_prob(3)
            for i in range(3, 5):
                spectrum(i)
            a_num(2)
            a_num(3)
            spectrum(5)
            dve.wait_ge(sem("a_num"), 8)
            dve.wait_ge(sem("a_ssq"), 8)
            dve.wait_ge(evac_act, ACT_EVACS[5])
            den = A_num[:, :, :, ADV]
            r8 = sm[:, 8:16].rearrange("p (t h) -> p t h", t=NT)
            link(v_.tensor_copy(r8, den))
            link(v_.scalar_tensor_tensor(r8, r8, -1.0, r8, ALU.mult, ALU.max))
            link(v_.tensor_tensor(r8, r8, am[:, :, 4:8], ALU.max))
            link(v_.reciprocal(sm[:, 16:24], sm[:, 8:16]))
            link(v_.tensor_tensor(sm[:, 24:32], sm[:, 16:24], sm[:, 16:24], ALU.mult))
            link(v_.tensor_tensor(rq_a[:, 0:8], sm[:, 24:32], sm[:, 32:40], ALU.mult))
            link(v_.tensor_scalar(rq_a[:, 0:8], rq_a[:, 0:8], 1.0 / ADV, EPS, ALU.mult, ALU.add))
            spectrum(6)
            rsqrt(sm[:, 40:48], 8)
            spectrum(7)
            link(v_.scalar_tensor_tensor(sm[:, 48:56], sm[:, 40:48], 0.5, sm[:, 16:24], ALU.mult, ALU.mult))
            for h in range(AH):
                for t in range(NT):
                    o = A_o[:, t, h * ADV:(h + 1) * ADV]
                    ins = v_.scalar_tensor_tensor(o, o, 1.0, A_num[:, t, h, 0:ADV], ALU.add, ALU.mult)
                link(ins)
                for t in range(NT):
                    o = A_o[:, t, h * ADV:(h + 1) * ADV]
                    v_.tensor_scalar(o, o, sm[:, 48 + 4 * t + h:49 + 4 * t + h], None, ALU.mult)\
                        .then_inc(sem("a_y"), 1)
            turn_lo(1, lambda f: gcol[:, GROWS["ago"] + f:GROWS["ago"] + f + 1])
            for i in range(8, 10):
                spectrum(i)
            feed(U_F0 + 3 + AHEAD)
            residual(0, U_F0)
            turn_lo(2, lambda f: gcol[:, GROWS["ffn"] + f:GROWS["ffn"] + f + 1])
            row_scale(1)
            ffn(0, U_F0, 1)

            residual(1, U_B)
            turn_lo(3, lambda f: gcol[:, GROWS["mix"] + 8 + f:GROWS["mix"] + 9 + f])
            row_scale(2)
            dve.wait_ge(sem("pos_loaded"), 16)
            dve.wait_ge(sem("con2_loaded"), 64)
            link(v_.tensor_copy(posf[:, :], posi[:, :]))
            for t in range(NT):
                link(v_.tensor_scalar(B_ang[:, 0, t, :], C("inv"), posf[:, t:t + 1], None, ALU.mult))
            link(turns(B_ang[:, 0, :, :], B_ang[:, 1, :, :], False, B_ang[:, 2, :, :]))
            turns(B_ang[:, 0, :, :], B_ang[:, 1, :, :], True, B_ang[:, 3, :, :]).then_inc(sem("b_args"), 1)
            feed(U_B + 7 + AHEAD)
            evac(6, B_q[:, 1, 0:512], n=2)
            dve.wait_ge(sem("b_sines"), 2)
            hr = BROT // 2
            for kind, name in enumerate(("gq", "gk")):
                def g(lo, hi):
                    return R(name)[:, lo:hi].unsqueeze(1).to_broadcast([P, NT, hi - lo])
                cs, sn = B_ang[:, 5, :, :], B_ang[:, 4, :, :]
                v_.tensor_tensor(B_T1[:, kind, :, 0:hr], cs, g(0, hr), ALU.mult).then_inc(sem("b_tables"), 1)
                v_.tensor_tensor(B_T1[:, kind, :, hr:BROT], cs, g(hr, BROT), ALU.mult).then_inc(sem("b_tables"), 1)
                v_.tensor_copy(B_T1[:, kind, :, BROT:], g(BROT, BD)).then_inc(sem("b_tables"), 1)
                v_.scalar_tensor_tensor(B_T2[:, kind, :, 0:hr], sn, -1.0, g(hr, BROT), ALU.mult, ALU.mult)\
                    .then_inc(sem("b_tables"), 1)
                v_.tensor_tensor(B_T2[:, kind, :, hr:BROT], sn, g(0, hr), ALU.mult).then_inc(sem("b_tables"), 1)
            dve.wait_ge(sem("b_tables"), 10)

            def b_rotate(b):
                dst, half = (B_q, b) if b < 2 else (B_k, b - 2)
                kind = b // 2
                dve.wait_ge(evac_act, ACT_EVACS[6 + b])
                dve.wait_ge(evac_dve, DVE_EVACS[6 + b])
                for t in range(NT):
                    y = dst[:, t, half * 512:(half + 1) * 512].rearrange("p (h d) -> p h d", h=4)
                    for lo in (0, hr):
                        v_.tensor_tensor(B_z[:, t, :, lo:lo + hr], y[:, :, hr - lo:BROT - lo],
                                         B_T2[:, kind, t, lo:lo + hr].unsqueeze(1).to_broadcast([P, 4, hr]), ALU.mult)\
                            .then_inc(sem("b_swapped") if lo else sem("b_swap0"), 1)
                for t in range(NT):
                    dve.wait_ge(sem("b_sq"), 2 * b + t + 1)
                    o = 384 + 16 * kind + 8 * t + 4 * half
                    v_.tensor_reduce(sm[:, o:o + 4], B_sq[:, t, :].rearrange("p (h d) -> p h d", h=4), AXX, ALU.add)\
                        .then_inc(sem("b_ssq"), 1)
                dve.wait_ge(sem("b_ssq"), 2 * b + 2)
                if half == 1:
                    link(v_.tensor_scalar(rq_a[:, 0:16], sm[:, 384 + 16 * kind:400 + 16 * kind], 1.0 / BD, EPS,
                                          ALU.mult, ALU.add))
                    rsqrt(sm[:, 416 + 16 * kind:432 + 16 * kind], 16)
                for t in range(NT):
                    y = dst[:, t, half * 512:(half + 1) * 512].rearrange("p (h d) -> p h d", h=4)
                    dve.wait_ge(sem("b_scaled"), 2 * b + t + 1)
                    v_.tensor_tensor(y[:, :, 0:BROT], y[:, :, 0:BROT], B_z[:, t, :, :], ALU.add)\
                        .then_inc(sem("b_rotated"), 1)

            def b_knorm(half):
                dve.wait_ge(sem("b_rotated"), 8 if half else 6)
                for t in range(NT):
                    y = B_k[:, t, half * 512:(half + 1) * 512].rearrange("p (h d) -> p h d", h=4)
                    o = 432 + 8 * t + 4 * half
                    v_.tensor_tensor(y, y, sm[:, o:o + 4].unsqueeze(2).to_broadcast([P, 4, BD]), ALU.mult)\
                        .then_inc(sem("b_knormed"), 1)

            def b_copy(b):
                dst, half = (B_qT, b) if b < 2 else (B_kT, b - 2)
                dve.wait_ge(sem("b_turned"), b + 1)
                v_.tensor_copy(dst[:, 4 * half + 2:4 * half + 4, :],
                               ps[5 + 2 * (b % 2)][:, :].rearrange("p (h t) -> p h t", h=2))\
                    .then_inc(sem("b_copied_dve"), 1)

            b_rotate(0)
            for b in range(1, 4):
                dst, half = (B_q, b) if b < 2 else (B_k, b - 2)
                feed(U_B + 4 * b + 7 + AHEAD)
                evac(6 + b, dst[:, 1, half * 512:(half + 1) * 512], n=2)
                if b < 3:
                    b_copy(b - 1)
                b_rotate(b)
                if b == 1:
                    link(v_.tensor_scalar(sm[:, 416:432], sm[:, 416:432], float(BD) ** -0.5, None, ALU.mult))
            b_knorm(0)
            b_knorm(1)
            feed(U_B + 21)
            b_copy(2)
            b_copy(3)
            evac(10, B_v[:, 1, 0:512], n=2)

            def b_feed(i):
                u, n = B_UNITS[i] if i <= BH else (U_BO, KT)
                feed(u + n)

            maskB = C("maskB")

            def b_logits(h):
                dve.wait_ge(sem("b_scores"), h + 1)
                if h >= 3:
                    dve.wait_ge(sem("b_p_turned"), h - 2)
                c = sm[:, 64 + 8 * (h % 3):]
                for t, (lo, hi) in enumerate(((0, P), (P, 3 * P))):
                    q = sm[:, 416 + 8 * t + h:417 + 8 * t + h]
                    v_.scalar_tensor_tensor(B_L[:, h % 3, lo:hi], ps[B_SCORE[h]][:, lo:hi], q, maskB[:, lo:hi],
                                            ALU.mult, ALU.add).then_inc(sem("b_l"), 1)
                dve.wait_ge(sem("b_l"), 2 * h + 2)
                for t, (lo, hi) in enumerate(((0, P), (P, 3 * P))):
                    ins = v_.tensor_reduce(c[:, 4 + t:5 + t], B_L[:, h % 3, lo:hi], AXX, ALU.max)
                link(ins)
                v_.tensor_scalar(c[:, 0:2], c[:, 4:6], -1.0, None, ALU.mult).then_inc(sem("b_max"), 1)

            def b_prob(h):
                dve.wait_ge(sem("b_exp"), 2 * h + 2)
                c = sm[:, 64 + 8 * (h % 3):]
                link(v_.reciprocal(c[:, 6:8], c[:, 2:4]))
                for t, (lo, hi) in enumerate(((0, P), (P, 3 * P))):
                    v_.tensor_scalar(B_L[:, h % 3, lo:hi], B_L[:, h % 3, lo:hi], c[:, 6 + t:7 + t], None, ALU.mult)\
                        .then_inc(sem("b_p"), 1)

            def b_out(h):
                dve.wait_ge(sem("b_out_hi"), h + 1)
                hi, lo = (brh, brl) if h < 4 else (ath, atl)
                v_.tensor_tensor(lo[:, h, :], ps[B_PV[h]][:, 0:S], hi[:, h, :], ALU.subtract).then_inc(sem("b_out_lo"), 1)

            for i in range(BH + 2):
                if 0 <= i - 1 < BH:
                    b_prob(i - 1)
                if i < BH:
                    b_logits(i)
                b_feed(i)
                if i == 4:
                    evac(11, B_v[:, 1, 512:1024], n=2)
                if 0 <= i - 2 < BH:
                    b_out(i - 2)
            feed(U_F1 + 3 + AHEAD)
            residual(2, U_F1)
            turn_lo(4, lambda f: gcol[:, GROWS["ffn"] + 8 + f:GROWS["ffn"] + 9 + f])
            row_scale(3)
            ffn(1, U_F1, 3)

            residual(3, U_C)
            turn_lo(5, lambda f: gcol[:, GROWS["n1"] + f:GROWS["n1"] + f + 1])
            row_scale(4)
            hh = HD // 2
            for kind, name in enumerate(("qa", "ka", "qc", "kc")):
                def g(lo, hi):
                    return R(name)[:, lo:hi].unsqueeze(1).to_broadcast([P, NT, hi - lo])
                v_.tensor_tensor(C_T1[:, kind, :, 0:hh], cosC, g(0, hh), ALU.mult)
                v_.tensor_tensor(C_T1[:, kind, :, hh:HD], cosC, g(hh, HD), ALU.mult)
                v_.scalar_tensor_tensor(C_T2[:, kind, :, 0:hh], sinC, -1.0, g(hh, HD), ALU.mult, ALU.mult)
                ins = v_.tensor_tensor(C_T2[:, kind, :, hh:HD], sinC, g(0, hh), ALU.mult)
            ins.then_inc(sem("c_tables"), 1)
            dve.wait_ge(sem("c_tables"), 1)

            def c_sums(i, src, o, nh):
                dve.wait_ge(sem("c_sq"), i + 1)
                v_.tensor_reduce(sm[:, o:o + nh], src.rearrange("p (h d) -> p h d", h=nh), AXX, ALU.add)\
                    .then_inc(sem("c_ssq"), 1)

            def c_norms(pieces, o, n):
                dve.wait_ge(sem("c_ssq"), pieces)
                link(v_.tensor_scalar(rq_a[:, 0:n], sm[:, o:o + n], 1.0 / HD, EPS, ALU.mult, ALU.add))
                rsqrt(sm[:, o:o + n], n)

            limit = [0]

            def tick():
                if fed[0] < limit[0]:
                    feed(fed[0] + 1)

            def c_rotate(t, c0, nh, kind, after):
                y = C_p[:, t, c0:c0 + nh * HD].rearrange("p (h d) -> p h d", h=nh)
                z = C_z[:, 0:nh * HD].rearrange("p (h d) -> p h d", h=nh)
                for lo in (0, hh):
                    ins = v_.tensor_tensor(z[:, :, lo:lo + hh], y[:, :, hh - lo:HD - lo],
                                           C_T2[:, kind, t, lo:lo + hh].unsqueeze(1).to_broadcast([P, nh, hh]), ALU.mult)
                link(ins)
                link(v_.tensor_tensor(y, y, C_T1[:, kind, t, :].unsqueeze(1).to_broadcast([P, nh, HD]), ALU.mult))
                tick()
                return v_.tensor_tensor(y, y, z, ALU.add)

            def c_scale(t, c0, nh, o, dst=None):
                y = C_p[:, t, c0:c0 + nh * HD].rearrange("p (h d) -> p h d", h=nh)
                return v_.tensor_tensor(y if dst is None else dst, y, sm[:, o:o + nh].unsqueeze(2).to_broadcast([P, nh, HD]), ALU.mult)

            feed(U_C + 11 + AHEAD)
            limit[0] = U_C + 23 + AHEAD
            c_sums(0, C_z[:, 0:640], 300, 10)
            tick()
            c_sums(1, C_z1[:, 0:640], 310, 10)
            tick()
            c_norms(2, 300, 20)
            tick()
            for t in range(NT):
                link(c_rotate(t, 0, 8, 0, None))
                tick()
                link(c_rotate(t, 512, 2, 1, None))
                for twin in range(2):
                    kd = C_kd[:, t, :].rearrange("p (h w d) -> p h w d", h=2, w=2)[:, :, twin, :]
                    link(c_scale(t, 512, 2, 308 + 10 * t, kd))
                tick()
            v_.tensor_scalar(sm[:, 300:320], sm[:, 300:320], float(HD) ** -0.5, None, ALU.mult)\
                .then_inc(sem("c_w_ready"), 1)
            dve.wait_ge(sem("c_w_ready"), 1)
            feed(U_C + 23 + AHEAD)

            def w_logits(h):
                dve.wait_ge(sem("w_scores"), h + 1)
                if h >= 2:
                    dve.wait_ge(sem("w_p_turned"), h - 1)
                c = sm[:, 128 + 16 * (h % 2):]
                for t in range(NT):
                    v_.scalar_tensor_tensor(C_L[:, h % 2, t * S:(t + 1) * S], ps[4 + h % 2][:, t * S:(t + 1) * S],
                                            sm[:, 300 + 10 * t + h:301 + 10 * t + h], maskW[:, t, :],
                                            ALU.mult, ALU.add).then_inc(sem("w_l"), 1)
                dve.wait_ge(sem("w_l"), 2 * h + 2)
                link(v_.tensor_reduce(c[:, 0:2], C_L[:, h % 2, :].rearrange("p (t s) -> p t s", t=NT), AXX, ALU.max))
                v_.tensor_scalar(c[:, 2:4], c[:, 0:2], R("sink")[:, h:h + 1], -1.0, ALU.max, ALU.mult)\
                    .then_inc(sem("w_max"), 1)

            def w_prob(h):
                dve.wait_ge(sem("w_exp"), 3 * h + 3)
                c = sm[:, 128 + 16 * (h % 2):]
                link(v_.tensor_tensor(c[:, 8:10], c[:, 4:6], c[:, 6:8], ALU.add))
                link(v_.reciprocal(c[:, 10:12], c[:, 8:10]))
                for t in range(NT):
                    v_.tensor_scalar(C_L[:, h % 2, t * S:(t + 1) * S], C_L[:, h % 2, t * S:(t + 1) * S],
                                     c[:, 10 + t:11 + t], None, ALU.mult).then_inc(sem("w_p"), 1)

            def w_out(i):
                dve.wait_ge(sem("w_out_hi"), i + 1)
                v_.tensor_tensor(brl[:, i, :], ps[2 + i % 2][:, 0:S], brh[:, i, :], ALU.subtract)\
                    .then_inc(sem("w_out_lo"), 1)

            for i in range(WQ + 2):
                if 0 <= i - 1 < WQ:
                    w_prob(i - 1)
                if i < WQ:
                    w_logits(i)
                feed(W_STEPS[min(i, WQ)])
                if i >= 3 and i % 2 == 1:
                    w_out((i - 3) // 2)
                if i == 5:
                    c_sums(2, C_z, 320, 16)
                if i == 6:
                    c_sums(3, hid_flat, 336, 8)
                    c_sums(4, sil_flat, 344, 8)
                if i == 7:
                    c_norms(5, 320, 32)
                    q_scale = sm[:, 320:352].rearrange("p (t h) -> p t h", t=NT)[:, :, 0:8]
                    v_.tensor_scalar(q_scale, q_scale, float(HD) ** -0.5, None, ALU.mult)\
                        .then_inc(sem("c_d_norms"), 1)
            dve.wait_ge(sem("c_d_norms"), 1)
            feed(U_OA + 3 + AHEAD)

            def merge(b, banks, u_last):
                if b == 0:
                    dve.wait_ge(sem("conv_done"), 3)
                dve.wait_ge(unit_used, u_last)
                dve.wait_ge(evac_act, ACT_EVACS[21 + 2 * b])
                for nb in range(2):
                    for t in range(NT):
                        th = C_th[:, t, nb * 512:(nb + 1) * 512]
                        m = C_mg[:, t, nb * 512:(nb + 1) * 512]
                        bk = ps[banks[2 * nb + t]][:, :]
                        if b == 0:
                            v_.scalar_tensor_tensor(m, th, 1.0, bk, ALU.add, ALU.mult).then_inc(sem("merged"), 1)
                        else:
                            link(v_.scalar_tensor_tensor(th, th, 1.0, bk, ALU.add, ALU.mult))
                            v_.tensor_tensor(m, m, th, ALU.add).then_inc(sem("merged"), 1)

            feed(U_GB + 2)
            merge(0, DOWN_BANKS, U_GB)
            feed(U_GB + 5 + AHEAD)

            def spectral(o):
                dve.wait_ge(sem("conv_done"), 3)
                dve.wait_ge(sem("h_fwd"), o + 1)
                ur0, ur1, ui0, ui1 = (ps[4 + i][:, :] for i in range(4))
                hc0, hc1, hn0, hs0, hs1 = (H[:, o, i, :] for i in range(NFT))
                for y, a, ha, b, hb in ((0, ur0, hc0, ui0, hs0), (1, ur1, hc1, ui1, hs1),
                                        (2, ur0, hs0, ui0, hn0), (3, ur1, hs1, ui1, hc1)):
                    v_.tensor_tensor(C_Y[:, y, :], a, ha, ALU.mult).then_inc(sem("h_prod"), 1)
                    v_.tensor_tensor(H_prod[y], b, hb, ALU.mult).then_inc(sem("h_prod"), 1)

            def hyena_gate(o):
                dve.wait_ge(sem("hyd_loaded"), 32)
                parts = [(C_p[:, t, 768:768 + HW], C_p[:, t, 768 + (o + 1) * HW:768 + (o + 2) * HW]) for t in range(NT)]
                for vv, xx in parts:
                    ins = v_.tensor_tensor(vv, vv, C_hd[:, o, :], ALU.mult)
                link(ins)
                dve.wait_ge(sem("h_bwd"), o + 1)
                for t, (vv, xx) in enumerate(parts):
                    link(v_.tensor_tensor(vv, vv, ps[2 + t][:, :], ALU.add))
                    v_.tensor_tensor(vv, vv, xx, ALU.mult).then_inc(sem("h_z"), 1)

            spectral(0)
            feed(U_GB + 7 + AHEAD)
            hyena_gate(0)
            spectral(1)
            feed(U_GB + 11 + AHEAD)
            hyena_gate(1)
            for p in range(2):
                dve.wait_ge(sem("h_hi"), p + 1)
                v_.tensor_tensor(brl[:, 2 * p:2 * p + 2, :], ps[6 + p][:, :].rearrange("p (f t) -> p f t", f=2),
                                 brh[:, 2 * p:2 * p + 2, :], ALU.subtract).then_inc(sem("h_lo"), 1)
            for i, (a, b) in enumerate((("lq1", "lk1"), ("lq2", "lk2"))):
                link(v_.tensor_tensor(rq_a[:, 0:64], R(a), R(b), ALU.mult))
                v_.tensor_reduce(sm[:, 200 + i:201 + i], rq_a[:, 0:64], AXX, ALU.add).then_inc(sem("lam_dots"), 1)
                dve.wait_ge(sem("lam_dots"), i + 1)
            feed(U_GC + 2)
            dve.wait_ge(sem("lam_exps"), 1)
            link(v_.tensor_tensor(sm[:, 204:205], sm[:, 203:204], sm[:, 202:203], ALU.subtract))
            link(v_.tensor_scalar(sm[:, 205:206], sm[:, 204:205], LAM0, None, ALU.subtract))
            v_.tensor_scalar(sm[:, 280:281], gcol[:, GROWS["subln"]:GROWS["subln"] + 1], 1.0 - LAM0, None, ALU.mult)\
                .then_inc(sem("sub_ready"), 1)
            dve.wait_ge(sem("sub_ready"), 1)

            def d_max(h):
                dve.wait_ge(sem("d_scores"), 2 * h + 2)
                c = sm[:, 208 + 32 * (h % 2):]
                if h >= 2:
                    dve.wait_ge(sem("d_p"), 2 * (h - 1))
                for comp in range(2):
                    link(v_.tensor_reduce(c[:, 2 * comp:2 * comp + 2],
                                          ps[D_SCORE[h % 2] + comp][:, :].rearrange("p (t s) -> p t s", t=NT), AXX, ALU.max))
                src = sm[:, 320:352].rearrange("p (t h) -> p h t", t=NT)[:, 2 * h:2 * h + 2, :]
                link(v_.tensor_copy(c[:, 4:8].rearrange("p (h t) -> p h t", h=2), src))
                v_.scalar_tensor_tensor(c[:, 8:12], c[:, 0:4], -1.0, c[:, 4:8], ALU.mult, ALU.mult)\
                    .then_inc(sem("d_max"), 1)

            def d_prob(h):
                dve.wait_ge(sem("d_exp"), 4 * h + 4)
                c = sm[:, 208 + 32 * (h % 2):]
                link(v_.reciprocal(c[:, 16:20], c[:, 12:16]))
                link(v_.tensor_scalar(c[:, 18:20], c[:, 18:20], sm[:, 205:206], None, ALU.mult))
                for t in range(NT):
                    e0 = C_L[:, 2 * (h % 2), t * S:(t + 1) * S]
                    e1 = C_L[:, 2 * (h % 2) + 1, t * S:(t + 1) * S]
                    link(v_.tensor_scalar(e0, e0, c[:, 16 + t:17 + t], None, ALU.mult))
                    v_.scalar_tensor_tensor(e0, e1, c[:, 18 + t:19 + t], e0, ALU.mult, ALU.add).then_inc(sem("d_p"), 1)

            d_max(0)
            d_prob(0)
            merge(1, DOWN_BANKS, U_GC)
            for i in range(1, CH + 1):
                if i > 1:
                    d_prob(i - 1)
                if i < CH:
                    d_max(i)
                feed(D_STEPS[min(i, CH)])
            dve.wait_ge(sem("d_ssq"), 8)
            dve.wait_ge(sem("d_oc"), 4)
            link(v_.tensor_scalar(rq_a[:, 0:8], sm[:, 272:280], 1.0 / (2 * HD), EPS, ALU.mult, ALU.add))
            rsqrt(sm[:, 284:292], 8)
            for t in range(NT):
                y = C_oc[:, t, :].rearrange("p (h d) -> p h d", h=CH)
                v_.tensor_tensor(y, y, sm[:, 284 + 4 * t:288 + 4 * t].unsqueeze(2).to_broadcast([P, CH, P]), ALU.mult)\
                    .then_inc(sem("d_y"), 1)
            feed(U_OC + 2)
            for p in range(2):
                dve.wait_ge(sem("c_hi"), p + 1)
                v_.scalar_tensor_tensor(brl[:, 2 * p:2 * p + 2, :], ps[4 + p][:, :].rearrange("p (f t) -> p f t", f=2),
                                        sm[:, 280:281], brh[:, 2 * p:2 * p + 2, :], ALU.mult, ALU.subtract)\
                    .then_inc(sem("c_lo"), 1)
            feed(U_W + 3 + AHEAD)
            merge(2, BR_BANKS, U_W)
            turn_lo(6, lambda f: 0.5)
            feed(U_F2 + 3 + AHEAD)
            residual(4, U_F2)
            turn_lo(7, lambda f: gcol[:, GROWS["n2"] + f:GROWS["n2"] + f + 1])
            row_scale(5)
            ffn(2, U_F2, 5)
            residual(5, U_END)

        @block.tensor
        def _(pe):
            mm = nc.tensor.matmul

            def split_mm(dst, h, lo, rh, rl, start, stop):
                mm(dst, h, rh, start=start, stop=False)
                mm(dst, h, rl, start=False, stop=False)
                return mm(dst, lo, rh, start=False, stop=stop)

            def up_unit(slot, i, bk, w, ready, turned_need=None, empty=None):
                if turned_need is not None:
                    pe.wait_ge(turned_lo, turned_need)
                pe.wait_ge(lo_ready, ready)
                rh, rl = unit_view(whi, slot, w), unit_view(wlo, slot, w)
                for kk, t in ((0, 0), (1, 0), (0, 1), (1, 1)):
                    if empty is not None and kk == 0:
                        pe.wait_ge(hid_ready, empty + t + 1)
                    k = 2 * i + kk
                    ins = split_mm(ps[bk + t][:, 0:w], ath[:, k, t * P:(t + 1) * P], atl[:, k, t * P:(t + 1) * P],
                                   rh[:, kk, :], rl[:, kk, :], k == 0, k == KT - 1)
                ins.then_inc(unit_used, 1)

            def down_unit(slot, k, first, last, ready, act_h, act_l, banks=DOWN_BANKS):
                pe.wait_ge(lo_ready, ready)
                rh, rl = unit_view(whi, slot, 512), unit_view(wlo, slot, 512)
                for nb in range(2):
                    for t in range(NT):
                        ins = split_mm(ps[banks[2 * nb + t]][:, :], act_h[:, k, t * P:(t + 1) * P],
                                       act_l[:, k, t * P:(t + 1) * P], rh[:, nb, :], rl[:, nb, :], first, last)
                ins.then_inc(unit_used, 1)

            def units(i, lo=0, hi=4, use=None):
                u0, w, bk = IN_BLOCKS[i]
                if lo == 0:
                    back = i - 1 if i >= 17 else i - 2
                    if back >= 0:
                        pe.wait_ge(evac_act, ACT_EVACS[back])
                        pe.wait_ge(evac_dve, DVE_EVACS[back])
                for c in range(lo, hi):
                    up_unit((u0 + c) % RING, c, bk, w, u0 + c + 1, None if use is None else 8 * use + 2 * (c + 1))

            def down(u0, n, act_h, act_l, banks=DOWN_BANKS):
                for k in range(n):
                    down_unit((u0 + k) % RING, k, k == 0, k == n - 1, u0 + k + 1, act_h, act_l, banks)

            def turn(src, ready):
                for p in range(4):
                    ready(p)
                    for f in range(2):
                        for t in range(NT):
                            c = (2 * p + f) * P
                            ins = nc.tensor.transpose(ps[TBANKS[p]][:, f * S + t * P:f * S + (t + 1) * P],
                                                      src(t)[:, c:c + P], ident)
                    ins.then_inc(turned, 1)

            def ffn(n, u0, use):
                def hid_turn(count):
                    pe.wait_ge(hid_ready, count)
                    for f in range(2):
                        for t in range(NT):
                            ins = nc.tensor.transpose(ps[2][:, f * S + t * P:f * S + (t + 1) * P],
                                                      hid[:, t, f * P:(f + 1) * P], ident)
                    ins.then_inc(hid_T, 1)

                def ffn_down(j, k2, wait, slot, ready, first, last):
                    if k2 == 0:
                        pe.wait_ge(hid_lo, wait)
                    down_unit(slot, k2, first, last, ready, brh, brl)

                for t in range(NT):
                    for c in range(4):
                        if t == 0:
                            pe.wait_ge(turned_lo, 8 * use + 2 * (c + 1))
                            pe.wait_ge(lo_ready, u0 + c + 1)
                        slot = (u0 + c) % RING
                        rh, rl = unit_view(whi, slot, 512), unit_view(wlo, slot, 512)
                        for kk in range(2):
                            k = 2 * c + kk
                            ins = split_mm(ps[t][:, :], ath[:, k, t * P:(t + 1) * P], atl[:, k, t * P:(t + 1) * P],
                                           rh[:, kk, :], rl[:, kk, :], k == 0, k == KT - 1)
                        if t == 1:
                            ins.then_inc(unit_used, 1)
                        elif c == 3:
                            ins.then_inc(sem("first_tile"), 1)

                def body(j, first):
                    for c in range(6):
                        slot = (u0 + 4 + c) % RING
                        ready = 6 * j + (u0 - 2 + c + 1)
                        if c == 2:
                            hid_turn(2 * j + 2 * FB * n)
                        if c < 4:
                            up_unit(slot, c, 0, 512, ready, empty=2 * j + (2 * FB * n - 2) if c == 0 else None)
                        else:
                            ffn_down(j, c - 4, j + FB * n, slot, ready, first and c == 4, False)

                body(1, True)
                with pe.Fori(2, FB) as j:
                    body(j, False)
                last = u0 + 4 + 6 * (FB - 1)
                hid_turn(2 * FB * (n + 1))
                for k2 in range(2):
                    ffn_down(FB, k2, FB * (n + 1), (last + k2) % RING, last + k2 + 1, False, k2 == 1)

            pe.wait_ge(sem("ident_loaded"), 16)
            pe.wait_ge(sem("mix_loaded"), 16)
            nc.tensor.transpose(ps[6][:, 0:16], grow[0:16, :], con[0:16, 0:16]).then_inc(sem("cols_turned"), 1)

            def x_first(p):
                if p == 0:
                    for t in range(NT):
                        pe.wait_ge(sem(f"x_loaded{t}"), 16)

            turn(lambda t: x[:, t, :], x_first)
            pe.wait_ge(sem("grow_loaded"), 16 * (len(GROWS) - 1))
            nc.tensor.transpose(ps[7][:, 256:320], grow[:, :], con[0:64, 0:64]).then_inc(sem("cols_turned"), 1)
            units(0, use=0)
            pe.wait_ge(sem("wg_split"), 2)
            for t in range(NT):
                for k in range(KT):
                    ins = split_mm(ps[6][:, 8 * t:8 * t + 8], ath[:, k, t * P:(t + 1) * P], atl[:, k, t * P:(t + 1) * P],
                                   wgh[:, k, :], wgl[:, k, :], k == 0, k == KT - 1)
            ins.then_inc(sem("gl_ready"), 1)
            pe.wait_ge(sem("con1_loaded"), 16)
            pe.wait_ge(sem("filt_loaded"), 48)
            mm(ps[7][0:64, 0:S], fw12[0:33, 0, :], con[0:33, CONSTS["zT"][0]:CONSTS["zT"][0] + S],
               start=True, stop=True).then_inc(sem("f_mm"), 1)
            units(1)

            def turn_qk(c0, n):
                for h in range(AH):
                    for t in range(NT):
                        ins = nc.tensor.transpose(ps[4 + h // 2][:, (h % 2) * S + t * P:(h % 2) * S + (t + 1) * P],
                                                  A_qk[:, t, c0 + h * ADK:c0 + (h + 1) * ADK], ident)
                ins.then_inc(sem("a_qk_turned"), 1)

            pe.wait_ge(evac_act, ACT_EVACS[0])
            pe.wait_ge(evac_dve, DVE_EVACS[0])
            turn_qk(0, 0)
            pe.wait_ge(sem("glog"), 2)
            pe.wait_ge(sem("f_arg"), 1)
            for g in range(2):
                for t in range(NT):
                    ins = nc.tensor.transpose(ps[7][0:4, g * S + t * P:g * S + (t + 1) * P],
                                              glog[:, t, 4 * g:4 * g + 4], ident)
            ins.then_inc(sem("gl_turned"), 1)
            pe.wait_ge(sem("f_hidden"), 1)
            mm(ps[6][0:64, 0:S], fw12[:, 1, :], fil[:, 2, :], start=True, stop=True).then_inc(sem("f_mm"), 1)
            units(2, 0, 2)
            pe.wait_ge(evac_act, ACT_EVACS[1])
            pe.wait_ge(evac_dve, DVE_EVACS[1])
            pe.wait_ge(sem("a_qk_copied"), 2)
            turn_qk(512, 1)
            units(2, 2, 4)

            def filter3(i):
                o, t = divmod(i, 2)
                pe.wait_ge(sem("f_hidden"), 2)
                if i >= 2:
                    pe.wait_ge(sem("fb_ready"), 2 * (i - 1))
                for d in range(2):
                    ins = mm(ps[(4, 6)[i % 2] + d][:, :], fil[:, 3, t * P:(t + 1) * P],
                             A_w3[:, (2 * o + d) * HW:(2 * o + d + 1) * HW], start=True, stop=True)
                ins.then_inc(sem("f3"), 1)

            def filter_norm(o):
                pe.wait_ge(sem("f_sum"), 2 * o + 2)
                for c in range(4):
                    ins = mm(ps[4][:, 4 * o + c:4 * o + c + 1], A_sq[:, 0, 0, c * P:(c + 1) * P], C("ones")[:, 0:1],
                             start=True, stop=True)
                ins.then_inc(sem("f_norm"), 1)

            pe.wait_ge(sem("a_qk_copied"), 4)
            filter3(0)
            units(3, 0, 2)
            pe.wait_ge(sem("g_rows"), 2)
            pe.wait_ge(sem("f_arg"), 2)
            filter3(1)
            units(3, 2, 4)
            filter3(2)
            units(4, 0, 2)
            filter3(3)
            pe.wait_ge(sem("fb_ready"), 6)
            pe.wait_ge(sem("g_em"), 1)
            for t in range(NT):
                for j, row in enumerate((5, 7)):
                    ins = nc.tensor.transpose(ps[5][:, 8 * t + 4 * j:8 * t + 4 * j + 4],
                                              gate[:, row, t * P:(t + 1) * P], con[0:4, 0:4])
            ins.then_inc(sem("am_turned"), 1)
            units(4, 2, 3)
            filter_norm(0)
            units(4, 3, 4)
            units(5, 0, 3)
            filter_norm(1)

            def a_scores(h):
                if h >= 2:
                    pe.wait_ge(sem("a_num"), 2 * (h - 1))
                    pe.wait_ge(sem("a_ssq"), 2 * (h - 1))
                mm(ps[6 + h % 2][:, 0:S], A_kT[:, h, 0:P], A_qT[:, h, :], start=True, stop=True)
                mm(ps[6 + h % 2][:, S:384], A_kT[:, h, P:S], A_qT[:, h, P:S], start=True, stop=True)
                mm(ps[4 + h % 2][:, 0:S], sel[0:4, h, :], gate[:, 6, :], start=True, stop=True)\
                    .then_inc(sem("a_scores"), 1)

            pe.wait_ge(sem("fb_ready"), 8)
            pe.wait_ge(sem("am_ready"), 1)
            pe.wait_ge(sem("f_norm_read"), 1)
            a_scores(0)
            a_scores(1)
            units(5, 3, 4)
            pe.wait_ge(sem("dg_ready"), 8)
            for o in range(2):
                for c in range(4):
                    ins = mm(ps[o][:, c * P:(c + 1) * P], C("ones"), A_dg[:, 4 * o + c, :], start=True, stop=True)
            ins.then_inc(sem("rn_spread"), 1)

            def spectrum(i):
                o, f = divmod(i, NFT)
                if i == 0:
                    pe.wait_ge(sem("con2_loaded"), 64)
                    pe.wait_ge(evac_act, ACT_EVACS[5])
                    pe.wait_ge(sem("ed_ready"), 8)
                if i >= 2:
                    pe.wait_ge(sem("spec_ready"), i - 1)
                d = 0 if f < 3 else 1
                for t in range(NT):
                    ins = mm(ps[2 + i % 2][:, :], fwd[:, t, f, :], A_ed[:, o, t, d, :], start=(t == 0), stop=(t == 1))
                ins.then_inc(sem("spec"), 1)

            def a_pv(h):
                pe.wait_ge(sem("a_p_masked"), 2 * h + 2)
                pe.wait_ge(sem("a_d_ready"), h + 1)
                pe.wait_ge(evac_act, ACT_EVACS[3])
                pe.wait_ge(evac_dve, DVE_EVACS[3])
                pe.wait_ge(sem("cleared"), 2)
                pt = A_P[:, h % 2, :]
                mm(ps[6 + h % 2][:, 0:ADV + 1], pt[:, 0:P], A_v[:, 0, h, :], start=True, stop=True)\
                    .then_inc(sem("a_pv"), 1)
                mm(ps[4 + h % 2][:, 0:ADV + 1], pt[:, P:S], A_v[:, 0, h, :], start=True, stop=False)
                mm(ps[4 + h % 2][:, 0:ADV + 1], pt[:, S:384], A_v[:, 1, h, :], start=False, stop=True)\
                    .then_inc(sem("a_pv"), 1)

            spectrum(0)
            spectrum(1)
            a_pv(0)
            a_pv(1)
            spectrum(2)
            a_scores(2)
            a_scores(3)
            for i in range(3, 5):
                spectrum(i)
            a_pv(2)
            a_pv(3)
            for i in range(5, 8):
                spectrum(i)

            def y_first(p):
                pe.wait_ge(sem("a_y"), 2 * (p + 1))
                if p == 0:
                    pe.wait_ge(sem("spec_ready"), 8)

            turn(lambda t: A_o[:, t, :], y_first)
            pe.wait_ge(turned_lo, 8 + 4)
            for i in range(8, 10):
                spectrum(i)
            pe.wait_ge(turned_lo, 16)
            down(U_AO, KT, ath, atl)

            def x_sum(r):
                def ready(p):
                    pe.wait_ge(x_ready, 4 * r + 2 * (p // 2 + 1))
                return ready

            def x_sum0(p):
                if p == 0:
                    pe.wait_ge(sem("spec_ready"), 10)
                x_sum(0)(p)

            turn(lambda t: x[:, t, :], x_sum0)
            ffn(0, U_F0, 2)

            turn(lambda t: x[:, t, :], x_sum(1))

            def b_turn(b):
                dst, half = (B_q, b) if b < 2 else (B_k, b - 2)
                if b < 2:
                    pe.wait_ge(sem("b_rotated"), 2 * b + 2)
                else:
                    pe.wait_ge(sem("b_knormed"), 2 * (b - 2) + 2)
                if b >= 2:
                    pe.wait_ge(sem("b_copied_act"), b - 1)
                    pe.wait_ge(sem("b_copied_dve"), b - 1)
                for h in range(4):
                    for t in range(NT):
                        ins = nc.tensor.transpose(
                            ps[4 + 2 * (b % 2) + h // 2][:, (h % 2) * S + t * P:(h % 2) * S + (t + 1) * P],
                            dst[:, t, (4 * half + h) * BD:(4 * half + h + 1) * BD], ident)
                ins.then_inc(sem("b_turned"), 1)

            units(6, use=3)
            units(7)
            b_turn(0)
            units(8)
            b_turn(1)
            units(9)
            units(10)
            b_turn(2)
            b_turn(3)

            def b_scores(h):
                if h == 0:
                    pe.wait_ge(sem("b_copied_act"), 4)
                    pe.wait_ge(sem("b_copied_dve"), 4)
                if h == 4:
                    pe.wait_ge(evac_act, ACT_EVACS[10])
                elif h >= 2:
                    pe.wait_ge(sem("b_l"), 2 * (h if h > 4 else h - 1))
                bk = ps[B_SCORE[h]]
                mm(bk[:, 0:P], B_qT[:, h, 0:P], B_kT[:, h, 0:P], start=True, stop=True)
                mm(bk[:, P:384], B_qT[:, h, P:S], B_kT[:, h, :], start=True, stop=True)\
                    .then_inc(sem("b_scores"), 1)

            def b_p_turn(h):
                pe.wait_ge(sem("b_p"), 2 * h + 2)
                if h == 4:
                    pe.wait_ge(evac_act, ACT_EVACS[11])
                elif h >= 2:
                    pe.wait_ge(sem("b_pt"), h if h > 4 else h - 1)
                for i in range(3):
                    ins = nc.tensor.transpose(ps[B_TURN[h]][:, i * P:(i + 1) * P], B_L[:, h % 3, i * P:(i + 1) * P], ident)
                ins.then_inc(sem("b_p_turned"), 1)

            def b_pv(h):
                pe.wait_ge(sem("b_pt"), h + 1)
                v_block = 10 if h < 4 else 11
                pe.wait_ge(evac_act, ACT_EVACS[v_block])
                pe.wait_ge(evac_dve, DVE_EVACS[v_block])
                if h not in (0, 4):
                    pe.wait_ge(sem("b_out_lo"), h)
                o = ps[B_PV[h]]
                mm(o[:, 0:S], B_v[:, 0, h * BD:(h + 1) * BD], B_PT[:, h % 2, 0:S], start=True, stop=False)
                mm(o[:, P:S], B_v[:, 1, h * BD:(h + 1) * BD], B_PT[:, h % 2, S:384], start=False, stop=True)\
                    .then_inc(sem("b_pv"), 1)

            b_scores(0)
            b_scores(1)

            def b_down(u, n):
                for u in range(u, u + n):
                    h = u - U_BO
                    if h == 0:
                        pe.wait_ge(sem("b_l"), 8)
                        pe.wait_ge(sem("b_pt"), 4)
                    pe.wait_ge(sem("b_out_lo"), h + 1)
                    down_unit(u % RING, h, h == 0, h == BH - 1, u + 1, *((brh, brl) if h < 4 else (ath, atl)))

            for h in range(BH + 1):
                if h < 4:
                    units(11, h, h + 1)
                else:
                    b_down(*B_UNITS[h])
                if h < BH:
                    b_p_turn(h)
                if h + 2 < BH:
                    b_scores(h + 2)
                if h >= 1:
                    b_pv(h - 1)
            b_down(U_BO + 6, 2)
            turn(lambda t: x[:, t, :], x_sum(2))
            ffn(1, U_F1, 4)

            turn(lambda t: x[:, t, :], x_sum(3))
            units(12, use=5)
            units(13)
            for i in range(14, 17):
                units(i)
            pe.wait_ge(sem("c_w_ready"), 1)
            for pr in range(4):
                for t in range(NT):
                    nc.tensor.transpose(ps[4 + pr // 2][:, (pr % 2) * S + t * P:(pr % 2) * S + (t + 1) * P],
                                        C_p[:, t, pr * P:(pr + 1) * P], ident)
            for g in range(2):
                for t in range(NT):
                    ins = nc.tensor.transpose(ps[6][:, g * S + t * P:g * S + (t + 1) * P],
                                              C_kd[:, t, g * P:(g + 1) * P], ident)
            ins.then_inc(sem("c_w_turned"), 1)
            def w_scores(h):
                if h == 0:
                    pe.wait_ge(sem("c_w_copied"), 3)
                if h >= 2:
                    pe.wait_ge(sem("w_l"), 2 * (h - 1))
                g, pr = h // 4, h // 2
                rows = slice(64 * (h % 2), 64 * (h % 2) + 64)
                for t in range(NT):
                    ins = mm(ps[4 + h % 2][:, t * S:(t + 1) * S], C_qT[rows, pr, t * P:(t + 1) * P], C_kT[rows, g, :],
                             start=True, stop=True)
                ins.then_inc(sem("w_scores"), 1)

            def p_turn(h, p_sem, pt_sem, out_sem, src):
                pe.wait_ge(sem(p_sem), 2 * h + 2)
                if h >= 2:
                    pe.wait_ge(sem(pt_sem), h - 1)
                for s in range(2):
                    for t in range(NT):
                        ins = nc.tensor.transpose(ps[6 + h % 2][:, s * S + t * P:s * S + (t + 1) * P],
                                                  src[:, t * S + s * P:t * S + (s + 1) * P], ident)
                ins.then_inc(sem(out_sem), 1)

            def w_pv(h):
                pe.wait_ge(sem("w_pt"), h + 1)
                i = h // 2
                if h % 2 == 0 and i >= 2:
                    pe.wait_ge(sem("w_out_lo"), i - 1)
                if h == 0:
                    pe.wait_ge(evac_act, ACT_EVACS[15])
                rows = slice(64 * (h % 2), 64 * (h % 2) + 64)
                g = h // 4
                for s in range(2):
                    ins = mm(ps[2 + i % 2][rows, 0:S], C_p[:, s, 640 + g * HD:640 + (g + 1) * HD],
                             C_PT[:, h % 2, s * S:(s + 1) * S], start=(s == 0), stop=(s == 1))
                ins.then_inc(sem("w_pv"), 1)

            w_scores(0)
            w_scores(1)
            w_pieces = [(17, 0, 2), (17, 2, 4), (18, 0, 2), (18, 2, 4), (19, 0, 4), (20, 0, 2), (20, 2, 4), (21, 0, 2)]
            for h in range(WQ + 1):
                if h < WQ:
                    units(*w_pieces[h])
                    p_turn(h, "w_p", "w_pt", "w_p_turned", C_L[:, h % 2, :])
                if h + 2 < WQ:
                    w_scores(h + 2)
                if h >= 1:
                    w_pv(h - 1)
            units(21, 2, 4)
            pe.wait_ge(sem("w_out_lo"), 4)
            down(U_OA, 4, brh, brl)

            def d_turn(c):
                if c == 0:
                    pe.wait_ge(sem("c_d_ready"), NT)
                else:
                    pe.wait_ge(sem("d_copied"), 2)
                for h in range(CH):
                    for t in range(NT):
                        c0 = (2304, 2816)[c] + h * P
                        ins = nc.tensor.transpose(ps[2 + h // 2][:, (h % 2) * S + t * P:(h % 2) * S + (t + 1) * P],
                                                  C_p[:, t, c0:c0 + P], ident)
                ins.then_inc(sem("d_turned"), 1)

            def forward(o):
                if o == 0:
                    pe.wait_ge(sem("conv_done"), 1)
                    pe.wait_ge(sem("merged"), 4)
                else:
                    pe.wait_ge(sem("h_z"), 2)
                for i in range(4):
                    for t in range(NT):
                        ins = mm(ps[4 + i][:, :], fwd[:, t, (0, 1, 5, 4)[i], :], C_p[:, t, 768:768 + HW],
                                 start=(t == 0), stop=(t == 1))
                ins.then_inc(sem("h_fwd"), 1)

            def backward(o):
                pe.wait_ge(sem("d_copied"), 4)
                for i in range(4):
                    pe.wait_ge(sem("h_y"), 4 * o + i + 1)
                    for t in range(NT):
                        ins = mm(ps[2 + t][:, :], bwd[:, i, t * P:(t + 1) * P], C_Y[:, i, :], start=(i == 0), stop=(i == 3))
                ins.then_inc(sem("h_bwd"), 1)

            d_turn(0)
            units(22, 0, 1)
            d_turn(1)
            units(22, 1, 2)
            forward(0)
            units(22, 2, 4)
            backward(0)
            units(23, 0, 2)
            forward(1)
            units(23, 2, 3)
            backward(1)
            units(23, 3, 4)
            for p in range(2):
                if p == 0:
                    pe.wait_ge(sem("h_z"), 4)
                for f in range(2):
                    for t in range(NT):
                        c = 768 + (2 * p + f) * P
                        ins = nc.tensor.transpose(ps[6 + p][:, f * S + t * P:f * S + (t + 1) * P], C_p[:, t, c:c + P], ident)
                ins.then_inc(sem("h_turned"), 1)

            def d_scores(h):
                if h == 0:
                    pe.wait_ge(sem("h_z"), 4)
                elif h == 1:
                    pe.wait_ge(sem("merged"), 8)
                else:
                    pe.wait_ge(sem("d_exp"), 4 * (h - 1))
                for comp in range(2):
                    rows = slice(64 * comp, 64 * comp + 64)
                    for t in range(NT):
                        ins = mm(ps[D_SCORE[h % 2] + comp][:, t * S:(t + 1) * S], C_qT[rows, h, t * P:(t + 1) * P],
                                 C_kT[rows, h, :], start=True, stop=True)
                    ins.then_inc(sem("d_scores"), 1)

            def d_p_turn(h):
                pe.wait_ge(sem("d_p"), 2 * h + 2)
                if h:
                    pe.wait_ge(sem("d_pt"), h)
                else:
                    pe.wait_ge(sem("merged"), 8)
                for s in range(2):
                    for t in range(NT):
                        ins = nc.tensor.transpose(ps[6][:, s * S + t * P:s * S + (t + 1) * P],
                                                  C_L[:, 2 * (h % 2), t * S + s * P:t * S + (s + 1) * P], ident)
                ins.then_inc(sem("d_p_turned"), 1)

            def d_pv(h):
                pe.wait_ge(sem("d_pt"), h + 1)
                if h:
                    pe.wait_ge(sem("d_oc"), h)
                for t in range(NT):
                    for s in range(2):
                        ins = mm(ps[7][:, t * P:(t + 1) * P], C_PT[:, h % 2, s * S + t * P:s * S + (t + 1) * P],
                                 C_p[:, s, 3328 + h * P:3328 + (h + 1) * P], start=(s == 0), stop=(s == 1))
                ins.then_inc(sem("d_pv"), 1)

            d_scores(0)
            pe.wait_ge(sem("h_lo"), 2)
            down(U_OB, 4, brh, brl)
            for h in range(CH + 1):
                if h < CH:
                    units(*((24, 0, 2), (24, 2, 4), (25, 0, 1), (25, 1, 2))[h])
                    if h == 0:
                        d_scores(1)
                    d_p_turn(h)
                    if h + 2 < CH:
                        d_scores(h + 2)
                if h >= 1:
                    d_pv(h - 1)
            units(25, 2, 4)
            for p in range(2):
                if p == 0:
                    pe.wait_ge(sem("d_y"), 2)
                for f in range(2):
                    for t in range(NT):
                        c = (2 * p + f) * P
                        ins = nc.tensor.transpose(ps[4 + p][:, f * S + t * P:f * S + (t + 1) * P], C_oc[:, t, c:c + P], ident)
                ins.then_inc(sem("c_turned"), 1)
            pe.wait_ge(sem("c_lo"), 2)
            pe.wait_ge(evac_act, ACT_EVACS[25])
            down(U_OC, 4, brh, brl, BR_BANKS)

            def merged_ready(p):
                pe.wait_ge(sem("merged"), 8 + 2 * (p // 2 + 1))

            turn(lambda t: C_mg[:, t, :], merged_ready)
            pe.wait_ge(turned_lo, 8 * 7)
            down(U_W, KT, ath, atl)
            turn(lambda t: x[:, t, :], x_sum(4))
            ffn(2, U_F2, 7)


_INS = ["x", "positions", "norm_mix", "norm_ffn", "ffn_w_in", "ffn_w_out", "a_w_in", "a_b_gates", "a_g_out",
        "a_w_out", "b_w_in", "b_g_q", "b_g_k", "b_w_out", "norm1_g_2", "w_in_2", "sink_a_2", "qn_a_2", "kn_a_2",
        "conv_w_2", "conv_b_2", "filt_w1_2", "filt_b1_2", "filt_f1_2", "filt_w2_2", "filt_b2_2", "filt_f2_2",
        "filt_w3_2", "hy_d_2", "qn_c_2", "kn_c_2", "lam_q1_2", "lam_k1_2", "lam_q2_2", "lam_k2_2", "subln_c_2",
        "w_oa_2", "w_ob_2", "w_oc_2", "w_out_2", "norm2_g_2", "ffn_w1_2", "ffn_w3_2", "ffn_w2_2"]


def kernel(**inputs):
    import concourse.bacc as _bacc
    from concourse.bass_utils import run_bass_kernel_spmd as _run

    nc = _bacc.Bacc("TRN2", target_bir_lowering=False, num_devices=1)
    arrays, D = {}, {}
    for name in _INS:
        arrays[f"in_{name}"] = np.ascontiguousarray(inputs[name])
    arrays["in_consts"] = constants()
    arrays["in_decay"] = decay_table()
    for key, a in arrays.items():
        D[key[3:]] = nc.dram_tensor(key, a.shape, mybir.dt.from_np(a.dtype), kind="ExternalInput").ap()
    out = nc.dram_tensor("out", (1, S, DM), F32, kind="ExternalOutput").ap()
    build(nc, D, out)
    r = _run(nc, [arrays], core_ids=[0])
    return r.results[0]["out"]
```
